# Optimizing a Trainium2 kernel written in Bass

```python
import jax, jax.numpy as jnp
from jax import lax
import numpy as np

D_MODEL = 1024
BATCH = 1
SEQ = 256
DEPTH = 2

N_MIXERS = 2
N_CONV_LAYERS = (DEPTH + 1) // 2
N_MLA_LAYERS = DEPTH // 2
N_DENSE_LAYERS = (DEPTH + 1) // 2
N_MOE_LAYERS = DEPTH // 2
CONV_WIDTH = 3
N_HEADS = 8
QK_NOPE_DIM = 128
QK_ROPE_DIM = 64
QK_HEAD_DIM = QK_NOPE_DIM + QK_ROPE_DIM
V_HEAD_DIM = 128
Q_LORA_RANK = 384
KV_LORA_RANK = 256
ROPE_THETA = 10000.0
Q_BLOCK = 128
D_FF_DENSE = 2816
N_EXPERTS = 8
TOP_K = 2
D_FF_EXPERT = 2048
EPS = 1e-6


def rmsnorm(x, g):
    xf = x.astype(jnp.float32)
    y = xf * lax.rsqrt(jnp.mean(xf * xf, axis=-1, keepdims=True) + EPS)
    return (y * g.astype(jnp.float32)).astype(x.dtype)

def rope_tables(positions):
    inv_freq = ROPE_THETA ** (-jnp.arange(0, QK_ROPE_DIM, 2, dtype=jnp.float32) / QK_ROPE_DIM)
    ang = positions.astype(jnp.float32)[..., None] * inv_freq
    return jnp.cos(ang)[:, :, None, :], jnp.sin(ang)[:, :, None, :]

def apply_rope(x, cos, sin):
    x1, x2 = jnp.split(x, 2, axis=-1)
    cos = cos.astype(x.dtype)
    sin = sin.astype(x.dtype)
    return jnp.concatenate([x1 * cos - x2 * sin, x2 * cos + x1 * sin], axis=-1)

def short_conv_mixer(h, w_in, w_conv, w_out):
    seq = h.shape[1]
    b_gate, c_gate, u = jnp.split(h @ w_in, 3, axis=-1)
    v = c_gate * u
    vp = jnp.pad(v, ((0, 0), (CONV_WIDTH - 1, 0), (0, 0)))
    conv = vp[:, 0:seq] * w_conv[0]
    for k in range(1, CONV_WIDTH):
        conv = conv + vp[:, k:k + seq] * w_conv[k]
    return (b_gate * conv) @ w_out

def mla_mixer(h, cos, sin, w_down, q_a_norm, kv_a_norm, w_uq, w_ukv, q_norm, k_norm, w_o):
    bsz, seq, _ = h.shape
    down = h @ w_down
    c_q = rmsnorm(down[..., :Q_LORA_RANK], q_a_norm)
    c_kv = rmsnorm(down[..., Q_LORA_RANK:Q_LORA_RANK + KV_LORA_RANK], kv_a_norm)
    k_rope = down[..., Q_LORA_RANK + KV_LORA_RANK:]
    q = (c_q @ w_uq).reshape(bsz, seq, N_HEADS, QK_HEAD_DIM)
    kv = (c_kv @ w_ukv).reshape(bsz, seq, N_HEADS, QK_NOPE_DIM + V_HEAD_DIM)
    k_nope, v = kv[..., :QK_NOPE_DIM], kv[..., QK_NOPE_DIM:]
    k_rope_h = jnp.broadcast_to(k_rope[:, :, None, :], (bsz, seq, N_HEADS, QK_ROPE_DIM))
    k = jnp.concatenate([k_nope, k_rope_h], axis=-1)
    q = rmsnorm(q, q_norm)
    k = rmsnorm(k, k_norm)
    q = jnp.concatenate([q[..., :QK_NOPE_DIM], apply_rope(q[..., QK_NOPE_DIM:], cos, sin)], axis=-1)
    k = jnp.concatenate([k[..., :QK_NOPE_DIM], apply_rope(k[..., QK_NOPE_DIM:], cos, sin)], axis=-1)
    scale = QK_HEAD_DIM ** -0.5
    neg = jnp.finfo(jnp.float32).min
    outs = []
    for blk in range(seq // Q_BLOCK):
        s0 = blk * Q_BLOCK
        end = s0 + Q_BLOCK
        scores = jnp.einsum('bqhd,bkhd->bhqk', q[:, s0:end], k[:, :end]).astype(jnp.float32) * scale
        mask = jnp.arange(end)[None, :] <= (s0 + jnp.arange(Q_BLOCK))[:, None]
        p = jax.nn.softmax(jnp.where(mask, scores, neg), axis=-1).astype(v.dtype)
        outs.append(jnp.einsum('bhqk,bkhd->bqhd', p, v[:, :end]))
    o = jnp.concatenate(outs, axis=1).reshape(bsz, seq, N_HEADS * V_HEAD_DIM)
    return o @ w_o

def swiglu(h, w_gate, w_up, w_down):
    return (jax.nn.silu(h @ w_gate) * (h @ w_up)) @ w_down

def moe_swiglu(h, router, w_gate, w_up, w_down):
    bsz, seq, d = h.shape
    ht = h.reshape(bsz * seq, d)
    probs = jax.nn.softmax((ht @ router).astype(jnp.float32), axis=-1)
    vals, idx = lax.top_k(probs, TOP_K)
    wts = vals / jnp.sum(vals, axis=-1, keepdims=True)
    gates = jnp.einsum('tk,tke->te', wts, jax.nn.one_hot(idx, N_EXPERTS, dtype=jnp.float32)).astype(h.dtype)
    out = jnp.zeros_like(ht)
    for e in range(N_EXPERTS):
        out = out + gates[:, e:e + 1] * swiglu(ht, w_gate[e], w_up[e], w_down[e])
    return out.reshape(bsz, seq, d)

def first_inputs(seed: int = 0) -> dict:
    key = jax.random.key(seed)
    ks = jax.random.split(key, 24)
    f32 = jnp.float32
    res_scale = (2 * DEPTH) ** -0.5

    def w(k, shape, fan_in, extra=1.0):
        return jax.random.normal(k, shape, f32) * (fan_in ** -0.5) * extra

    def gain(k, shape):
        return 1.0 + 0.02 * jax.random.normal(k, shape, f32)

    x = jax.random.normal(ks[0], (BATCH, SEQ, D_MODEL), f32)
    start = jax.random.randint(ks[1], (BATCH, 1), 0, 4096, dtype=jnp.int32)
    positions = (start + jnp.arange(SEQ, dtype=jnp.int32)[None, :]).astype(jnp.int32)
    return {
        "x": x,
        "positions": positions,
        "norm_mix": gain(ks[2], (DEPTH, D_MODEL)),
        "norm_ffn": gain(ks[3], (DEPTH, D_MODEL)),
        "conv_w_in": w(ks[4], (N_CONV_LAYERS, D_MODEL, 3 * D_MODEL), D_MODEL),
        "conv_w": w(ks[5], (N_CONV_LAYERS, CONV_WIDTH, D_MODEL), CONV_WIDTH),
        "conv_w_out": w(ks[6], (N_CONV_LAYERS, D_MODEL, D_MODEL), D_MODEL, res_scale),
        "mla_w_down": w(ks[7], (N_MLA_LAYERS, D_MODEL, Q_LORA_RANK + KV_LORA_RANK + QK_ROPE_DIM), D_MODEL),
        "mla_q_a_norm": gain(ks[8], (N_MLA_LAYERS, Q_LORA_RANK)),
        "mla_kv_a_norm": gain(ks[9], (N_MLA_LAYERS, KV_LORA_RANK)),
        "mla_w_uq": w(ks[10], (N_MLA_LAYERS, Q_LORA_RANK, N_HEADS * QK_HEAD_DIM), Q_LORA_RANK),
        "mla_w_ukv": w(ks[11], (N_MLA_LAYERS, KV_LORA_RANK, N_HEADS * (QK_NOPE_DIM + V_HEAD_DIM)), KV_LORA_RANK),
        "mla_q_norm": gain(ks[12], (N_MLA_LAYERS, QK_HEAD_DIM)),
        "mla_k_norm": gain(ks[13], (N_MLA_LAYERS, QK_HEAD_DIM)),
        "mla_w_o": w(ks[14], (N_MLA_LAYERS, N_HEADS * V_HEAD_DIM, D_MODEL), N_HEADS * V_HEAD_DIM, res_scale),
        "ffn_w_gate": w(ks[15], (N_DENSE_LAYERS, D_MODEL, D_FF_DENSE), D_MODEL),
        "ffn_w_up": w(ks[16], (N_DENSE_LAYERS, D_MODEL, D_FF_DENSE), D_MODEL),
        "ffn_w_down": w(ks[17], (N_DENSE_LAYERS, D_FF_DENSE, D_MODEL), D_FF_DENSE, res_scale),
        "moe_router": w(ks[18], (N_MOE_LAYERS, D_MODEL, N_EXPERTS), D_MODEL),
        "moe_w_gate": w(ks[19], (N_MOE_LAYERS, N_EXPERTS, D_MODEL, D_FF_EXPERT), D_MODEL),
        "moe_w_up": w(ks[20], (N_MOE_LAYERS, N_EXPERTS, D_MODEL, D_FF_EXPERT), D_MODEL),
        "moe_w_down": w(ks[21], (N_MOE_LAYERS, N_EXPERTS, D_FF_EXPERT, D_MODEL), D_FF_EXPERT, res_scale),
    }

def first_block(x, positions, norm_mix, norm_ffn, conv_w_in, conv_w, conv_w_out,
              mla_w_down, mla_q_a_norm, mla_kv_a_norm, mla_w_uq, mla_w_ukv,
              mla_q_norm, mla_k_norm, mla_w_o, ffn_w_gate, ffn_w_up, ffn_w_down,
              moe_router, moe_w_gate, moe_w_up, moe_w_down):
    cos, sin = rope_tables(positions)
    for i in range(DEPTH):
        j = i // 2
        h = rmsnorm(x, norm_mix[i])
        if i % N_MIXERS == 0:
            x = x + short_conv_mixer(h, conv_w_in[j], conv_w[j], conv_w_out[j])
        else:
            x = x + mla_mixer(h, cos, sin, mla_w_down[j], mla_q_a_norm[j], mla_kv_a_norm[j],
                              mla_w_uq[j], mla_w_ukv[j], mla_q_norm[j], mla_k_norm[j], mla_w_o[j])
        h = rmsnorm(x, norm_ffn[i])
        if i % 2 == 0:
            x = x + swiglu(h, ffn_w_gate[j], ffn_w_up[j], ffn_w_down[j])
        else:
            x = x + moe_swiglu(h, moe_router[j], moe_w_gate[j], moe_w_up[j], moe_w_down[j])
    return x


DEPTH_2 = 1

CHUNK = 64
MEM_LEN = 256
FOX_HEADS = 8
FOX_HEAD_DIM = 64
FOX_WIDTH = FOX_HEADS * FOX_HEAD_DIM
POOL_WIDTH = D_MODEL - FOX_WIDTH
POOL_WINDOWS = (2, 4, 8, 16)
POOL_GROUPS = len(POOL_WINDOWS)
POOL_GROUP_DIM = POOL_WIDTH // POOL_GROUPS
IN_COLS = 3 * FOX_WIDTH + POOL_WIDTH + FOX_HEADS
MEM_HEADS = 4
MEM_HEAD_DIM = 128
MEM_WIDTH = MEM_HEADS * MEM_HEAD_DIM
D_FF = ((-(-8 * D_MODEL // 3) + 255) // 256) * 256


def rmsnorm_2(x, g):
    xf = x.astype(jnp.float32)
    y = xf * lax.rsqrt(jnp.mean(xf * xf, axis=-1, keepdims=True) + EPS)
    return (y * g.astype(jnp.float32)).astype(x.dtype)

def forgetting_attention(q, k, v, f_logit):
    c = jnp.cumsum(jax.nn.log_sigmoid(f_logit.astype(jnp.float32)), axis=-1)
    scale = FOX_HEAD_DIM ** -0.5
    S = q.shape[2]
    outs = []
    for start in range(0, S, Q_BLOCK):
        end = start + Q_BLOCK
        qb = q[:, :, start:end]
        kb = k[:, :, :end]
        vb = v[:, :, :end]
        s = jnp.einsum('bhqd,bhkd->bhqk', qb, kb, preferred_element_type=jnp.float32) * scale
        s = s + c[:, :, start:end, None] - c[:, :, None, :end]
        qpos = start + jnp.arange(Q_BLOCK)
        kpos = jnp.arange(end)
        s = jnp.where(kpos[None, :] <= qpos[:, None], s, -jnp.inf)
        p = jax.nn.softmax(s, axis=-1)
        outs.append(jnp.einsum('bhqk,bhkd->bhqd', p.astype(vb.dtype), vb))
    return jnp.concatenate(outs, axis=2)

def multiscale_pool(p, w_pool, pool_scale):
    B, S, _ = p.shape
    pf = p.astype(jnp.float32).reshape(B, S, POOL_GROUPS, POOL_GROUP_DIM)
    cs = jnp.concatenate([jnp.zeros((B, 1, POOL_GROUPS, POOL_GROUP_DIM), jnp.float32),
                          jnp.cumsum(pf, axis=1)], axis=1)
    t = jnp.arange(S)
    outs = []
    for g, w in enumerate(POOL_WINDOWS):
        csg = cs[:, :, g]
        lower = jnp.pad(csg, ((0, 0), (w - 1, 0), (0, 0)))[:, :S]
        cnt = jnp.minimum(t + 1, w).astype(jnp.float32)[None, :, None]
        mixed = (csg[:, 1:] - lower) / cnt - pf[:, :, g]
        outs.append(jnp.einsum('bsc,cd->bsd', mixed, w_pool[g].astype(jnp.float32)))
    y = jnp.concatenate(outs, axis=-1) * pool_scale.astype(jnp.float32)
    return y.astype(p.dtype)

def head_split(t, n_heads, head_dim):
    B, S, _ = t.shape
    return t.reshape(B, S, n_heads, head_dim)

def second_inputs(seed: int = 0) -> dict:
    key = jax.random.key(seed)
    ks = jax.random.split(key, 24)
    f32 = jnp.float32
    D = D_MODEL

    def nrm(k, shape, fan_in):
        return jax.random.normal(k, shape, f32) * (fan_in ** -0.5)

    def gain(k, shape):
        return 1.0 + 0.05 * jax.random.normal(k, shape, f32)

    return {
        "x": jax.random.normal(ks[0], (BATCH, SEQ, D), f32),
        "mem": jax.random.normal(ks[1], (BATCH, MEM_LEN, D), f32),
        "g_mix": gain(ks[2], (DEPTH_2, D)),
        "w_in": nrm(ks[3], (DEPTH_2, D, IN_COLS), D),
        "b_forget": 3.0 + 0.5 * jax.random.normal(ks[4], (DEPTH_2, FOX_HEADS), f32),
        "g_q_fox": gain(ks[5], (DEPTH_2, FOX_HEAD_DIM)),
        "g_k_fox": gain(ks[6], (DEPTH_2, FOX_HEAD_DIM)),
        "w_pool": nrm(ks[7], (DEPTH_2, POOL_GROUPS, POOL_GROUP_DIM, POOL_GROUP_DIM), POOL_GROUP_DIM),
        "pool_scale": gain(ks[8], (DEPTH_2, POOL_WIDTH)),
        "w_out": nrm(ks[9], (DEPTH_2, D, D), D),
        "g_mem_q": gain(ks[10], (DEPTH_2, D)),
        "g_mem_kv": gain(ks[11], (DEPTH_2, D)),
        "w_mem_q": nrm(ks[12], (DEPTH_2, D, MEM_WIDTH), D),
        "w_mem_kv": nrm(ks[13], (DEPTH_2, D, 2 * MEM_WIDTH), D),
        "g_q_mem": gain(ks[14], (DEPTH_2, MEM_HEAD_DIM)),
        "g_k_mem": gain(ks[15], (DEPTH_2, MEM_HEAD_DIM)),
        "w_mem_out": nrm(ks[16], (DEPTH_2, MEM_WIDTH, D), MEM_WIDTH),
        "g_ffn": gain(ks[17], (DEPTH_2, D)),
        "w_gate_up": nrm(ks[18], (DEPTH_2, D, 2 * D_FF), D),
        "w_down": nrm(ks[19], (DEPTH_2, D_FF, D), D_FF),
    }

def second_block(x, mem, g_mix, w_in, b_forget, g_q_fox, g_k_fox, w_pool, pool_scale, w_out,
              g_mem_q, g_mem_kv, w_mem_q, w_mem_kv, g_q_mem, g_k_mem, w_mem_out,
              g_ffn, w_gate_up, w_down):
    B, S, _ = x.shape
    h = x
    for l in range(DEPTH_2):
        xn = rmsnorm_2(h, g_mix[l])
        z = jnp.einsum('bsd,dc->bsc', xn, w_in[l])
        q = z[..., :FOX_WIDTH]
        k = z[..., FOX_WIDTH:2 * FOX_WIDTH]
        v = z[..., 2 * FOX_WIDTH:3 * FOX_WIDTH]
        p_in = z[..., 3 * FOX_WIDTH:3 * FOX_WIDTH + POOL_WIDTH]
        f_logit = z[..., 3 * FOX_WIDTH + POOL_WIDTH:] + b_forget[l]
        q = rmsnorm_2(head_split(q, FOX_HEADS, FOX_HEAD_DIM), g_q_fox[l]).transpose(0, 2, 1, 3)
        k = rmsnorm_2(head_split(k, FOX_HEADS, FOX_HEAD_DIM), g_k_fox[l]).transpose(0, 2, 1, 3)
        v = head_split(v, FOX_HEADS, FOX_HEAD_DIM).transpose(0, 2, 1, 3)
        fox = forgetting_attention(q, k, v, f_logit.transpose(0, 2, 1))
        fox = fox.transpose(0, 2, 1, 3).reshape(B, S, FOX_WIDTH)
        pool = multiscale_pool(p_in, w_pool[l], pool_scale[l])
        h = h + jnp.einsum('bsc,cd->bsd', jnp.concatenate([fox, pool], axis=-1), w_out[l])

        hn = rmsnorm_2(h, g_mem_q[l])
        mn = rmsnorm_2(mem, g_mem_kv[l])
        mq = rmsnorm_2(head_split(jnp.einsum('bsd,dc->bsc', hn, w_mem_q[l]), MEM_HEADS, MEM_HEAD_DIM), g_q_mem[l])
        mkv = jnp.einsum('bmd,dc->bmc', mn, w_mem_kv[l])
        mk = rmsnorm_2(head_split(mkv[..., :MEM_WIDTH], MEM_HEADS, MEM_HEAD_DIM), g_k_mem[l])
        mv = head_split(mkv[..., MEM_WIDTH:], MEM_HEADS, MEM_HEAD_DIM)
        sc = jnp.einsum('bshd,bmhd->bhsm', mq, mk, preferred_element_type=jnp.float32) * (MEM_HEAD_DIM ** -0.5)
        pm = jax.nn.softmax(sc, axis=-1).astype(mv.dtype)
        mo = jnp.einsum('bhsm,bmhd->bshd', pm, mv).reshape(B, S, MEM_WIDTH)
        h = h + jnp.einsum('bsc,cd->bsd', mo, w_mem_out[l])

        hn = rmsnorm_2(h, g_ffn[l])
        gu = jnp.einsum('bsd,df->bsf', hn, w_gate_up[l])
        act = jax.nn.silu(gu[..., :D_FF]) * gu[..., D_FF:]
        h = h + jnp.einsum('bsf,fd->bsd', act, w_down[l])
    return h


def setup_inputs(seed=0):
    out = dict(first_inputs(seed))
    for name, value in second_inputs(seed + 1).items():
        if name != "x":
            out[name + "_2"] = value
    return out


def reference(
    x, positions, norm_mix, norm_ffn, conv_w_in, conv_w, conv_w_out, mla_w_down, mla_q_a_norm,
    mla_kv_a_norm, mla_w_uq, mla_w_ukv, mla_q_norm, mla_k_norm, mla_w_o, ffn_w_gate, ffn_w_up,
    ffn_w_down, moe_router, moe_w_gate, moe_w_up, moe_w_down, mem_2, g_mix_2, w_in_2,
    b_forget_2, g_q_fox_2, g_k_fox_2, w_pool_2, pool_scale_2, w_out_2, g_mem_q_2, g_mem_kv_2,
    w_mem_q_2, w_mem_kv_2, g_q_mem_2, g_k_mem_2, w_mem_out_2, g_ffn_2, w_gate_up_2, w_down_2,
):
    x = first_block(
        x, positions, norm_mix, norm_ffn, conv_w_in, conv_w, conv_w_out, mla_w_down,
        mla_q_a_norm, mla_kv_a_norm, mla_w_uq, mla_w_ukv, mla_q_norm, mla_k_norm, mla_w_o,
        ffn_w_gate, ffn_w_up, ffn_w_down, moe_router, moe_w_gate, moe_w_up, moe_w_down,
    )
    return second_block(
        x, mem_2, g_mix_2, w_in_2, b_forget_2, g_q_fox_2, g_k_fox_2, w_pool_2, pool_scale_2,
        w_out_2, g_mem_q_2, g_mem_kv_2, w_mem_q_2, w_mem_kv_2, g_q_mem_2, g_k_mem_2,
        w_mem_out_2, g_ffn_2, w_gate_up_2, w_down_2,
    )


_drawn_inputs = setup_inputs


def setup_inputs(seed=0):
    import zlib

    import numpy as np

    out = dict(_drawn_inputs(seed))
    spreads = {}
    factors = {'mla_q_a_norm': 8.0,
     'mla_kv_a_norm': 6.504,
     'mla_q_norm': 8.0,
     'mla_k_norm': 7.701,
     'g_q_fox_2': 6.218,
     'g_k_fox_2': 8.0,
     'g_mem_q_2': 8.0,
     'g_mem_kv_2': 8.0,
     'g_q_mem_2': 8.0,
     'g_k_mem_2': 8.0,
     'g_ffn_2': 8.0}
    for name, (base, spread) in spreads.items():
        noise = np.random.default_rng([zlib.crc32(name.encode()), seed]).standard_normal(out[name].shape)
        drawn = base * np.exp(spread * noise) if base else spread * noise
        out[name] = __import__('jax').numpy.asarray(drawn.astype(out[name].dtype))
    for name, factor in factors.items():
        out[name] = (out[name] * factor).astype(out[name].dtype)
    return out
```

```python
from contextlib import ExitStack

import concourse.bass as bass
import numpy as np
from concourse import mybir

P = 128
F32 = mybir.dt.float32
F32R = mybir.dt.float32r
I32 = mybir.dt.int32
ALU = mybir.AluOpType
ACT = mybir.ActivationFunctionType
AX = mybir.AxisListType

D = 1024
KD = D // P
T = 2
S = T * P
HALF = 512
EPS = 1e-6
FF = 2816
KF = FF // P
FF_GROUPS = [(i * HALF, min(HALF, FF - i * HALF)) for i in range(-(-FF // HALF))]
CHUNK = 2048
RING = 4
AHEAD = 3
HEADS, NOPE, ROPE = 8, 128, 64
QK = NOPE + ROPE
Q_RANK, KV_RANK = 384, 256
KQ, KKV = Q_RANK // P, KV_RANK // P
DOWN_COLS = Q_RANK + KV_RANK + ROPE
E = 8
FE = 2048
EG = FE // HALF
EXPERT_CHUNKS = 4 * EG + FE // 256
FOX_HEADS, FOX_DIM = 8, 64
FOX = FOX_HEADS * FOX_DIM
WINDOWS = (2, 4, 8, 16)
MEM_HEADS, MEM_DIM = 4, 128
MEM = MEM_HEADS * MEM_DIM
NEG = -1e30
JOB_SCATTER, JOB_TURN, JOB_PUT, JOB_GATHER, JOB_GATE = (0, 1, 3, 4), (2, 5, 7, 11), 6, (8, 9), 10
JOBS, PROLOGUE_JOBS = 12, 4

C_IDENT, C_MASK, C_BEFORE, C_UPTO, C_ONES, C_IOTA, C_FREQ, C_TIE, C_SEL = np.cumsum(
    [0, P, 3 * P, P, P, P, P, ROPE // 2, E]).tolist()
C_END = C_SEL + FOX_HEADS * P


def shape_constants():
    c = np.zeros((P, C_END), np.float32)
    row, col = np.arange(P)[:, None], np.arange(P)[None, :]
    c[:, C_IDENT:C_IDENT + P] = row == col
    for at in (0, 2 * P):
        c[:, C_MASK + at:C_MASK + at + P] = np.where(col <= row, 0.0, NEG)
    c[:, C_BEFORE:C_BEFORE + P] = row < col
    c[:, C_UPTO:C_UPTO + P] = row <= col
    c[:, C_ONES:C_ONES + P] = 1.0
    c[:, C_IOTA:C_IOTA + P] = col
    c[:, C_FREQ:C_FREQ + ROPE // 2] = np.float32(10000.0) ** (
        -np.arange(0, ROPE, 2, dtype=np.float32) / np.float32(ROPE))
    c[:, C_TIE:C_TIE + E] = E - np.arange(E)
    for h in range(FOX_HEADS):
        c[h, C_SEL + h * P:C_SEL + (h + 1) * P] = -(FOX_DIM ** 0.5)
    bands = np.zeros((P, len(WINDOWS), T, S), np.float32)
    now = np.arange(S)[None, :]
    for g, w in enumerate(WINDOWS):
        for t in range(T):
            then = t * P + np.arange(P)[:, None]
            inside = (then <= now) & (then > now - w)
            bands[:, g, t] = inside / np.minimum(now + 1, w) - (then == now)
    return c, bands.reshape(P, -1)


GAINS = [
    ("norm_mix0", 8), ("norm_ffn0", 8), ("conv_w", 24), ("norm_mix1", 8), ("q_a", 3), ("kv_a", 2),
    ("q_nope", 1), ("k_nope", 1), ("g_mix_2", 8), ("g_q_fox", 1), ("g_k_fox", 1), ("pool_scale", 4),
    ("g_mem_q", 8), ("g_mem_kv", 8), ("g_q_mem", 1), ("g_k_mem", 1), ("g_ffn_2", 8)]
GAIN_AT = {name: sum(n for _, n in GAINS[:i]) for i, (name, _) in enumerate(GAINS)}
N_GAINS = sum(n for _, n in GAINS)


def weight_stream(A):
    def rows(w, k0, kn, c0, n):
        return w[k0 * P:(k0 + kn) * P, c0:c0 + n].rearrange("(k p) n -> p k n", p=P)

    def tall(name, w, k, c0, n):
        step = min(k, CHUNK // n)
        return [(name, rows(w, k0, step, c0, n), step, n) for k0 in range(0, k, step)]

    def wide(name, w, k):
        return [(name, rows(w, k0, 2, 0, D), 2, D) for k0 in range(0, k, 2)]

    def ffn(tag, gate, gate_at, up, up_at, down):
        out = []
        for c0, n in FF_GROUPS:
            out += tall(tag + "_up", gate, KD, gate_at + c0, n) + tall(tag + "_up", up, KD, up_at + c0, n)
        return out + wide(tag + "_down", down, KF)

    first = []
    for half in range(2):
        for part in (1, 2, 0):
            first += tall("conv_in", A["conv_w_in"][0], KD, part * D + half * HALF, HALF)
    first += wide("conv_out", A["conv_w_out"][0], KD)
    first += ffn("ffn1", A["ffn_w_gate"][0], 0, A["ffn_w_up"][0], 0, A["ffn_w_down"][0])
    for q in range(2):
        w, n = A["mla_w_down"][0], DOWN_COLS // 2
        first += [("mla_down", rows(w, k0, 4, q * n, n), 4, n) for k0 in (0, 4)]
    for q in range(3):
        first.append(("mla_uq", rows(A["mla_w_uq"][0], 0, KQ, q * HALF, HALF), KQ, HALF))
    for q in range(2):
        first.append(("mla_ukv", rows(A["mla_w_ukv"][0], 0, KKV, q * D, D), KKV, D))
    first += wide("mla_o", A["mla_w_o"][0], KD)

    last = []
    for q in range(4):
        last += tall("fox_in", A["w_in_2"][0], KD, q * HALF, HALF)
    last += wide("fox_out", A["w_out_2"][0], KD)
    for q in range(2):
        last += tall("mem_kv", A["w_mem_kv_2"][0], KD, q * HALF, HALF)
    last += tall("mem_q", A["w_mem_q_2"][0], KD, 0, HALF)
    last += wide("mem_out", A["w_mem_out_2"][0], MEM // P)
    gu = A["w_gate_up_2"][0]
    last += ffn("ffn2", gu, 0, gu, FF, A["w_down_2"][0])
    return first, last


def expert_chunk(A, e, c):
    if c < 4 * EG:
        g, part, half = c // 4, c // 2 % 2, c % 2
        w = A["moe_w_up" if part else "moe_w_gate"][0]
        v = w[bass.ds(e, 1), half * 4 * P:(half + 1) * 4 * P, g * HALF:(g + 1) * HALF]
        return v.rearrange("e (k p) n -> p (e k) n", p=P), 4, HALF
    k0 = 2 * (c - 4 * EG)
    v = A["moe_w_down"][0][bass.ds(e, 1), k0 * P:(k0 + 2) * P, :]
    return v.rearrange("e (k p) n -> p (e k) n", p=P), 2, D


def build(nc, A, out, upto=None):
    first, last = weight_stream(A)
    start_of = {}
    for chunks in (first, last):
        for i, c in enumerate(chunks):
            start_of.setdefault(c[0], i)
    MOE0 = len(first)
    PARTS = ["conv", "ffn1", "mla", "moe", "fox", "mem", "ffn2"]
    parts = PARTS if upto is None else PARTS[:PARTS.index(upto) + 1]

    with ExitStack() as ctx:
        sems = {}

        def sem(name):
            if name not in sems:
                sems[name] = ctx.enter_context(nc.semaphore(name))
            return sems[name]

        def sb(name, shape, dt=F32):
            return ctx.enter_context(nc.sbuf_tensor(name, shape, dt))

        raw = sb("raw", [P, RING, CHUNK])
        w_hi = sb("w_hi", [P, RING, CHUNK], F32R)
        w_lo = sb("w_lo", [P, RING, CHUNK], F32R)
        x = sb("x", [P, T, D])
        xT_hi = sb("xT_hi", [P, KD, S], F32R)
        xT_lo = sb("xT_lo", [P, KD, S], F32R)
        junk = sb("junk", [P, T, D], mybir.dt.bfloat16)
        const = sb("const", [P, C_END])
        gain = sb("gain", [P, N_GAINS])
        eps = sb("eps", [P, 1])
        sumsq = sb("sumsq", [P, T])
        root = sb("root", [P, T])
        rinv = sb("rinv", [P, T])
        router = sb("router", [P, KD, E])
        forget_w = sb("forget_w", [P, KD, FOX_HEADS])
        forget_b = sb("forget_b", [P, FOX_HEADS])
        rope_g = sb("rope_g", [P, 2, ROPE])
        pos_i = sb("pos_i", [P, T], I32)
        pos_f = sb("pos_f", [P, T])
        angle = sb("angle", [P, 2, T, ROPE // 2])
        turns = sb("turns", [P, T, ROPE // 2])
        cos2 = sb("cos2", [P, T, 2, ROPE // 2])
        sin = sb("sin", [P, T, ROPE // 2])
        nsin = sb("nsin", [P, T, ROPE // 2])
        overflow = sb("overflow", [1, 1], I32)
        ident = const[:, C_IDENT:C_IDENT + P]
        mask = const[:, C_MASK:C_MASK + 3 * P]
        earlier = const[:, C_BEFORE:C_BEFORE + P]
        upto_now = const[:, C_UPTO:C_UPTO + P]
        ones = const[:, C_ONES:C_ONES + P]
        iota = const[:, C_IOTA:C_IOTA + P]

        M = {}

        def region(**shapes):
            with ExitStack() as inner:
                for name, spec in shapes.items():
                    shape, dt = spec if isinstance(spec, tuple) else (spec, F32)
                    M[name] = inner.enter_context(nc.sbuf_tensor(name, shape, dt))

        region(gain_rows=[P, P], conv_c=[P, T, HALF], conv_v=[P, T, HALF], conv_b=[P, T, HALF],
               vT=[P, KD, S + 2], conv_t=[P, S], conv_y=[P, 4, S],
               yT_hi=([P, KD, S], F32R), yT_lo=([P, KD, S], F32R))
        for p in ("ffn1", "ffn2"):
            region(**{p + "_silu": [P, T, HALF], p + "_act": [P, T, HALF],
                      p + "_hi": ([P, KF, S], F32R), p + "_lo": ([P, KF, S], F32R)})
        region(dn=[P, T, DOWN_COLS], q=[P, T, HEADS * QK], kv=[P, T, HEADS * 2 * P],
               rope=[P, T, 2 * HEADS, ROPE], tmp=[P, CHUNK], cT_hi=([P, KQ + KKV, S], F32R),
               cT_lo=([P, KQ + KKV, S], F32R), qkT=[P, 2, 2 * S], ropeT=[ROPE, 2, 2 * S],
               mla_st=[P, 2, 4, 2],
               c_ss=[P, 4], c_root=[P, 4], c_rinv=[P, 4], rope_ss=[P, T],
               qk_ss=[P, T, 2 * HEADS], qk_root=[P, T, 2 * HEADS], qk_rinv=[P, T, 2 * HEADS])
        region(moe_g=[P, D], h=[P, T, D], hT=[P, KD, S], rt=[P, 20, T, E], rc=[P, 8, T],
               slot_of=[P, T, 2 * E + 1], gate_of=[P, T, 2 * E + 1], most=[P, 2],
               pick=[P, T, P], put=[P, S], gslot=[P, 1],
               gT_hi=([P, KD, P], F32R), gT_lo=([P, KD, P], F32R), e_silu=[P, HALF], e_act=[P, HALF],
               eT_hi=([P, FE // P, P], F32R), eT_lo=([P, FE // P, P], F32R), y=[P, D])
        region(z=[P, T, 3 * FOX + HALF], fqT=[P, FOX_HEADS // 2, S], fkT=[P, FOX_HEADS // 2, S],
               mixed=[P, S], cs=[P, 6, T, FOX_HEADS], cT=[FOX_HEADS, S],
               f_ss=[P, T, 2 * FOX_HEADS], f_root=[P, T, 2 * FOX_HEADS], f_rinv=[P, T, 2 * FOX_HEADS],
               fox_st=[P, 2, 4, 2], fox_tmp=[P, CHUNK], bands=[P, len(WINDOWS), T, S], w_pool=[P, len(WINDOWS), P])
        region(mem=[P, T, D], mkv=[P, T, 2 * MEM], mkT=[P, MEM_HEADS, S], mq=[P, T, MEM], mqT=[P, MEM_HEADS, S],
               memT_hi=([P, KD, S], F32R), memT_lo=([P, KD, S], F32R), m_ss=[P, T], m_root=[P, T], m_rinv=[P, T],
               mh_ss=[P, 2, T, MEM_HEADS], mh_root=[P, 2, T, MEM_HEADS], mh_rinv=[P, 2, T, MEM_HEADS],
               mem_st=[P, 2, 4, 2], mem_tmp=[P, 5 * HALF])

        def scratch(v, width):
            return (v[:, :width], v[:, width:3 * width].rearrange("p (b n) -> p b n", b=2),
                    v[:, 3 * width:5 * width].rearrange("p (b n) -> p b n", b=2))

        M["mla_s"], M["mla_p"], M["mla_pT"] = scratch(M["tmp"], 3 * P)
        M["fox_s"], M["fox_p"], M["fox_pT"] = scratch(M["fox_tmp"], 3 * P)
        M["mem_s"], M["mem_p"], M["mem_pT"] = scratch(M["mem_tmp"], 4 * P)

        bank = [ctx.enter_context(nc.psum_tensor(f"bank{i}", [P, HALF], F32)) for i in range(8)]
        block = ctx.enter_context(nc.Block())

        class Stream:
            def __init__(self, tag, chunks):
                self.chunks = chunks
                self.landed = [sem(f"{tag}_landed{i}") for i in range(RING)]
                self.high, self.low, self.used = sem(tag + "_high"), sem(tag + "_low"), sem(tag + "_used")

            def size(self, i):
                return self.chunks[i][2] * self.chunks[i][3] if i < len(self.chunks) else CHUNK

        W1, W2 = Stream("w1", first), Stream("w2", last)

        def load(i, e, stream, view, k, n):
            slot = i % RING
            if i >= RING:
                nc.sync.wait_ge(stream.low, i - RING + 1 + EXPERT_CHUNKS * e)
            nc.sync.dma_start(raw[:, slot, :k * n].rearrange("p (k n) -> p k n", k=k), view)\
                .then_inc(stream.landed[slot], 16)

        def split_high(i, e, stream):
            slot, n = i % RING, stream.size(i)
            nc.scalar.wait_ge(stream.landed[slot], 16 * (i // RING + 1) + 16 * (EXPERT_CHUNKS // RING) * e)
            if i >= RING:
                nc.scalar.wait_ge(stream.used, i - RING + 1 + EXPERT_CHUNKS * e)
            nc.scalar.activation(w_hi[:, slot, :n], raw[:, slot, :n], ACT.Copy).then_inc(stream.high, 1)

        def split_low(i, e, stream):
            slot, n = i % RING, stream.size(i)
            nc.vector.wait_ge(stream.high, i + 1 + EXPERT_CHUNKS * e)
            nc.vector.tensor_tensor(w_lo[:, slot, :n], raw[:, slot, :n], w_hi[:, slot, :n].bitcast(F32),
                                    ALU.subtract).then_inc(stream.low, 1)

        norm_parts = ["conv", "ffn1", "mla", "moe", "fox", "memkv", "mem", "ffn2"]
        per_norm, ffns = {p: 1 for p in norm_parts}, {"ffn1": 1, "ffn2": 1}
        heads = {"mla": HEADS, "fox": FOX_HEADS, "mem": MEM_HEADS}
        gives = {"xT_turned": (4, per_norm), "xT_high": (4, per_norm | {"moe": 0}), "xT_low": (4, per_norm | {"moe": 0}),
                 "squares": (T, per_norm), "root": (1, per_norm), "rinv": (1, per_norm),
                 "silu_done": (len(FF_GROUPS), ffns), "act_done": (len(FF_GROUPS), ffns),
                 "act_turned": (KF // 2, ffns), "act_high": (KF // 2, ffns), "act_low": (KF // 2, ffns),
                 "x_updated": (4, {p: 1 for p in PARTS})}
        gives |= {n: (1, heads) for n in ("scores_in_psum", "scores_ready", "exps_done", "probs_ready", "pT_turned", "pT",
                                          "values_in_psum", "value_high", "value_low")}

        def before(part, signal):
            times, by = gives[signal]
            names = list(by)
            return times * sum(by[n] for n in names[:names.index(part)])

        class Splitter:
            def __init__(self, split, stream, end):
                self.split, self.stream, self.end, self.done = split, stream, end, 0

            def ahead(self, i):
                while self.done < min(i + AHEAD + 1, self.end):
                    self.split(self.done, 0, self.stream)
                    self.done += 1

        ENDS1 = MOE0 + AHEAD if "moe" in parts else min(MOE0, start_of.get({"conv": "ffn1_up", "ffn1": "mla_down"}.get(parts[-1], ""), MOE0))
        ENDS2 = {"moe": 0, "fox": start_of["mem_kv"], "mem": start_of["ffn2_up"]}.get(parts[-1], len(last))

        x_ready = {"conv": ("loaded_x", 16)} | {p: ("x_updated", before(p, "x_updated")) for p in PARTS[1:]}
        GAIN_OF = {"conv": "norm_mix0", "ffn1": "norm_ffn0", "mla": "norm_mix1", "fox": "g_mix_2",
                   "mem": "g_mem_q", "ffn2": "g_ffn_2"}

        def g(name, k=0):
            return gain[:, GAIN_AT[name] + k:GAIN_AT[name] + k + 1]

        def per_feature(c, n):
            return c.unsqueeze(len(c.shape)).broadcast_to(list(c.shape) + [n])

        @block.sync
        def _(sp):
            sp.dma_start(x[:, :, :], A["x"][0].rearrange("(t p) d -> p t d", p=P)).then_inc(sem("loaded_x"), 16)
            sp.dma_start(const[:, :], A["shape_const"]).then_inc(sem("loaded_const"), 16)
            for i, (_, view, k, n) in enumerate(first[:min(ENDS1, MOE0)]):
                load(i, 0, W1, view, k, n)
            if "moe" in parts:
                with sp.Fori(0, E) as e:
                    for c in range(EXPERT_CHUNKS):
                        load(MOE0 + c, e, W1, *expert_chunk(A, e, c))
                sp.wait_ge(sem("overflow_known"), 1)
                over = sp.value_load(overflow[0:1, 0:1], min_val=0, max_val=1)
                with sp.If(over > 0):
                    with sp.Fori(0, E) as e:
                        for c in range(EXPERT_CHUNKS):
                            load(MOE0 + E * EXPERT_CHUNKS + c, e, W1, *expert_chunk(A, e, c))
                if ENDS2:
                    sp.wait_ge(W1.low, MOE0 + E * EXPERT_CHUNKS + over * (E * EXPERT_CHUNKS))
                for i, (_, view, k, n) in enumerate(last[:ENDS2]):
                    load(i, 0, W2, view, k, n)
            for t in range(T):
                sp.wait_ge(sem("x_updated"), before(parts[-1], "x_updated") + 2 * t + 2)
                sp.dma_start(out[0, t * P:(t + 1) * P, :], x[:, t, :]).then_inc(sem("stored"), 16)
            sp.wait_ge(sem("stored"), 16 * T)

        @block.gpsimd
        def _(pool):
            def small(dst, src, name, scattered=False):
                pool.dma_start(dst, src, allow_slow_non_contiguous=scattered).then_inc(sem("loaded_" + name), 16)

            small(pos_i[:, :], A["positions"][0].rearrange("(t p) -> p t", p=P), "rope", True)
            small(rope_g[:, 0, :], A["mla_q_norm"][0:1, NOPE:].partition_broadcast(P), "rope")
            small(rope_g[:, 1, :], A["mla_k_norm"][0:1, NOPE:].partition_broadcast(P), "rope")
            small(router[:, :, :], A["moe_router"][0].rearrange("(k p) e -> p k e", p=P), "router")
            small(forget_w[:, :, :], A["w_in_2"][0][:, 3 * FOX + HALF:].rearrange("(k p) h -> p k h", p=P), "forget")
            small(forget_b[:, :], A["b_forget_2"][0:1, :].partition_broadcast(P), "forget")
            if "moe" in parts:
                pool.wait_ge(sem("x_updated"), before("mla", "x_updated") + 4)
                small(M["moe_g"][:, :], A["norm_ffn"][1:2, :].partition_broadcast(P), "moe_g")
            if "fox" in parts:
                pool.wait_ge(sem("x_updated"), before("moe", "x_updated") + 4)
                small(M["bands"][:, :, :, :].rearrange("p g t s -> p (g t s)"), A["shape_bands"], "pool")
                small(M["w_pool"][:, :, :], A["w_pool_2"][0].rearrange("g c d -> c g d"), "pool")
            if "mem" in parts:
                pool.wait_ge(sem("x_updated"), before("fox", "x_updated") + 4)
                small(M["mem"][:, :, :], A["mem_2"][0].rearrange("(t p) d -> p t d", p=P), "mem")

        @block.scalar
        def _(act):
            A_ = nc.scalar.activation
            at = GAIN_AT
            rows = M["gain_rows"]

            def load_rows(name, src, n):
                act.dma_start(rows[at[name]:at[name] + n, :], src).then_inc(sem("loaded_gains"), 16)

            def rows_of(v):
                return v.rearrange("(k p) -> k p", p=P)

            def load_pair(name, src):
                for half in (0, 1):
                    act.dma_start(rows[at[name]:at[name] + 1, half * FOX_DIM:(half + 1) * FOX_DIM],
                                  src).then_inc(sem("loaded_gains"), 16)

            load_rows("norm_mix0", rows_of(A["norm_mix"][0]), 8)
            load_rows("norm_ffn0", rows_of(A["norm_ffn"][0]), 8)
            load_rows("conv_w", A["conv_w"][0].rearrange("w (k p) -> (w k) p", p=P), 24)
            load_rows("norm_mix1", rows_of(A["norm_mix"][1]), 8)
            load_rows("q_a", rows_of(A["mla_q_a_norm"][0]), 3)
            load_rows("kv_a", rows_of(A["mla_kv_a_norm"][0]), 2)
            load_rows("q_nope", A["mla_q_norm"][0:1, :NOPE], 1)
            load_rows("k_nope", A["mla_k_norm"][0:1, :NOPE], 1)
            load_rows("g_mix_2", rows_of(A["g_mix_2"][0]), 8)
            load_pair("g_q_fox", A["g_q_fox_2"])
            load_pair("g_k_fox", A["g_k_fox_2"])
            load_rows("pool_scale", rows_of(A["pool_scale_2"][0]), 4)
            load_rows("g_mem_q", rows_of(A["g_mem_q_2"][0]), 8)
            load_rows("g_mem_kv", rows_of(A["g_mem_kv_2"][0]), 8)
            load_rows("g_q_mem", A["g_q_mem_2"], 1)
            load_rows("g_k_mem", A["g_k_mem_2"], 1)
            load_rows("g_ffn_2", rows_of(A["g_ffn_2"][0]), 8)

            w1, w2 = Splitter(split_high, W1, ENDS1), Splitter(split_high, W2, ENDS2)

            def used(w, i):
                w.ahead(i)
                act.wait_ge(w.stream.used, i + 1)

            def norm(p, src, ready, gname, hi, ss, rt, n=D):
                act.wait_ge(sem(ready[0]), ready[1])
                for b in range(4):
                    act.wait_ge(sem("xT_turned"), before(p, "xT_turned") + b + 1)
                    for j in range(2):
                        k = 2 * b + j
                        ins = A_(hi[:, k, :], bank[4 + b][:, j * S:(j + 1) * S], ACT.Copy, scale=g(gname, k))
                    ins.then_inc(sem("xT_high"), 1)
                mean_square(p, src, ss, rt)

            def mean_square(p, src, ss, rt):
                for t in range(T):
                    ins = A_(junk[:, t, :], src[:, t, :], ACT.Square, accum_out=ss[:, t:t + 1])
                    ins.then_inc(sem("squares"), 1)
                act.wait_ge(sem("squares"), before(p, "squares") + T)
                A_(rt[:, :], ss[:, :], ACT.Sqrt, bias=eps[:, :], scale=1.0 / D).then_inc(sem("root"), 1)

            def ffn(p, w):
                first_chunk, hi = start_of[p + "_up"], M[p + "_hi"]
                norm(p, x, x_ready[p], GAIN_OF[p], xT_hi, sumsq, root)
                act.wait_ge(sem("rinv"), before(p, "rinv") + 1)
                turned = 0

                def act_high(group):
                    nonlocal turned
                    for j in range(FF_GROUPS[group][1] // S):
                        act.wait_ge(sem("act_turned"), before(p, "act_turned") + turned + 1)
                        b = 4 + 2 * (group % 2) + j
                        A_(hi[:, 2 * turned:2 * turned + 2, :].rearrange("p k s -> p (k s)"), bank[b][:, :],
                           ACT.Copy).then_inc(sem("act_high"), 1)
                        turned += 1

                i = first_chunk
                for group, (_, n) in enumerate(FF_GROUPS):
                    parts_of = KD // (CHUNK // n) if CHUNK // n < KD else 1
                    used(w, i + parts_of - 1)
                    i += 2 * parts_of
                    if group:
                        act.wait_ge(sem("act_done"), before(p, "act_done") + group)
                    for t in range(T):
                        ins = A_(M[p + "_silu"][:, t, :n], bank[t][:, :n], ACT.Silu, scale=rinv[:, t:t + 1])
                    ins.then_inc(sem("silu_done"), 1)
                    if group:
                        act_high(group - 1)
                w.ahead(i - 1)
                act_high(len(FF_GROUPS) - 1)
                w.ahead(start_of[p + "_down"] + KF // 2 - 1)

            def attention(p, n_heads, blocks, scale, turn, value_part):
                st, s_, p_, pT = M[p + "_st"], M[p + "_s"], M[p + "_p"], M[p + "_pT"]
                width = blocks[-1][1]

                def exps(h):
                    act.wait_ge(sem("scores_ready"), before(p, "scores_ready") + h + 1)
                    if h >= 2:
                        act.wait_ge(sem("pT_turned"), before(p, "pT_turned") + h - 1)
                    for t, (a, b) in enumerate(blocks):
                        ins = A_(p_[:, h % 2, a:b], s_[:, a:b], ACT.Exp, bias=st[:, h % 2, 1, t:t + 1],
                                 scale=scale, accum_out=st[:, h % 2, 2, t:t + 1])
                    ins.then_inc(sem("exps_done"), 1)

                turn(0)
                exps(0)
                for h in range(n_heads):
                    if h + 1 < n_heads:
                        turn(h + 1)
                    act.wait_ge(sem("pT_turned"), before(p, "pT_turned") + h + 1)
                    if h >= 2:
                        act.wait_ge(sem("values_in_psum"), before(p, "values_in_psum") + h - 1)
                    A_(pT[:, h % 2, :], bank[7][:, :width], ACT.Copy).then_inc(sem("pT"), 1)
                    if h + 1 < n_heads:
                        exps(h + 1)
                    act.wait_ge(sem("values_in_psum"), before(p, "values_in_psum") + h + 1)
                    dst, src = value_part(h, xT_hi)
                    A_(dst, src, ACT.Copy).then_inc(sem("value_high"), 1)

            act.wait_ge(sem("gains_turned"), 1)
            A_(gain[:, :], bank[0][:, :N_GAINS], ACT.Copy).then_inc(sem("gains_ready"), 1)
            act.wait_ge(sem("angles"), 1)
            act.wait_ge(sem("gains_ready"), 1)
            for j in range(2):
                A_(cos2[:, :, j, :], angle[:, 1, :, :], ACT.Sin)
            A_(sin[:, :, :], angle[:, 0, :, :], ACT.Sin).then_inc(sem("rope_tables"), 1)
            act.wait_ge(sem("rope_tables"), 1)
            A_(nsin[:, :, :], sin[:, :, :], ACT.Copy, scale=-1.0).then_inc(sem("rope_tables"), 1)

            w1.ahead(0)
            norm("conv", x, x_ready["conv"], GAIN_OF["conv"], xT_hi, sumsq, root)
            act.wait_ge(sem("rinv"), before("conv", "rinv") + 1)

            def conv_gate(q, buf, name):
                used(w1, 2 * q + 1)
                for t in range(T):
                    ins = A_(buf[:, t, :], bank[2 * (q % 2) + t][:, :], ACT.Copy, scale=rinv[:, t:t + 1])
                ins.then_inc(sem(name), 1)

            def conv_v_turned(half):
                for j in range(2):
                    act.wait_ge(sem("conv_v_turned"), 2 * half + j + 1)
                    k = 4 * half + 2 * j
                    A_(M["vT"][:, k:k + 2, 2:], bank[4 + j][:, :].rearrange("p (k s) -> p k s", k=2),
                       ACT.Copy).then_inc(sem("conv_vT"), 1)

            def conv_high(half):
                act.wait_ge(sem("conv_y_done"), 4 * half + 4)
                A_(M["yT_hi"][:, 4 * half:4 * half + 4, :], M["conv_y"][:, :, :], ACT.Copy)\
                    .then_inc(sem("conv_y_high"), 1)

            conv_gate(0, M["conv_c"], "conv_c_done")
            conv_gate(2, M["conv_b"], "conv_b_done")
            conv_v_turned(0)
            act.wait_ge(sem("conv_v_done"), 1)
            conv_gate(3, M["conv_c"], "conv_c_done")
            w1.ahead(9)
            conv_high(0)
            act.wait_ge(sem("conv_b_turned"), 2)
            conv_gate(5, M["conv_b"], "conv_b_done")
            conv_v_turned(1)
            conv_high(1)
            w1.ahead(start_of["conv_out"] + 3)

            if "ffn1" in parts:
                ffn("ffn1", w1)

            if "mla" in parts:
                dn, q, kv, tmp = M["dn"], M["q"], M["kv"], M["tmp"]
                norm("mla", x, x_ready["mla"], GAIN_OF["mla"], xT_hi, sumsq, root)
                act.wait_ge(sem("rinv"), before("mla", "rinv") + 1)
                i, n = start_of["mla_down"], DOWN_COLS // 2
                for j in range(2):
                    used(w1, i + 2 * j + 1)
                    for t in range(T):
                        ins = A_(dn[:, t, j * n:(j + 1) * n], bank[2 * j + t][:, :n], ACT.Copy,
                                 scale=rinv[:, t:t + 1])
                    ins.then_inc(sem("mla_dn"), 1)
                for b in range(3):
                    act.wait_ge(sem("mla_c_turned"), b + 1)
                    for k in range(2 * b, min(2 * b + 2, KQ + KKV)):
                        gk = g("q_a", k) if k < KQ else g("kv_a", k - KQ)
                        ins = A_(M["cT_hi"][:, k, :], bank[4 + b][:, (k % 2) * S:(k % 2 + 1) * S], ACT.Copy, scale=gk)
                    ins.then_inc(sem("mla_c_high"), 1)
                act.wait_ge(sem("mla_dn"), 2)
                for t in range(T):
                    for j, (a, b) in enumerate(((0, Q_RANK), (Q_RANK, Q_RANK + KV_RANK))):
                        ins = A_(junk[:, t, a:b], dn[:, t, a:b], ACT.Square, accum_out=M["c_ss"][:, 2 * j + t:2 * j + t + 1])
                    ins.then_inc(sem("mla_c_squares"), 1)
                act.wait_ge(sem("mla_c_squares"), T)
                A_(M["c_root"][:, 0:2], M["c_ss"][:, 0:2], ACT.Sqrt, bias=eps[:, :], scale=1.0 / Q_RANK)
                A_(M["c_root"][:, 2:4], M["c_ss"][:, 2:4], ACT.Sqrt, bias=eps[:, :], scale=1.0 / KV_RANK)\
                    .then_inc(sem("mla_c_root"), 1)
                for t in range(T):
                    ins = A_(junk[:, t, Q_RANK + KV_RANK:DOWN_COLS], dn[:, t, Q_RANK + KV_RANK:], ACT.Square,
                             accum_out=M["rope_ss"][:, t:t + 1])
                ins.then_inc(sem("mla_rope_squares"), 1)
                act.wait_ge(sem("mla_c_rinv"), 1)
                for j in range(3):
                    used(w1, start_of["mla_uq"] + j)
                    for t in range(T):
                        ins = A_(q[:, t, j * HALF:(j + 1) * HALF], bank[2 * (j % 2) + t][:, :], ACT.Copy,
                                 scale=M["c_rinv"][:, t:t + 1])
                    ins.then_inc(sem("mla_q_done"), 1)
                w1.ahead(start_of["mla_ukv"] + 1)
                for t in range(T):
                    act.wait_ge(sem("mla_q_done"), 3)
                    if t:
                        act.wait_ge(sem("mla_sums"), 2 * t)
                    A_(tmp[:, :HEADS * QK], q[:, t, :], ACT.Square).then_inc(sem("mla_qk_squares"), 1)
                    act.wait_ge(sem("mla_kv_done"), 4)
                    act.wait_ge(sem("mla_sums"), 2 * t + 1)
                    A_(tmp[:, :HEADS * NOPE].rearrange("p (h d) -> p h d", h=HEADS),
                       kv[:, t, :].rearrange("p (h d) -> p h d", h=HEADS)[:, :, :NOPE], ACT.Square)\
                        .then_inc(sem("mla_qk_squares"), 1)
                act.wait_ge(sem("mla_sums"), 2 * T)
                A_(M["qk_root"][:, :, :], M["qk_ss"][:, :, :], ACT.Sqrt, bias=eps[:, :], scale=1.0 / QK)\
                    .then_inc(sem("mla_qk_root"), 1)

                def turn(h):
                    act.wait_ge(sem("mla_nope_turned"), h + 1)
                    if h >= 2:
                        act.wait_ge(sem("scores_in_psum"), before("mla", "scores_in_psum") + h - 1)
                    A_(M["qkT"][:, h % 2, :S], bank[4][:, :S], ACT.Copy, scale=g("q_nope"))
                    A_(M["qkT"][:, h % 2, S:], bank[4][:, S:], ACT.Copy, scale=g("k_nope")).then_inc(sem("mla_qkT"), 1)

                attention("mla", HEADS, [(0, P), (P, 3 * P)], QK ** -0.5, turn,
                          lambda h, o: (o[:, h, :], bank[h % 2][:, :S]))
                w1.ahead(start_of["mla_o"] + 3)

            if "moe" in parts:
                h_, rt, rc = M["h"], M["rt"], M["rc"]
                act.wait_ge(sem("x_updated"), before("mla", "x_updated") + 4)
                mean_square("moe", x, sumsq, root)
                for b in range(4):
                    act.wait_ge(sem("xT_turned"), before("moe", "xT_turned") + b + 1)
                    A_(M["hT"][:, 2 * b:2 * b + 2, :].rearrange("p k s -> p (k s)"), bank[4 + b][:, :],
                       ACT.Copy).then_inc(sem("moe_hT"), 1)
                act.wait_ge(sem("moe_logits_ready"), 1)
                for t in range(T):
                    ins = A_(rt[:, 1, t, :], rt[:, 0, t, :], ACT.Exp, bias=rc[:, 0, t:t + 1],
                             accum_out=rc[:, 1, t:t + 1])
                ins.then_inc(sem("moe_exp"), 1)

                def job_high(job, e, dst):
                    act.wait_ge(sem("moe_job"), PROLOGUE_JOBS + job + 1 + JOBS * e)
                    A_(dst, bank[6 + job % 2][:, :], ACT.Copy).then_inc(sem("moe_job_high"), 1)

                def gather_high(job, e, half):
                    job_high(job, e, M["gT_hi"][:, 4 * half:4 * half + 4, :].rearrange("p k s -> p (k s)"))

                def turn_high(job, e, group):
                    job_high(job, e, M["eT_hi"][:, 4 * group:4 * group + 4, :].rearrange("p k s -> p (k s)"))

                def silu(e, group):
                    act.wait_ge(W1.used, MOE0 + 4 * group + 2 + EXPERT_CHUNKS * e)
                    act.wait_ge(sem("moe_act_done"), 1 + group + EG * e)
                    A_(M["e_silu"][:, :], bank[2 * (group % 2)][:, :], ACT.Silu).then_inc(sem("moe_silu_done"), 1)

                def expert(e, more):
                    for c in range(EXPERT_CHUNKS):
                        if c + AHEAD < EXPERT_CHUNKS or more:
                            split_high(MOE0 + c + AHEAD, e, W1)
                        if c in (1, 5, 9, 13):
                            silu(e, c // 4)
                        if c in (5, 9, 13):
                            turn_high(JOB_TURN[c // 4 - 1], e, c // 4 - 1)
                        if c == 15:
                            gather_high(8, e, 0)
                            gather_high(9, e, 1)
                        if c == 16:
                            turn_high(11, e, 3)
                    act.wait_ge(W1.used, MOE0 + EXPERT_CHUNKS + EXPERT_CHUNKS * e)
                    for half in range(2):
                        ins = A_(M["y"][:, half * HALF:(half + 1) * HALF], bank[4 + half][:, :], ACT.Copy)
                    ins.then_inc(sem("moe_y"), 1)

                A_(M["y"][:, :], const[:, :D], ACT.Copy, scale=0.0).then_inc(sem("moe_y"), 1)
                gather_high(-4, 0, 0)
                gather_high(-3, 0, 1)
                with act.Fori(0, E - 1) as e:
                    expert(e, True)
                expert(E - 1, False)
                act.wait_ge(sem("overflow_known"), 1)
                over = act.value_load(overflow[0:1, 0:1], min_val=0, max_val=1)
                with act.If(over > 0):
                    for c in range(AHEAD):
                        split_high(MOE0 + c, E, W1)
                    with act.Fori(E, 2 * E - 1) as e:
                        expert(e, True)
                    expert(2 * E - 1, False)

            if "fox" in parts:
                act.wait_ge(W1.used, MOE0 + E * EXPERT_CHUNKS + over * (E * EXPERT_CHUNKS))
                w2.ahead(0)

                z, cs = M["z"], M["cs"]
                norm("fox", x, x_ready["fox"], GAIN_OF["fox"], xT_hi, sumsq, root)
                act.wait_ge(sem("rinv"), before("fox", "rinv") + 1)
                for j in range(2):
                    used(w2, 2 * j + 1)
                    for t in range(T):
                        ins = A_(z[:, t, j * HALF:(j + 1) * HALF], bank[2 * j + t][:, :], ACT.Copy,
                                 scale=rinv[:, t:t + 1])
                    ins.then_inc(sem("fox_qk_done"), 1)
                w2.ahead(start_of["fox_out"] - 1)
                for t in range(T):
                    act.wait_ge(sem("fox_qk_done"), 2)
                    if t:
                        act.wait_ge(sem("fox_sums"), 1)
                    A_(M["fox_tmp"][:, :2 * FOX], z[:, t, :2 * FOX], ACT.Square).then_inc(sem("fox_head_squares"), 1)
                act.wait_ge(sem("fox_sums"), T)
                A_(M["f_root"][:, :, :], M["f_ss"][:, :, :], ACT.Sqrt, bias=eps[:, :], scale=1.0 / FOX_DIM)\
                    .then_inc(sem("fox_qk_root"), 1)
                act.wait_ge(sem("forget_abs"), 1)
                A_(cs[:, 2, :, :], cs[:, 1, :, :], ACT.Exp).then_inc(sem("forget_exp"), 1)
                act.wait_ge(sem("forget_exp"), 1)
                A_(cs[:, 3, :, :], cs[:, 2, :, :], ACT.Ln, bias=ones[:, 0:1]).then_inc(sem("forget_ln"), 1)
                w2.ahead(start_of["fox_out"] - 1)
                for k in range(len(WINDOWS)):
                    act.wait_ge(sem("pool_mixed"), k + 1)
                    if k:
                        act.wait_ge(sem("pool_mapped"), k)
                    A_(M["mixed"][:, :], bank[k % 2][:, :S], ACT.Copy).then_inc(sem("pool_mixed_copied"), 1)
                    act.wait_ge(sem("pool_mapped"), k + 1)
                    A_(xT_hi[:, KD // 2 + k, :], bank[2 + k % 2][:, :S], ACT.Copy, scale=g("pool_scale", k))\
                        .then_inc(sem("pool_high"), 1)
                for k in range(FOX_HEADS // 2):
                    act.wait_ge(sem("fox_pair_turned"), k + 1)
                    A_(M["fqT"][:, k, :], bank[4 + k % 2][:, :S], ACT.Copy, scale=g("g_q_fox"))
                    A_(M["fkT"][:, k, :], bank[4 + k % 2][:, S:], ACT.Copy, scale=g("g_k_fox"))\
                        .then_inc(sem("fox_qkT"), 1)

                def fox_value(h, o):
                    rows_ = slice(FOX_DIM * (h % 2), FOX_DIM * (h % 2 + 1))
                    return o[rows_, h // 2, :], bank[h // 2 % 2][rows_, :S]

                attention("fox", FOX_HEADS, [(0, P), (P, 3 * P)], FOX_DIM ** -0.5, lambda h: None, fox_value)
                w2.ahead(start_of["fox_out"] + 3)

            if "mem" in parts:
                mem, mkv, mq = M["mem"], M["mkv"], M["mq"]
                norm("memkv", mem, ("loaded_mem", 16), "g_mem_kv", M["memT_hi"], M["m_ss"], M["m_root"])
                norm("mem", x, x_ready["mem"], GAIN_OF["mem"], xT_hi, sumsq, root)
                act.wait_ge(sem("rinv"), before("memkv", "rinv") + 1)
                used(w2, start_of["mem_kv"] + 1)
                for t in range(T):
                    ins = A_(mkv[:, t, :MEM], bank[t][:, :], ACT.Copy, scale=M["m_rinv"][:, t:t + 1])
                ins.then_inc(sem("mem_k_done"), 1)
                act.wait_ge(sem("rinv"), before("mem", "rinv") + 1)
                used(w2, start_of["mem_q"] + 1)
                for t in range(T):
                    ins = A_(mq[:, t, :], bank[t][:, :], ACT.Copy, scale=rinv[:, t:t + 1])
                ins.then_inc(sem("mem_q_done"), 1)
                act.wait_ge(sem("mem_q_done"), 1)
                for j, src in enumerate((mkv[:, :, :MEM], mq[:, :, :])):
                    if j:
                        act.wait_ge(sem("mem_sums"), 1)
                    A_(M["mem_tmp"][:, :T * MEM].rearrange("p (t n) -> p t n", t=T), src, ACT.Square)\
                        .then_inc(sem("mem_head_squares"), 1)
                act.wait_ge(sem("mem_sums"), 2)
                A_(M["mh_root"][:, :, :, :], M["mh_ss"][:, :, :, :], ACT.Sqrt, bias=eps[:, :], scale=1.0 / MEM_DIM)\
                    .then_inc(sem("mem_qk_root"), 1)
                for k in range(MEM_HEADS):
                    act.wait_ge(sem("mem_head_turned"), k + 1)
                    A_(M["mqT"][:, k, :], bank[4 + k % 2][:, :S], ACT.Copy, scale=g("g_q_mem"))
                    A_(M["mkT"][:, k, :], bank[4 + k % 2][:, S:], ACT.Copy, scale=g("g_k_mem"))\
                        .then_inc(sem("mem_qkT"), 1)
                attention("mem", MEM_HEADS, [(0, S), (S, 2 * S)], MEM_DIM ** -0.5, lambda h: None,
                          lambda h, o: (o[:, h, :], bank[h % 2][:, :S]))
                w2.ahead(start_of["mem_out"] + 1)

            if "ffn2" in parts:
                ffn("ffn2", w2)

        @block.vector
        def _(dve):
            V = nc.vector
            links = 0

            def link(ins):
                nonlocal links
                links += 1
                ins.then_inc(sem("vector_chain"), 1)
                dve.wait_ge(sem("vector_chain"), links)

            w1, w2 = Splitter(split_low, W1, ENDS1), Splitter(split_low, W2, ENDS2)

            def used(w, i):
                w.ahead(i)
                dve.wait_ge(w.stream.used, i + 1)

            def norm_low(p, gname, lo, hi):
                for b in range(4):
                    dve.wait_ge(sem("xT_high"), before(p, "xT_high") + b + 1)
                    for j in range(2):
                        k = 2 * b + j
                        ins = V.scalar_tensor_tensor(lo[:, k, :], bank[4 + b][:, j * S:(j + 1) * S], g(gname, k),
                                                     hi[:, k, :].bitcast(F32), ALU.mult, ALU.subtract)
                    ins.then_inc(sem("xT_low"), 1)

            def inverse(of, name, n, out_, in_):
                dve.wait_ge(sem(of), n)
                V.reciprocal(out_, in_).then_inc(sem(name), 1)
                dve.wait_ge(sem(name), n)

            def norm(p):
                norm_low(p, GAIN_OF[p], xT_lo, xT_hi)
                inverse("root", "rinv", before(p, "rinv") + 1, rinv[:, :], root[:, :])

            def residual(p, w, last_chunk):
                used(w, last_chunk)
                for t in range(T):
                    for half in range(2):
                        xs = x[:, t, half * HALF:(half + 1) * HALF]
                        V.tensor_tensor(xs, xs, bank[2 * t + half][:, :], ALU.add).then_inc(sem("x_updated"), 1)
                dve.wait_ge(sem("x_updated"), before(p, "x_updated") + 4)

            def ffn(p, w):
                act_, lo, hi = M[p + "_act"], M[p + "_lo"], M[p + "_hi"]
                norm(p)
                turned = 0

                def act_low(group):
                    nonlocal turned
                    for j in range(FF_GROUPS[group][1] // S):
                        dve.wait_ge(sem("act_high"), before(p, "act_high") + turned + 1)
                        b = 4 + 2 * (group % 2) + j
                        pair = slice(2 * turned, 2 * turned + 2)
                        V.tensor_tensor(lo[:, pair, :].rearrange("p k s -> p (k s)"), bank[b][:, :],
                                        hi[:, pair, :].bitcast(F32).rearrange("p k s -> p (k s)"),
                                        ALU.subtract).then_inc(sem("act_low"), 1)
                        turned += 1

                i = start_of[p + "_up"]
                for group, (_, n) in enumerate(FF_GROUPS):
                    parts_of = KD // (CHUNK // n) if CHUNK // n < KD else 1
                    i += 2 * parts_of
                    if group:
                        w.ahead(i - parts_of - 1)
                        act_low(group - 1)
                    used(w, i - 1)
                    dve.wait_ge(sem("silu_done"), before(p, "silu_done") + group + 1)
                    for t in range(T):
                        ins = V.scalar_tensor_tensor(act_[:, t, :n], bank[2 + t][:, :n], rinv[:, t:t + 1],
                                                     M[p + "_silu"][:, t, :n], ALU.mult, ALU.mult)
                    ins.then_inc(sem("act_done"), 1)
                w.ahead(i - 1)
                act_low(len(FF_GROUPS) - 1)
                residual(p, w, start_of[p + "_down"] + KF // 2 - 1)

            def attention(p, n_heads, blocks, scale, turn, add_bias, value_part):
                st, s_, p_ = M[p + "_st"], M[p + "_s"], M[p + "_p"]

                def scores(h):
                    dve.wait_ge(sem("scores_in_psum"), before(p, "scores_in_psum") + h + 1)
                    if h:
                        dve.wait_ge(sem("exps_done"), before(p, "exps_done") + h)
                    add_bias(h, s_)
                    for t, (a, b) in enumerate(blocks):
                        ins = V.tensor_reduce(st[:, h % 2, 0, t:t + 1], s_[:, a:b], AX.X, ALU.max)
                    link(ins)
                    V.tensor_scalar(st[:, h % 2, 1, :], st[:, h % 2, 0, :], -scale, None, ALU.mult)\
                        .then_inc(sem("scores_ready"), 1)

                def probabilities(h):
                    dve.wait_ge(sem("exps_done"), before(p, "exps_done") + h + 1)
                    link(V.reciprocal(st[:, h % 2, 3, :], st[:, h % 2, 2, :]))
                    for t, (a, b) in enumerate(blocks):
                        ins = V.tensor_scalar(p_[:, h % 2, a:b], p_[:, h % 2, a:b], st[:, h % 2, 3, t:t + 1], None,
                                              ALU.mult)
                    ins.then_inc(sem("probs_ready"), 1)

                turn(0)
                scores(0)
                probabilities(0)
                for h in range(n_heads):
                    if h + 1 < n_heads:
                        turn(h + 1)
                        scores(h + 1)
                    dve.wait_ge(sem("value_high"), before(p, "value_high") + h + 1)
                    lo_, src = value_part(h, xT_lo)
                    hi_, _ = value_part(h, xT_hi)
                    V.tensor_tensor(lo_, src, hi_.bitcast(F32), ALU.subtract).then_inc(sem("value_low"), 1)
                    if h + 1 < n_heads:
                        probabilities(h + 1)

            V.memset(eps[:, :], EPS).then_inc(sem("zeroed"), 1)
            V.memset(M["vT"][:, :, 0:2], 0.0).then_inc(sem("zeroed"), 1)
            dve.wait_ge(sem("zeroed"), 2)
            dve.wait_ge(sem("loaded_rope"), 48)
            dve.wait_ge(sem("loaded_const"), 16)
            link(V.tensor_copy(pos_f[:, :], pos_i[:, :]))
            freq = const[:, C_FREQ:C_FREQ + ROPE // 2]
            for t in range(T):
                ins = V.tensor_scalar(angle[:, 0, t, :], freq, pos_f[:, t:t + 1], None, ALU.mult)
            link(ins)
            a0, a1 = angle[:, 0, :, :], angle[:, 1, :, :]
            link(V.tensor_scalar(turns[:, :, :], a0, float(1 / (2 * np.pi)), 1.5 * 2.0 ** 23, ALU.mult, ALU.add))
            link(V.tensor_scalar(turns[:, :, :], turns[:, :, :], 1.5 * 2.0 ** 23, None, ALU.subtract))
            two_pi = 2 * np.pi
            c1 = 6.28125
            c2 = float(np.round((two_pi - c1) * 2.0 ** 20) / 2.0 ** 20)
            c3 = float(two_pi - c1 - c2)
            for c in (c1, c2, c3):
                link(V.scalar_tensor_tensor(a0, turns[:, :, :], -c, a0, ALU.mult, ALU.add))
            link(V.tensor_scalar(a1, a0, float(np.pi / 2), None, ALU.add))
            link(V.tensor_scalar(turns[:, :, :], a1, float(np.pi), -two_pi, ALU.is_gt, ALU.mult))
            link(V.tensor_tensor(a1, a1, turns[:, :, :], ALU.add))
            V.tensor_scalar(angle[:, :, :, :], angle[:, :, :, :], 3.1415925, -3.1415925, ALU.min, ALU.max)\
                .then_inc(sem("angles"), 1)

            dve.wait_ge(sem("gains_ready"), 1)
            w1.ahead(0)
            norm("conv")

            def conv_v(half):
                used(w1, 6 * half + 3)
                dve.wait_ge(sem("conv_c_done"), half + 1)
                if half:
                    dve.wait_ge(sem("conv_v_turned"), 2)
                for t in range(T):
                    ins = V.scalar_tensor_tensor(M["conv_v"][:, t, :], bank[2 * ((3 * half + 1) % 2) + t][:, :],
                                                 rinv[:, t:t + 1], M["conv_c"][:, t, :], ALU.mult, ALU.mult)
                ins.then_inc(sem("conv_v_done"), 1)

            def conv_taps(half):
                if half:
                    dve.wait_ge(sem("conv_y_high"), 1)
                for k in range(4 * half, 4 * half + 4):
                    j = k // 2 % 2
                    dve.wait_ge(sem("conv_vT"), 2 * half + j + 1)
                    vT, t1 = M["vT"], M["conv_t"][:, :]
                    link(V.tensor_scalar(t1, vT[:, k, 0:S], g("conv_w", k), None, ALU.mult))
                    for tap in (1, 2):
                        link(V.scalar_tensor_tensor(t1, vT[:, k, tap:tap + S], g("conv_w", KD * tap + k), t1,
                                                    ALU.mult, ALU.add))
                    dve.wait_ge(sem("conv_b_turned"), 2 * half + j + 1)
                    V.tensor_tensor(M["conv_y"][:, k % 4, :], t1, bank[6 + j][:, (k % 2) * S:(k % 2 + 1) * S],
                                    ALU.mult).then_inc(sem("conv_y_done"), 1)
                    dve.wait_ge(sem("conv_y_done"), k + 1)
                dve.wait_ge(sem("conv_y_high"), half + 1)
                part = slice(4 * half, 4 * half + 4)
                V.tensor_tensor(M["yT_lo"][:, part, :], M["conv_y"][:, :, :], M["yT_hi"][:, part, :].bitcast(F32),
                                ALU.subtract).then_inc(sem("conv_y_low"), 1)

            conv_v(0)
            w1.ahead(8)
            conv_taps(0)
            conv_v(1)
            w1.ahead(11)
            conv_taps(1)
            residual("conv", w1, start_of["conv_out"] + 3)

            if "ffn1" in parts:
                ffn("ffn1", w1)

            if "mla" in parts:
                dn, q, kv, tmp, rp = M["dn"], M["q"], M["kv"], M["tmp"], M["rope"]
                norm("mla")
                w1.ahead(start_of["mla_down"] + 3)
                for b in range(3):
                    dve.wait_ge(sem("mla_c_high"), b + 1)
                    for k in range(2 * b, min(2 * b + 2, KQ + KKV)):
                        gk = g("q_a", k) if k < KQ else g("kv_a", k - KQ)
                        ins = V.scalar_tensor_tensor(M["cT_lo"][:, k, :], bank[4 + b][:, (k % 2) * S:(k % 2 + 1) * S],
                                                     gk, M["cT_hi"][:, k, :].bitcast(F32), ALU.mult, ALU.subtract)
                    ins.then_inc(sem("mla_c_low"), 1)
                inverse("mla_c_root", "mla_c_rinv", 1, M["c_rinv"][:, :], M["c_root"][:, :])
                for c in range(2):
                    for s in range(2):
                        if s == 0:
                            w1.ahead(start_of["mla_ukv"] + c)
                            dve.wait_ge(sem("mla_kv_first"), c + 1)
                        else:
                            used(w1, start_of["mla_ukv"] + c)
                        pair = (3 + 2 * c + s) % 2
                        for t in range(T):
                            ins = V.tensor_scalar(kv[:, t, c * D + s * HALF:c * D + (s + 1) * HALF],
                                                  bank[2 * pair + t][:, :], M["c_rinv"][:, 2 + t:3 + t], None, ALU.mult)
                        ins.then_inc(sem("mla_kv_done"), 1)
                w1.ahead(start_of["mla_ukv"] + 1)
                for t in range(T):
                    dve.wait_ge(sem("mla_qk_squares"), 2 * t + 1)
                    V.tensor_reduce(M["qk_ss"][:, t, :HEADS], tmp[:, :HEADS * QK].rearrange("p (h d) -> p h d", h=HEADS),
                                    AX.X, ALU.add).then_inc(sem("mla_sums"), 1)
                    dve.wait_ge(sem("mla_qk_squares"), 2 * t + 2)
                    link(V.tensor_reduce(M["qk_ss"][:, t, HEADS:],
                                         tmp[:, :HEADS * NOPE].rearrange("p (h d) -> p h d", h=HEADS), AX.X, ALU.add))
                    dve.wait_ge(sem("mla_rope_squares"), 1)
                    V.tensor_scalar(M["qk_ss"][:, t, HEADS:], M["qk_ss"][:, t, HEADS:], M["rope_ss"][:, t:t + 1], None,
                                    ALU.add).then_inc(sem("mla_sums"), 1)
                inverse("mla_qk_root", "mla_qk_rinv", 1, M["qk_rinv"][:, :, :], M["qk_root"][:, :, :])
                ri = M["qk_rinv"]
                for t in range(T):
                    qh = q[:, t, :].rearrange("p (h d) -> p h d", h=HEADS)
                    kh = kv[:, t, :].rearrange("p (h d) -> p h d", h=HEADS)
                    V.tensor_tensor(rp[:, t, :HEADS, :], qh[:, :, NOPE:], per_feature(ri[:, t, :HEADS], ROPE), ALU.mult)
                    link(V.tensor_tensor(rp[:, t, HEADS:, :],
                                         dn[:, t, Q_RANK + KV_RANK:].unsqueeze(1).broadcast_to([P, HEADS, ROPE]),
                                         per_feature(ri[:, t, HEADS:], ROPE), ALU.mult))
                    r4 = rp[:, t, :, :].rearrange("p (s h) d -> p s h d", s=2)
                    link(V.tensor_tensor(r4, r4, rope_g[:, :, :].unsqueeze(2).broadcast_to([P, 2, HEADS, ROPE]), ALU.mult))
                    dve.wait_ge(sem("rope_tables"), 2)
                    turned_ = tmp[:, :2 * HEADS * ROPE].rearrange("p (h d) -> p h d", h=2 * HEADS)
                    n2 = ROPE // 2

                    def over_heads(v):
                        return v.unsqueeze(1).broadcast_to([P, 2 * HEADS, n2])
                    V.tensor_tensor(turned_[:, :, :n2], rp[:, t, :, n2:], over_heads(nsin[:, t, :]), ALU.mult)
                    link(V.tensor_tensor(turned_[:, :, n2:], rp[:, t, :, :n2], over_heads(sin[:, t, :]), ALU.mult))
                    cosb = cos2[:, t, :, :].rearrange("p a b -> p (a b)").unsqueeze(1).broadcast_to([P, 2 * HEADS, ROPE])
                    link(V.tensor_tensor(rp[:, t, :, :], rp[:, t, :, :], cosb, ALU.mult))
                    V.tensor_tensor(rp[:, t, :, :], rp[:, t, :, :], turned_, ALU.add)
                    V.tensor_tensor(qh[:, :, :NOPE], qh[:, :, :NOPE], per_feature(ri[:, t, :HEADS], NOPE), ALU.mult)
                    link(V.tensor_tensor(kh[:, :, :NOPE], kh[:, :, :NOPE], per_feature(ri[:, t, HEADS:], NOPE), ALU.mult))
                V.memset(M["mla_st"][:, :, :, :], 0.0).then_inc(sem("mla_heads_ready"), 1)

                def turn(h):
                    dve.wait_ge(sem("mla_rope_turned"), h + 1)
                    if h >= 2:
                        dve.wait_ge(sem("scores_in_psum"), before("mla", "scores_in_psum") + h - 1)
                    V.tensor_copy(M["ropeT"][:, h % 2, :], bank[5][:ROPE, :]).then_inc(sem("mla_ropeT"), 1)

                def add_mask(h, s_):
                    link(V.tensor_tensor(s_, bank[6][:, :3 * P], mask, ALU.add))

                attention("mla", HEADS, [(0, P), (P, 3 * P)], QK ** -0.5, turn, add_mask,
                          lambda h, o: (o[:, h, :], bank[h % 2][:, :S]))
                residual("mla", w1, start_of["mla_o"] + 3)

            if "moe" in parts:
                rt, rc, slot_of, gate_of = M["rt"], M["rc"], M["slot_of"], M["gate_of"]
                inverse("root", "rinv", before("moe", "rinv") + 1, rinv[:, :], root[:, :])
                dve.wait_ge(sem("loaded_moe_g"), 16)
                for t in range(T):
                    ins = V.scalar_tensor_tensor(M["h"][:, t, :], x[:, t, :], rinv[:, t:t + 1], M["moe_g"][:, :],
                                                 ALU.mult, ALU.mult)
                    ins.then_inc(sem("moe_h"), 1)
                w1.ahead(MOE0 - 1)
                dve.wait_ge(sem("moe_logits"), 1)
                L = [rt[:, j, :, :] for j in range(20)]
                R = [rc[:, j, :] for j in range(8)]

                def wide_(c):
                    return per_feature(c, E)

                link(V.tensor_copy(L[0], bank[0][:, :T * E].rearrange("p (t e) -> p t e", t=T)))
                link(V.tensor_reduce(R[2], L[0], AX.X, ALU.max))
                V.tensor_scalar(R[0], R[2], -1.0, None, ALU.mult).then_inc(sem("moe_logits_ready"), 1)
                dve.wait_ge(sem("moe_exp"), 1)
                link(V.reciprocal(R[3], R[1]))
                link(V.tensor_tensor(L[2], L[1], wide_(R[3]), ALU.mult))
                ties = const[:, C_TIE:C_TIE + E].unsqueeze(1).broadcast_to([P, T, E])
                p_at = L[2]
                for n, (best, hot) in enumerate(((R[4], L[5]), (R[5], L[9]))):
                    link(V.tensor_reduce(best, p_at, AX.X, ALU.max))
                    link(V.tensor_tensor(L[3], p_at, wide_(best), ALU.is_equal))
                    link(V.tensor_tensor(L[4], L[3], ties, ALU.mult))
                    link(V.tensor_reduce(R[6], L[4], AX.X, ALU.max))
                    link(V.tensor_tensor(hot, L[4], wide_(R[6]), ALU.is_equal))
                    if n == 0:
                        link(V.scalar_tensor_tensor(L[6], L[5], -2.0, L[2], ALU.mult, ALU.add))
                        p_at = L[6]
                link(V.tensor_tensor(L[7], L[5], L[9], ALU.add))
                V.tensor_copy(L[8], L[7]).then_inc(sem("moe_chosen"), 1)
                link(V.tensor_tensor(R[7], R[4], R[5], ALU.add))
                link(V.reciprocal(R[6], R[7]))
                link(V.tensor_tensor(L[10], L[7], L[2], ALU.mult))
                V.memset(gate_of[:, :, 2 * E:], 0.0).then_inc(sem("moe_act_done"), 1)
                for n in range(2):
                    link(V.tensor_tensor(gate_of[:, :, n * E:(n + 1) * E], L[10], wide_(R[6]), ALU.mult))
                dve.wait_ge(sem("moe_placed"), 1)
                place = bank[1][:, :3 * E]
                link(V.tensor_scalar(L[11], place[:, :T * E].rearrange("p (t e) -> p t e", t=T), 1.0, None, ALU.add))
                link(V.tensor_tensor(L[12], L[11], L[7], ALU.mult))
                V.memset(slot_of[:, :, 2 * E:], -1.0)
                V.tensor_scalar(slot_of[:, :, :E], L[12], -1.0, None, ALU.add)
                link(V.tensor_scalar(slot_of[:, :, E:2 * E], L[12], -1.0 - P, None, ALU.add))
                link(V.tensor_reduce(M["most"][:, 0:1], place[:, T * E:], AX.X, ALU.max))
                V.tensor_scalar(overflow[:, :], M["most"][0:1, 0:1], float(P) + 0.5, None, ALU.is_gt)\
                    .then_inc(sem("overflow_known"), 1)

                def pick(e):
                    for t in range(T):
                        ins = V.tensor_scalar(M["pick"][:, t, :], iota, slot_of[:, t, bass.ds(e, 1)], None,
                                              ALU.is_equal)
                    ins.then_inc(sem("moe_pick"), 1)

                def job_left(job, e):
                    dve.wait_ge(sem("moe_job"), PROLOGUE_JOBS + job + 1 + JOBS * e)
                    return bank[6 + job % 2]

                def job_low(job, n_high, e, lo, hi):
                    src = bank[6 + job % 2]
                    dve.wait_ge(sem("moe_job_high"), 2 + n_high + 1 + 6 * e)
                    V.tensor_tensor(lo.rearrange("p k s -> p (k s)"), src[:, :],
                                    hi.bitcast(F32).rearrange("p k s -> p (k s)"), ALU.subtract)\
                        .then_inc(sem("moe_drained"), 1)

                def gather_low(job, n_high, e, half):
                    part = slice(4 * half, 4 * half + 4)
                    job_low(job, n_high, e, M["gT_lo"][:, part, :], M["gT_hi"][:, part, :])

                def turn_low(group, n_high, e):
                    part = slice(4 * group, 4 * group + 4)
                    job_low(JOB_TURN[group], n_high, e, M["eT_lo"][:, part, :], M["eT_hi"][:, part, :])

                def scatter_add(job, e, t, half, done):
                    xs = x[:, t, half * HALF:(half + 1) * HALF]
                    V.tensor_tensor(xs, xs, job_left(job, e)[:, :], ALU.add).then_inc(sem(done), 1)

                def gate_copy(job, e):
                    V.tensor_copy(M["gslot"][:, :], job_left(job, e)[:, 0:1]).then_inc(sem("moe_drained"), 1)

                def put_copy(job, e):
                    V.tensor_copy(M["put"][:, :], job_left(job, e)[:, :S]).then_inc(sem("moe_drained"), 1)

                def expert_act(e, group):
                    dve.wait_ge(W1.used, MOE0 + 4 * group + 4 + EXPERT_CHUNKS * e)
                    dve.wait_ge(sem("moe_silu_done"), 1 + group + EG * e)
                    if group:
                        dve.wait_ge(sem("moe_job"), PROLOGUE_JOBS + JOB_TURN[group - 1] + 1 + JOBS * e)
                    else:
                        dve.wait_ge(sem("moe_job"), PROLOGUE_JOBS + JOBS * e)
                    V.scalar_tensor_tensor(M["e_act"][:, :], bank[2 * (group % 2) + 1][:, :], M["gslot"][:, :],
                                           M["e_silu"][:, :], ALU.mult, ALU.mult).then_inc(sem("moe_act_done"), 1)

                def expert(e, more):
                    for c in range(EXPERT_CHUNKS):
                        if c + AHEAD < EXPERT_CHUNKS or more:
                            split_low(MOE0 + c + AHEAD, e, W1)
                        if c == 3:
                            expert_act(e, 0)
                            scatter_add(0, e, 0, 0, "moe_drained")
                            scatter_add(1, e, 0, 1, "moe_drained")
                        if c == 5:
                            turn_low(0, 0, e)
                        if c == 7:
                            expert_act(e, 1)
                            scatter_add(3, e, 1, 0, "moe_drained")
                            scatter_add(4, e, 1, 1, "moe_drained")
                        if c == 9:
                            turn_low(1, 1, e)
                        if c == 11:
                            expert_act(e, 2)
                            put_copy(JOB_PUT, e)
                            pick(e + 1)
                        if c == 13:
                            turn_low(2, 2, e)
                        if c == 15:
                            expert_act(e, 3)
                            gather_low(8, 3, e, 0)
                            gather_low(9, 4, e, 1)
                            gate_copy(JOB_GATE, e)
                        if c == 16:
                            turn_low(3, 5, e)

                w1.ahead(MOE0)
                pick(0)
                gather_low(-4, -2, 0, 0)
                gather_low(-3, -1, 0, 1)
                gate_copy(-2, 0)
                put_copy(-1, 0)
                with dve.Fori(0, E - 1) as e:
                    expert(e, True)
                expert(E - 1, False)
                dve.wait_ge(sem("overflow_known"), 1)
                over = dve.value_load(overflow[0:1, 0:1], min_val=0, max_val=1)
                with dve.If(over > 0):
                    for c in range(AHEAD):
                        split_low(MOE0 + c, E, W1)
                    with dve.Fori(E, 2 * E - 1) as e:
                        expert(e, True)
                    expert(2 * E - 1, False)
                for n, (t, half) in enumerate(((0, 0), (0, 1), (1, 0), (1, 1))):
                    dve.wait_ge(sem("moe_last_scatter"), n + 1)
                    xs = x[:, t, half * HALF:(half + 1) * HALF]
                    V.tensor_tensor(xs, xs, bank[4 + n][:, :], ALU.add).then_inc(sem("x_updated"), 1)
                dve.wait_ge(sem("x_updated"), before("moe", "x_updated") + 4)

            if "fox" in parts:
                z, cs = M["z"], M["cs"]
                w2.ahead(0)
                norm("fox")
                for j in (2, 3):
                    used(w2, 2 * j + 1)
                    for t in range(T):
                        ins = V.tensor_scalar(z[:, t, j * HALF:(j + 1) * HALF], bank[2 * (j % 2) + t][:, :],
                                              rinv[:, t:t + 1], None, ALU.mult)
                    ins.then_inc(sem("fox_vp_done"), 1)
                for t in range(T):
                    dve.wait_ge(sem("fox_head_squares"), t + 1)
                    V.tensor_reduce(M["f_ss"][:, t, :],
                                    M["fox_tmp"][:, :2 * FOX].rearrange("p (h d) -> p h d", h=2 * FOX_HEADS),
                                    AX.X, ALU.add).then_inc(sem("fox_sums"), 1)
                dve.wait_ge(sem("loaded_forget"), 32)
                dve.wait_ge(sem("forget_logits"), 1)
                for t in range(T):
                    ins = V.scalar_tensor_tensor(cs[:, 0, t, :], bank[7][:, t * FOX_HEADS:(t + 1) * FOX_HEADS],
                                                 rinv[:, t:t + 1], forget_b[:, :], ALU.mult, ALU.add)
                link(ins)
                link(V.tensor_scalar(cs[:, 4, :, :], cs[:, 0, :, :], -1.0, None, ALU.mult))
                V.tensor_tensor(cs[:, 1, :, :], cs[:, 0, :, :], cs[:, 4, :, :], ALU.min).then_inc(sem("forget_abs"), 1)
                inverse("fox_qk_root", "fox_qk_rinv", 1, M["f_rinv"][:, :, :], M["f_root"][:, :, :])
                for t in range(T):
                    zh = z[:, t, :2 * FOX].rearrange("p (h d) -> p h d", h=2 * FOX_HEADS)
                    ins = V.tensor_tensor(zh, zh, per_feature(M["f_rinv"][:, t, :], FOX_DIM), ALU.mult)
                    ins.then_inc(sem("fox_heads_ready"), 1)
                dve.wait_ge(sem("forget_ln"), 1)
                V.scalar_tensor_tensor(cs[:, 5, :, :], cs[:, 0, :, :], 0.0, cs[:, 3, :, :], ALU.min, ALU.subtract)\
                    .then_inc(sem("forget_log"), 1)
                dve.wait_ge(sem("forget_sum"), 1)
                summed = bank[7][:, :T * FOX_HEADS].rearrange("p (t h) -> p t h", t=T)
                V.tensor_copy(cs[:, 0, :, :], summed)
                V.tensor_scalar(cs[:, 4, :, :], summed, FOX_DIM ** 0.5, None, ALU.mult).then_inc(sem("forget_sum_copied"), 1)
                dve.wait_ge(sem("forget_sum_turned"), 1)
                V.tensor_copy(M["cT"][:, :], bank[7][:FOX_HEADS, :S]).then_inc(sem("forget_cT"), 1)
                w2.ahead(start_of["fox_out"] - 1)
                for k in range(len(WINDOWS)):
                    dve.wait_ge(sem("pool_high"), k + 1)
                    V.scalar_tensor_tensor(xT_lo[:, KD // 2 + k, :], bank[2 + k % 2][:, :S], g("pool_scale", k),
                                           xT_hi[:, KD // 2 + k, :].bitcast(F32), ALU.mult, ALU.subtract)\
                        .then_inc(sem("pool_low"), 1)

                def add_forget(h, s_):
                    for t, (a, b) in enumerate(((0, P), (P, 3 * P))):
                        ins = V.scalar_tensor_tensor(s_[:, a:b], bank[6][:, a:b], cs[:, 4, t, h:h + 1], mask[:, a:b],
                                                     ALU.add, ALU.add)
                    link(ins)

                def fox_value(h, o):
                    rows_ = slice(FOX_DIM * (h % 2), FOX_DIM * (h % 2 + 1))
                    return o[rows_, h // 2, :], bank[h // 2 % 2][rows_, :S]

                attention("fox", FOX_HEADS, [(0, P), (P, 3 * P)], FOX_DIM ** -0.5, lambda h: None, add_forget,
                          fox_value)
                residual("fox", w2, start_of["fox_out"] + 3)

            if "mem" in parts:
                mkv, mq = M["mkv"], M["mq"]
                norm_low("memkv", "g_mem_kv", M["memT_lo"], M["memT_hi"])
                inverse("root", "rinv", before("memkv", "rinv") + 1, M["m_rinv"][:, :], M["m_root"][:, :])
                norm("mem")
                used(w2, start_of["mem_kv"] + 3)
                for t in range(T):
                    ins = V.tensor_scalar(mkv[:, t, MEM:], bank[2 + t][:, :], M["m_rinv"][:, t:t + 1], None, ALU.mult)
                ins.then_inc(sem("mem_v_done"), 1)
                w2.ahead(start_of["mem_q"] + 1)
                for j in range(2):
                    dve.wait_ge(sem("mem_head_squares"), j + 1)
                    V.tensor_reduce(M["mh_ss"][:, j, :, :].rearrange("p t h -> p (t h)"),
                                    M["mem_tmp"][:, :T * MEM].rearrange("p (h d) -> p h d", d=MEM_DIM),
                                    AX.X, ALU.add).then_inc(sem("mem_sums"), 1)
                inverse("mem_qk_root", "mem_qk_rinv", 1, M["mh_rinv"][:, :, :, :], M["mh_root"][:, :, :, :])
                for j, src in enumerate((mkv[:, :, :MEM], mq[:, :, :])):
                    for t in range(T):
                        v = src[:, t, :].rearrange("p (h d) -> p h d", h=MEM_HEADS)
                        ins = V.tensor_tensor(v, v, per_feature(M["mh_rinv"][:, j, t, :], MEM_DIM), ALU.mult)
                ins.then_inc(sem("mem_heads_ready"), 1)

                def copy_scores(h, s_):
                    link(V.tensor_copy(s_, bank[6][:, :]))

                attention("mem", MEM_HEADS, [(0, S), (S, 2 * S)], MEM_DIM ** -0.5, lambda h: None, copy_scores,
                          lambda h, o: (o[:, h, :], bank[h % 2][:, :S]))
                residual("mem", w2, start_of["mem_out"] + 1)

            if "ffn2" in parts:
                ffn("ffn2", w2)

        @block.tensor
        def _(pe):
            mm, turn_ = nc.tensor.matmul, nc.tensor.transpose

            def weights(w, i, e, hold=False):
                pe.wait_ge(w.low, i + 1 + EXPERT_CHUNKS * e)
                slot = i % RING
                return w_hi[:, slot, :], w_lo[:, slot, :]

            def three(dst, a_hi, a_lo, b_hi, b_lo, start, stop):
                mm(dst, a_hi, b_hi, start=start, stop=False)
                mm(dst, a_hi, b_lo, start=False, stop=False)
                return mm(dst, a_lo, b_hi, start=False, stop=stop)

            def tall(w, i, e, xh, xl, k0, kn, n, banks, start, stop, tokens=T):
                wh, wl = weights(w, i, e)
                for k in range(kn):
                    for t in range(tokens):
                        tok = slice(t * P, (t + 1) * P)
                        ins = three(bank[banks[t]][:, :n], xh[:, k0 + k, tok], xl[:, k0 + k, tok],
                                    wh[:, k * n:(k + 1) * n], wl[:, k * n:(k + 1) * n],
                                    start and k == 0, stop and k == kn - 1)
                ins.then_inc(w.used, 1)

            def wide(w, i, e, xh, xl, k0, banks, start, stop, tokens=T):
                wh, wl = weights(w, i, e)
                for k in range(2):
                    for t in range(tokens):
                        tok = slice(t * P, (t + 1) * P)
                        for half in range(2):
                            cols = slice(k * D + half * HALF, k * D + (half + 1) * HALF)
                            ins = three(bank[banks[2 * t + half]][:, :], xh[:, k0 + k, tok], xl[:, k0 + k, tok],
                                        wh[:, cols], wl[:, cols], start and k == 0, stop and k == 1)
                ins.then_inc(w.used, 1)

            def group(w, i, xh, xl, n, banks, turned_for=None):
                step = CHUNK // n if CHUNK // n < KD else KD
                for j in range(KD // step):
                    if turned_for:
                        pe.wait_ge(sem("xT_low"), before(turned_for, "xT_low") + min((j + 1) * step, KD) // 2)
                    tall(w, i + j, 0, xh, xl, j * step, step, n, banks, j == 0, (j + 1) * step == KD)

            def wide_all(w, name, xh, xl, kn, ready):
                for c in range(kn // 2):
                    ready(c)
                    wide(w, start_of[name] + c, 0, xh, xl, 2 * c, (0, 1, 2, 3), c == 0, c == kn // 2 - 1)

            def norm(p, src, ready):
                pe.wait_ge(sem(ready[0]), ready[1])
                for b in range(4):
                    for k in (2 * b, 2 * b + 1):
                        for t in range(T):
                            at_ = ((k % 2) * T + t) * P
                            ins = turn_(bank[4 + b][:, at_:at_ + P], src[:, t, k * P:(k + 1) * P], ident)
                    ins.then_inc(sem("xT_turned"), 1)

            def ffn(p, w):
                norm(p, x, x_ready[p])
                i, turned = start_of[p + "_up"], 0

                def turn_group(gr):
                    nonlocal turned
                    pe.wait_ge(sem("act_done"), before(p, "act_done") + gr + 1)
                    n = FF_GROUPS[gr][1]
                    for j in range(n // S):
                        if gr >= 2:
                            pe.wait_ge(sem("act_low"), before(p, "act_low") + 2 * (gr - 2) + j + 1)
                        for k in range(2):
                            for t in range(T):
                                c0 = (2 * j + k) * P
                                ins = turn_(bank[4 + 2 * (gr % 2) + j][:, (k * T + t) * P:(k * T + t + 1) * P],
                                            M[p + "_act"][:, t, c0:c0 + P], ident)
                        ins.then_inc(sem("act_turned"), 1)
                        turned += 1

                for gr, (_, n) in enumerate(FF_GROUPS):
                    parts_of = KD // (CHUNK // n) if CHUNK // n < KD else 1
                    if gr:
                        pe.wait_ge(sem("silu_done"), before(p, "silu_done") + gr)
                    group(w, i, xT_hi, xT_lo, n, (0, 1), p)
                    if gr:
                        turn_group(gr - 1)
                        pe.wait_ge(sem("act_done"), before(p, "act_done") + gr)
                    group(w, i + parts_of, xT_hi, xT_lo, n, (2, 3))
                    i += 2 * parts_of
                turn_group(len(FF_GROUPS) - 1)
                wide_all(w, p + "_down", M[p + "_hi"], M[p + "_lo"], KF,
                         lambda c: pe.wait_ge(sem("act_low"), before(p, "act_low") + c + 1))

            def attention(p, n_heads, blocks, turn, score, value):
                def probabilities(h):
                    pe.wait_ge(sem("probs_ready"), before(p, "probs_ready") + h + 1)
                    if h:
                        pe.wait_ge(sem("pT"), before(p, "pT") + h)
                    for at_, (a, b) in enumerate(blocks):
                        ins = turn_(bank[7][:, at_ * P:(at_ + 1) * P], M[p + "_p"][:, h % 2, a:b], ident)
                    ins.then_inc(sem("pT_turned"), 1)

                turn(0)
                score(0)
                for h in range(n_heads):
                    if h + 1 < n_heads:
                        turn(h + 1)
                        pe.wait_ge(sem("scores_ready"), before(p, "scores_ready") + h + 1)
                        score(h + 1)
                    probabilities(h)
                    pe.wait_ge(sem("pT"), before(p, "pT") + h + 1)
                    value(h)

            pe.wait_ge(sem("loaded_const"), 16)
            pe.wait_ge(sem("loaded_gains"), 16 * N_GAIN_LOADS)
            turn_(bank[0][:, :N_GAINS], M["gain_rows"][:N_GAINS, :], ident[:N_GAINS, :N_GAINS])\
                .then_inc(sem("gains_turned"), 1)

            def turn_half(buf, first_bank, name):
                for j in range(2):
                    for k in range(2):
                        for t in range(T):
                            c0 = (2 * j + k) * P
                            ins = turn_(bank[first_bank + j][:, (k * T + t) * P:(k * T + t + 1) * P],
                                        buf[:, t, c0:c0 + P], ident)
                    ins.then_inc(sem(name), 1)

            norm("conv", x, x_ready["conv"])
            pe.wait_ge(sem("gains_ready"), 1)
            bank_free = [None, None, ("conv_c_done", 1), ("conv_v_done", 1), ("conv_b_done", 1), ("conv_c_done", 2)]
            for q_ in range(6):
                if bank_free[q_]:
                    pe.wait_ge(sem(bank_free[q_][0]), bank_free[q_][1])
                pair = (2 * (q_ % 2), 2 * (q_ % 2) + 1)
                group(W1, 2 * q_, xT_hi, xT_lo, HALF, pair, "conv" if q_ == 0 else None)
                if q_ == 2:
                    pe.wait_ge(sem("conv_v_done"), 1)
                    turn_half(M["conv_v"], 4, "conv_v_turned")
                if q_ == 3:
                    pe.wait_ge(sem("conv_b_done"), 1)
                    turn_half(M["conv_b"], 6, "conv_b_turned")
            pe.wait_ge(sem("conv_v_done"), 2)
            pe.wait_ge(sem("conv_vT"), 2)
            turn_half(M["conv_v"], 4, "conv_v_turned")
            pe.wait_ge(sem("conv_b_done"), 2)
            pe.wait_ge(sem("conv_y_done"), 4)
            turn_half(M["conv_b"], 6, "conv_b_turned")
            wide_all(W1, "conv_out", M["yT_hi"], M["yT_lo"], KD,
                     lambda c: pe.wait_ge(sem("conv_y_low"), c // 2 + 1))

            if "ffn1" in parts:
                ffn("ffn1", W1)

            if "mla" in parts:
                dn, q, kv = M["dn"], M["q"], M["kv"]
                norm("mla", x, x_ready["mla"])
                n = DOWN_COLS // 2
                for j in range(2):
                    for c in range(2):
                        pe.wait_ge(sem("xT_low"), before("mla", "xT_low") + 2 * c + 2)
                        tall(W1, start_of["mla_down"] + 2 * j + c, 0, xT_hi, xT_lo, 4 * c, 4, n, (2 * j, 2 * j + 1),
                             c == 0, c == 1)
                pe.wait_ge(sem("mla_dn"), 2)
                for b in range(3):
                    for k in range(2 * b, min(2 * b + 2, KQ + KKV)):
                        for t in range(T):
                            ins = turn_(bank[4 + b][:, ((k % 2) * T + t) * P:((k % 2) * T + t + 1) * P],
                                        dn[:, t, k * P:(k + 1) * P], ident)
                    ins.then_inc(sem("mla_c_turned"), 1)
                cth, ctl = M["cT_hi"], M["cT_lo"]
                pe.wait_ge(sem("mla_c_low"), 2)
                for j in range(3):
                    if j == 2:
                        pe.wait_ge(sem("mla_q_done"), 1)
                    tall(W1, start_of["mla_uq"] + j, 0, cth, ctl, 0, KQ, HALF, (2 * (j % 2), 2 * (j % 2) + 1), True, True)
                pe.wait_ge(sem("mla_c_low"), 3)
                free = [("mla_q_done", 2), ("mla_q_done", 3), ("mla_kv_done", 1), ("mla_kv_done", 2)]
                for c in range(2):
                    wh, wl = weights(W1, start_of["mla_ukv"] + c, 0)
                    for s in range(2):
                        pair = (3 + 2 * c + s) % 2
                        pe.wait_ge(sem(free[2 * c + s][0]), free[2 * c + s][1])
                        for k in range(KKV):
                            cols = slice(k * D + s * HALF, k * D + (s + 1) * HALF)
                            for t in range(T):
                                tok = slice(t * P, (t + 1) * P)
                                ins = three(bank[2 * pair + t][:, :], cth[:, KQ + k, tok], ctl[:, KQ + k, tok],
                                            wh[:, cols], wl[:, cols], k == 0, k == KKV - 1)
                        ins.then_inc(W1.used if s else sem("mla_kv_first"), 1)
                pe.wait_ge(sem("mla_heads_ready"), 1)

                def turn(h):
                    if h:
                        pe.wait_ge(sem("mla_qkT"), h)
                    for j, (src, c0) in enumerate(((q, h * QK), (kv, h * 2 * P))):
                        for t in range(T):
                            ins = turn_(bank[4][:, (j * T + t) * P:(j * T + t + 1) * P], src[:, t, c0:c0 + P], ident)
                    ins.then_inc(sem("mla_nope_turned"), 1)
                    if h:
                        pe.wait_ge(sem("mla_ropeT"), h)
                    for j in range(2):
                        for t in range(T):
                            ins = turn_(bank[5][:ROPE, (j * T + t) * P:(j * T + t + 1) * P],
                                        M["rope"][:, t, j * HEADS + h, :], ident)
                    ins.then_inc(sem("mla_rope_turned"), 1)

                def score(h):
                    pe.wait_ge(sem("mla_qkT"), h + 1)
                    pe.wait_ge(sem("mla_ropeT"), h + 1)
                    qk, ro = M["qkT"][:, h % 2, :], M["ropeT"][:, h % 2, :]
                    for t, (a, keys) in enumerate(((0, P), (P, S))):
                        tok = slice(t * P, (t + 1) * P)
                        mm(bank[6][:, a:a + keys], qk[:, tok], qk[:, S:S + keys], start=True, stop=False)
                        ins = mm(bank[6][:, a:a + keys], ro[:, tok], ro[:, S:S + keys], start=False, stop=True)
                    ins.then_inc(sem("scores_in_psum"), 1)

                def value(h):
                    if h >= 2:
                        pe.wait_ge(sem("value_low"), before("mla", "value_low") + h - 1)
                    v = kv[:, :, h * 2 * P + P:(h + 1) * 2 * P]
                    pT = M["mla_pT"][:, h % 2, :]
                    mm(bank[h % 2][:, :S], v[:, 0, :], pT[:, :S], start=True, stop=False)
                    mm(bank[h % 2][:, P:S], v[:, 1, :], pT[:, S:], start=False, stop=True).then_inc(sem("values_in_psum"), 1)

                CAUSAL = [(0, P), (P, 2 * P), (2 * P, 3 * P)]
                attention("mla", HEADS, CAUSAL, turn, score, value)
                wide_all(W1, "mla_o", xT_hi, xT_lo, KD, lambda c: pe.wait_ge(sem("value_low"), before("mla", "value_low") + HEADS))

            if "moe" in parts:
                pe.wait_ge(sem("loaded_router"), 16)
                for b in range(4):
                    for k in (2 * b, 2 * b + 1):
                        for t in range(T):
                            pe.wait_ge(sem("moe_h"), t + 1)
                            at_ = ((k % 2) * T + t) * P
                            ins = turn_(bank[4 + b][:, at_:at_ + P], M["h"][:, t, k * P:(k + 1) * P], ident)
                    ins.then_inc(sem("xT_turned"), 1)
                pe.wait_ge(sem("moe_hT"), 4)
                for t in range(T):
                    for k in range(KD):
                        ins = mm(bank[0][:, t * E:(t + 1) * E], M["hT"][:, k, t * P:(t + 1) * P], router[:, k, :],
                                 start=(k == 0), stop=(k == KD - 1))
                ins.then_inc(sem("moe_logits"), 1)
                pe.wait_ge(sem("moe_chosen"), 1)
                chosen = M["rt"][:, 8, :, :]
                mm(bank[1][:, 0:E], earlier, chosen[:, 0, :], start=True, stop=True)
                mm(bank[1][:, E:2 * E], ones, chosen[:, 0, :], start=True, stop=False)
                mm(bank[1][:, E:2 * E], earlier, chosen[:, 1, :], start=False, stop=True)
                mm(bank[1][:, 2 * E:3 * E], ones, chosen[:, 0, :], start=True, stop=False)
                mm(bank[1][:, 2 * E:3 * E], ones, chosen[:, 1, :], start=False, stop=True).then_inc(sem("moe_placed"), 1)
                pick_, put = M["pick"], M["put"]

                def job_bank(job, e):
                    if job >= 0:
                        pe.wait_ge(sem("moe_drained"), PROLOGUE_JOBS + job - 1 + JOBS * e)
                    elif job >= -2:
                        pe.wait_ge(sem("moe_drained"), PROLOGUE_JOBS + job - 1)
                    return bank[6 + job % 2]

                def gather(job, e, half):
                    b = job_bank(job, e)
                    for k in range(4):
                        feat = slice((4 * half + k) * P, (4 * half + k + 1) * P)
                        for t in range(T):
                            ins = mm(b[:, k * P:(k + 1) * P], M["h"][:, t, feat], pick_[:, t, :],
                                     start=(t == 0), stop=(t == T - 1))
                    ins.then_inc(sem("moe_job"), 1)

                def gates(job, e, e_next):
                    b = job_bank(job, e)
                    for t in range(T):
                        ins = mm(b[:, 0:1], pick_[:, t, :], M["gate_of"][:, t, bass.ds(e_next, 1)],
                                 start=(t == 0), stop=(t == T - 1))
                    ins.then_inc(sem("moe_job"), 1)

                def turn_pick(job, e):
                    b = job_bank(job, e)
                    for t in range(T):
                        ins = turn_(b[:, t * P:(t + 1) * P], pick_[:, t, :], ident)
                    ins.then_inc(sem("moe_job"), 1)

                def turn_act(job, e, gr):
                    pe.wait_ge(sem("moe_act_done"), gr + 2 + EG * e)
                    b = job_bank(job, e)
                    for k in range(4):
                        ins = turn_(b[:, k * P:(k + 1) * P], M["e_act"][:, k * P:(k + 1) * P], ident)
                    ins.then_inc(sem("moe_job"), 1)

                def scatter_into(b, t, half):
                    return mm(b[:, :], put[:, t * P:(t + 1) * P], M["y"][:, half * HALF:(half + 1) * HALF],
                              start=True, stop=True)

                def scatter(job, e, t, half):
                    scatter_into(job_bank(job, e), t, half).then_inc(sem("moe_job"), 1)

                gth, gtl, eth, etl = M["gT_hi"], M["gT_lo"], M["eT_hi"], M["eT_lo"]

                def expert(e):
                    for c in range(4 * EG):
                        gr, up, half = c // 4, c // 2 % 2, c % 2
                        if c == 0:
                            pe.wait_ge(sem("moe_drained"), PROLOGUE_JOBS - 2 + JOBS * e)
                        if half == 0:
                            pe.wait_ge(sem("moe_act_done"), max(gr, 1) + EG * e)
                        tall(W1, MOE0 + c, e, gth, gtl, 4 * half, 4, HALF, (2 * (gr % 2) + up,), half == 0, half == 1,
                             tokens=1)
                        if c == 3:
                            pe.wait_ge(sem("moe_y"), 1 + e)
                            scatter(0, e, 0, 0)
                            scatter(1, e, 0, 1)
                        if c == 5:
                            turn_act(2, e, 0)
                        if c == 7:
                            scatter(3, e, 1, 0)
                            scatter(4, e, 1, 1)
                        if c == 9:
                            turn_act(5, e, 1)
                        if c == 11:
                            turn_pick(JOB_PUT, e)
                        if c == 13:
                            turn_act(7, e, 2)
                    pe.wait_ge(sem("moe_pick"), 2 + e)
                    gather(8, e, 0)
                    gather(9, e, 1)
                    gates(JOB_GATE, e, e + 1)
                    for c in range(FE // 256):
                        if c == 1:
                            turn_act(11, e, 3)
                        if c == 0:
                            pe.wait_ge(sem("moe_drained"), PROLOGUE_JOBS + 8 + JOBS * e)
                        if c == 6:
                            pe.wait_ge(sem("moe_drained"), PROLOGUE_JOBS + 12 + JOBS * e)
                        wide(W1, MOE0 + 4 * EG + c, e, eth, etl, 2 * c, (4, 5), c == 0, c == FE // 256 - 1, tokens=1)

                pe.wait_ge(sem("moe_pick"), 1)
                gather(-4, 0, 0)
                gather(-3, 0, 1)
                gates(-2, 0, 0)
                turn_pick(-1, 0)
                with pe.Fori(0, E) as e:
                    expert(e)
                pe.wait_ge(sem("overflow_known"), 1)
                over = pe.value_load(overflow[0:1, 0:1], min_val=0, max_val=1)
                with pe.If(over > 0):
                    with pe.Fori(E, 2 * E) as e:
                        expert(e)
                pe.wait_ge(sem("moe_y"), 1 + E + over * E)
                pe.wait_ge(sem("moe_drained"), PROLOGUE_JOBS + E * JOBS + over * (E * JOBS))
                for n_, (t, half) in enumerate(((0, 0), (0, 1), (1, 0), (1, 1))):
                    scatter_into(bank[4 + n_], t, half).then_inc(sem("moe_last_scatter"), 1)

            if "fox" in parts:
                z, cs = M["z"], M["cs"]
                norm("fox", x, x_ready["fox"])
                free = [None, None, ("fox_qk_done", 1), ("fox_qk_done", 2)]
                for j in range(4):
                    if free[j]:
                        pe.wait_ge(sem(free[j][0]), free[j][1])
                    group(W2, 2 * j, xT_hi, xT_lo, HALF, (2 * (j % 2), 2 * (j % 2) + 1), "fox" if j == 0 else None)
                    if j == 0:
                        pe.wait_ge(sem("loaded_forget"), 32)
                        for t in range(T):
                            for k in range(KD):
                                for part, xt in enumerate((xT_hi, xT_lo)):
                                    ins = mm(bank[7][:, t * FOX_HEADS:(t + 1) * FOX_HEADS],
                                             xt[:, k, t * P:(t + 1) * P].bitcast(F32), forget_w[:, k, :],
                                             start=(k == 0 and part == 0), stop=(k == KD - 1 and part == 1))
                        ins.then_inc(sem("forget_logits"), 1)
                pe.wait_ge(sem("forget_log"), 1)
                b = bank[7]
                ls = cs[:, 5, :, :]
                mm(b[:, 0:FOX_HEADS], upto_now, ls[:, 0, :], start=True, stop=True)
                mm(b[:, FOX_HEADS:2 * FOX_HEADS], ones, ls[:, 0, :], start=True, stop=False)
                mm(b[:, FOX_HEADS:2 * FOX_HEADS], upto_now, ls[:, 1, :], start=False, stop=True)\
                    .then_inc(sem("forget_sum"), 1)
                pe.wait_ge(sem("forget_sum_copied"), 1)
                for t in range(T):
                    ins = turn_(b[:FOX_HEADS, t * P:(t + 1) * P], cs[:, 0, t, :], ident)
                ins.then_inc(sem("forget_sum_turned"), 1)
                pe.wait_ge(sem("fox_vp_done"), 2)
                pe.wait_ge(sem("loaded_pool"), 32)
                for k in range(len(WINDOWS)):
                    zp = z[:, :, 3 * FOX + k * P:3 * FOX + (k + 1) * P]
                    mm(bank[k % 2][:, :S], zp[:, 0, :], M["bands"][:, k, 0, :], start=True, stop=False)
                    mm(bank[k % 2][:, P:S], zp[:, 1, :], M["bands"][:, k, 1, P:], start=False, stop=True)\
                        .then_inc(sem("pool_mixed"), 1)
                    pe.wait_ge(sem("pool_mixed_copied"), k + 1)
                    if k >= 2:
                        pe.wait_ge(sem("pool_low"), k - 1)
                    mm(bank[2 + k % 2][:, :S], M["w_pool"][:, k, :], M["mixed"][:, :], start=True, stop=True)\
                        .then_inc(sem("pool_mapped"), 1)
                pe.wait_ge(sem("fox_heads_ready"), 2)
                for k in range(FOX_HEADS // 2):
                    if k >= 2:
                        pe.wait_ge(sem("fox_qkT"), k - 1)
                    for j in range(2):
                        for t in range(T):
                            c0 = j * FOX + k * P
                            ins = turn_(bank[4 + k % 2][:, (j * T + t) * P:(j * T + t + 1) * P], z[:, t, c0:c0 + P], ident)
                    ins.then_inc(sem("fox_pair_turned"), 1)
                pe.wait_ge(sem("forget_cT"), 1)

                def score(h):
                    pe.wait_ge(sem("fox_qkT"), h // 2 + 1)
                    rows_ = slice(FOX_DIM * (h % 2), FOX_DIM * (h % 2 + 1))
                    qT, kT = M["fqT"][rows_, h // 2, :], M["fkT"][rows_, h // 2, :]
                    sel = const[:FOX_HEADS, C_SEL + h * P:C_SEL + (h + 1) * P]
                    for t, (a, keys) in enumerate(((0, P), (P, S))):
                        mm(bank[6][:, a:a + keys], qT[:, t * P:(t + 1) * P], kT[:, :keys], start=True, stop=False)
                        ins = mm(bank[6][:, a:a + keys], sel, M["cT"][:, :keys], start=False, stop=True)
                    ins.then_inc(sem("scores_in_psum"), 1)

                def value(h):
                    if h >= 4:
                        pe.wait_ge(sem("value_low"), before("fox", "value_low") + h - 3)
                    v = z[:, :, 2 * FOX + h * FOX_DIM:2 * FOX + (h + 1) * FOX_DIM]
                    o = bank[h // 2 % 2][FOX_DIM * (h % 2):FOX_DIM * (h % 2 + 1), :]
                    pT = M["fox_pT"][:, h % 2, :]
                    mm(o[:, :S], v[:, 0, :], pT[:, :S], start=True, stop=False)
                    mm(o[:, P:S], v[:, 1, :], pT[:, S:], start=False, stop=True).then_inc(sem("values_in_psum"), 1)

                attention("fox", FOX_HEADS, CAUSAL, lambda h: None, score, value)
                wide_all(W2, "fox_out", xT_hi, xT_lo, KD,
                         lambda c: pe.wait_ge(sem("value_low"), before("fox", "value_low") + FOX_HEADS))

            if "mem" in parts:
                mkv, mq = M["mkv"], M["mq"]
                norm("memkv", M["mem"], ("loaded_mem", 16))
                pe.wait_ge(sem("xT_low"), before("memkv", "xT_low") + 4)
                norm("mem", x, x_ready["mem"])
                for j in range(2):
                    group(W2, start_of["mem_kv"] + 2 * j, M["memT_hi"], M["memT_lo"], HALF, (2 * j, 2 * j + 1))
                pe.wait_ge(sem("mem_k_done"), 1)
                group(W2, start_of["mem_q"], xT_hi, xT_lo, HALF, (0, 1), "mem")
                pe.wait_ge(sem("mem_heads_ready"), 1)
                for k in range(MEM_HEADS):
                    if k >= 2:
                        pe.wait_ge(sem("mem_qkT"), k - 1)
                    for j, src in enumerate((mq, mkv)):
                        for t in range(T):
                            ins = turn_(bank[4 + k % 2][:, (j * T + t) * P:(j * T + t + 1) * P],
                                        src[:, t, k * P:(k + 1) * P], ident)
                    ins.then_inc(sem("mem_head_turned"), 1)

                def score_m(h):
                    pe.wait_ge(sem("mem_qkT"), h + 1)
                    for t in range(T):
                        ins = mm(bank[6][:, t * S:(t + 1) * S], M["mqT"][:, h, t * P:(t + 1) * P], M["mkT"][:, h, :],
                                 start=True, stop=True)
                    ins.then_inc(sem("scores_in_psum"), 1)

                def value_m(h):
                    if h >= 2:
                        pe.wait_ge(sem("value_low"), before("mem", "value_low") + h - 1)
                    pT = M["mem_pT"][:, h % 2, :]
                    for m in range(T):
                        ins = mm(bank[h % 2][:, :S], mkv[:, m, MEM + h * P:MEM + (h + 1) * P], pT[:, m * S:(m + 1) * S],
                                 start=(m == 0), stop=(m == T - 1))
                    ins.then_inc(sem("values_in_psum"), 1)

                attention("mem", MEM_HEADS, [(0, P), (S, S + P), (P, S), (S + P, 2 * S)], lambda h: None, score_m, value_m)
                wide_all(W2, "mem_out", xT_hi, xT_lo, MEM // P, lambda c: pe.wait_ge(sem("value_low"), before("mem", "value_low") + MEM_HEADS))

            if "ffn2" in parts:
                ffn("ffn2", W2)


N_GAIN_LOADS = len(GAINS) + 2


def layout(inputs):
    const, bands = shape_constants()
    arrays = {n: np.ascontiguousarray(a) for n, a in inputs.items()}
    return arrays | {"shape_const": const, "shape_bands": bands}


def kernel(**inputs):
    import concourse.bacc as bacc
    from concourse.bass_utils import run_bass_kernel_spmd

    nc = bacc.Bacc("TRN2", target_bir_lowering=False, num_devices=1)
    arrays = {f"in_{n}": a for n, a in layout(inputs).items()}
    A = {n[3:]: nc.dram_tensor(n, a.shape, mybir.dt.from_np(a.dtype), kind="ExternalInput").ap()
         for n, a in arrays.items()}
    out = nc.dram_tensor("out_0", (1, S, D), F32, kind="ExternalOutput").ap()
    build(nc, A, out)
    return run_bass_kernel_spmd(nc, [arrays], core_ids=[0]).results[0]["out_0"]
```

```python
from contextlib import ExitStack

import concourse.bass as bass
import numpy as np
from concourse import mybir

P = 128
F32 = mybir.dt.float32
F32R = mybir.dt.float32r
I32 = mybir.dt.int32
ALU = mybir.AluOpType
ACT = mybir.ActivationFunctionType
AX = mybir.AxisListType

D = 1024
KD = D // P
T = 2
S = T * P
HALF = 512
EPS = 1e-6
FF = 2816
KF = FF // P
FF_GROUPS = [(i * HALF, min(HALF, FF - i * HALF)) for i in range(-(-FF // HALF))]
CHUNK = 2048
RING = 4
AHEAD = 3
HEADS, NOPE, ROPE = 8, 128, 64
QK = NOPE + ROPE
Q_RANK, KV_RANK = 384, 256
KQ, KKV = Q_RANK // P, KV_RANK // P
DOWN_COLS = Q_RANK + KV_RANK + ROPE
E = 8
FE = 2048
EG = FE // HALF
EXPERT_CHUNKS = 4 * EG + FE // 256
FOX_HEADS, FOX_DIM = 8, 64
FOX = FOX_HEADS * FOX_DIM
WINDOWS = (2, 4, 8, 16)
MEM_HEADS, MEM_DIM = 4, 128
MEM = MEM_HEADS * MEM_DIM
NEG = -1e30
JOB_SCATTER, JOB_TURN, JOB_PUT, JOB_GATHER, JOB_GATE = (0, 1, 3, 4), (2, 5, 7, 11), 6, (8, 9), 10
JOBS, PROLOGUE_JOBS = 12, 4

UQ_GROUPS = HEADS // 2

SPLIT_BESIDE = (0, 2, 4)

C_IDENT, C_MASK, C_BEFORE, C_UPTO, C_ONES, C_IOTA, C_FREQ, C_TIE, C_SEL = np.cumsum(
    [0, P, 3 * P, P, P, P, P, ROPE // 2, E]).tolist()
C_END = C_SEL + FOX_HEADS * P


def shape_constants():
    c = np.zeros((P, C_END), np.float32)
    row, col = np.arange(P)[:, None], np.arange(P)[None, :]
    c[:, C_IDENT:C_IDENT + P] = row == col
    for at in (0, 2 * P):
        c[:, C_MASK + at:C_MASK + at + P] = np.where(col <= row, 0.0, NEG)
    c[:, C_BEFORE:C_BEFORE + P] = row < col
    c[:, C_UPTO:C_UPTO + P] = row <= col
    c[:, C_ONES:C_ONES + P] = 1.0
    c[:, C_IOTA:C_IOTA + P] = col
    c[:, C_FREQ:C_FREQ + ROPE // 2] = np.float32(10000.0) ** (
        -np.arange(0, ROPE, 2, dtype=np.float32) / np.float32(ROPE))
    c[:, C_TIE:C_TIE + E] = E - np.arange(E)
    for h in range(FOX_HEADS):
        c[h, C_SEL + h * P:C_SEL + (h + 1) * P] = -(FOX_DIM ** 0.5)
    bands = np.zeros((P, len(WINDOWS), T, S), np.float32)
    now = np.arange(S)[None, :]
    for g, w in enumerate(WINDOWS):
        for t in range(T):
            then = t * P + np.arange(P)[:, None]
            inside = (then <= now) & (then > now - w)
            bands[:, g, t] = inside / np.minimum(now + 1, w) - (then == now)
    return c, bands.reshape(P, -1)


GAINS = [
    ("norm_mix0", 8), ("norm_ffn0", 8), ("conv_w", 24), ("norm_mix1", 8), ("norm_ffn1", 8), ("q_a", 3), ("kv_a", 2),
    ("q_nope", 1), ("k_nope", 1), ("g_mix_2", 8), ("g_q_fox", 1), ("g_k_fox", 1), ("pool_scale", 4),
    ("g_mem_q", 8), ("g_mem_kv", 8), ("g_q_mem", 1), ("g_k_mem", 1), ("g_ffn_2", 8)]
GAIN_AT = {name: sum(n for _, n in GAINS[:i]) for i, (name, _) in enumerate(GAINS)}
N_GAINS = sum(n for _, n in GAINS)


def weight_stream(A):
    def rows(w, k0, kn, c0, n):
        return w[k0 * P:(k0 + kn) * P, c0:c0 + n].rearrange("(k p) n -> p k n", p=P)

    def tall(name, w, k, c0, n):
        step = min(k, CHUNK // n)
        return [(name, rows(w, k0, step, c0, n), step, n) for k0 in range(0, k, step)]

    def wide(name, w, k):
        return [(name, rows(w, k0, 2, 0, D), 2, D) for k0 in range(0, k, 2)]

    def ffn(tag, gate, gate_at, up, up_at, down):
        out = []
        for c0, n in FF_GROUPS:
            out += tall(tag + "_up", gate, KD, gate_at + c0, n) + tall(tag + "_up", up, KD, up_at + c0, n)
        return out + wide(tag + "_down", down, KF)

    first = []
    for half in range(2):
        for part in (1, 2, 0):
            first += tall("conv_in", A["conv_w_in"][0], KD, part * D + half * HALF, HALF)
    first += wide("conv_out", A["conv_w_out"][0], KD)
    first += ffn("ffn1", A["ffn_w_gate"][0], 0, A["ffn_w_up"][0], 0, A["ffn_w_down"][0])
    for q in range(2):
        w, n = A["mla_w_down"][0], DOWN_COLS // 2
        first += [("mla_down", rows(w, k0, 4, q * n, n), 4, n) for k0 in (0, 4)]
    for q in range(2):
        first.append(("mla_ukv", rows(A["mla_w_ukv"][0], 0, KKV, q * D, D), KKV, D))
    for q in range(UQ_GROUPS):
        first.append(("mla_uq", rows(A["mla_w_uq"][0], 0, KQ, q * 2 * QK, 2 * QK), KQ, 2 * QK))
    first += wide("mla_o", A["mla_w_o"][0], KD)

    last = []
    for q in range(4):
        last += tall("fox_in", A["w_in_2"][0], KD, q * HALF, HALF)
    for q in range(2):
        last += tall("mem_kv", A["w_mem_kv_2"][0], KD, q * HALF, HALF)
    last += wide("fox_out", A["w_out_2"][0], KD)
    last += tall("mem_q", A["w_mem_q_2"][0], KD, 0, HALF)
    last += wide("mem_out", A["w_mem_out_2"][0], MEM // P)
    gu = A["w_gate_up_2"][0]
    last += ffn("ffn2", gu, 0, gu, FF, A["w_down_2"][0])
    return first, last


def expert_chunk(A, e, c):
    if c < 4 * EG:
        g, part, half = c // 4, c // 2 % 2, c % 2
        w = A["moe_w_up" if part else "moe_w_gate"][0]
        v = w[bass.ds(e, 1), half * 4 * P:(half + 1) * 4 * P, g * HALF:(g + 1) * HALF]
        return v.rearrange("e (k p) n -> p (e k) n", p=P), 4, HALF
    k0 = 2 * (c - 4 * EG)
    v = A["moe_w_down"][0][bass.ds(e, 1), k0 * P:(k0 + 2) * P, :]
    return v.rearrange("e (k p) n -> p (e k) n", p=P), 2, D


def build(nc, A, out, upto=None):
    first, last = weight_stream(A)
    start_of = {}
    for chunks in (first, last):
        for i, c in enumerate(chunks):
            start_of.setdefault(c[0], i)
    MOE0 = len(first)
    PARTS = ["conv", "ffn1", "mla", "moe", "fox", "mem", "ffn2"]
    parts = PARTS if upto is None else PARTS[:PARTS.index(upto) + 1]

    with ExitStack() as ctx:
        sems = {}

        def sem(name):
            if name not in sems:
                sems[name] = ctx.enter_context(nc.semaphore(name))
            return sems[name]

        def sb(name, shape, dt=F32):
            return ctx.enter_context(nc.sbuf_tensor(name, shape, dt))

        raw = sb("raw", [P, RING, CHUNK])
        w_hi = sb("w_hi", [P, RING, CHUNK], F32R)
        w_lo = sb("w_lo", [P, RING, CHUNK], F32R)
        x = sb("x", [P, T, D])
        xT_hi = sb("xT_hi", [P, KD, S], F32R)
        xT_lo = sb("xT_lo", [P, KD, S], F32R)
        junk = sb("junk", [P, T, D], mybir.dt.bfloat16)
        const = sb("const", [P, C_END])
        gain = sb("gain", [P, N_GAINS])
        eps = sb("eps", [P, 1])
        sumsq = sb("sumsq", [P, T])
        root = sb("root", [P, T])
        rinv = sb("rinv", [P, T])
        router = sb("router", [P, KD, E])
        router_hi = sb("router_hi", [P, KD, E], F32R)
        router_lo = sb("router_lo", [P, KD, E], F32R)
        forget_w = sb("forget_w", [P, KD, FOX_HEADS])
        forget_hi = sb("forget_hi", [P, KD, FOX_HEADS], F32R)
        forget_lo = sb("forget_lo", [P, KD, FOX_HEADS], F32R)
        forget_b = sb("forget_b", [P, FOX_HEADS])
        rope_g = sb("rope_g", [P, 2, ROPE])
        pos_i = sb("pos_i", [P, T], I32)
        pos_f = sb("pos_f", [P, T])
        angle = sb("angle", [P, 2, T, ROPE // 2])
        turns = sb("turns", [P, T, ROPE // 2])
        cos2 = sb("cos2", [P, T, 2, ROPE // 2])
        sin = sb("sin", [P, T, ROPE // 2])
        nsin = sb("nsin", [P, T, ROPE // 2])
        overflow = sb("overflow", [1, 1], I32)
        ident = const[:, C_IDENT:C_IDENT + P]
        mask = const[:, C_MASK:C_MASK + 3 * P]
        earlier = const[:, C_BEFORE:C_BEFORE + P]
        upto_now = const[:, C_UPTO:C_UPTO + P]
        ones = const[:, C_ONES:C_ONES + P]
        iota = const[:, C_IOTA:C_IOTA + P]

        M = {}

        def region(**shapes):
            with ExitStack() as inner:
                for name, spec in shapes.items():
                    shape, dt = spec if isinstance(spec, tuple) else (spec, F32)
                    M[name] = inner.enter_context(nc.sbuf_tensor(name, shape, dt))

        region(gain_rows=[P, P], conv_c=[P, T, HALF], conv_v=[P, T, HALF], conv_b=[P, T, HALF],
               vT=[P, KD, S + 2], conv_t=[P, S], conv_y=[P, 4, S],
               yT_hi=([P, KD, S], F32R), yT_lo=([P, KD, S], F32R))
        for p in ("ffn1", "ffn2"):
            region(**{p + "_silu": [P, T, HALF], p + "_act": [P, T, HALF],
                      p + "_hi": ([P, KF, S], F32R), p + "_lo": ([P, KF, S], F32R)})
        region(dn=[P, T, DOWN_COLS], q=[P, T, HEADS * QK], kv=[P, T, HEADS * 2 * P],
               rope=[P, T, 2 * HEADS, ROPE], tmp=[P, CHUNK], cT_hi=([P, KQ + KKV, S], F32R),
               cT_lo=([P, KQ + KKV, S], F32R), qkT=[P, 2, 2 * S], ropeT=[ROPE, 2, 2 * S],
               mla_st=[P, 2, 4, 2],
               rope_cos=[P, 2, T, ROPE], rope_sin=[P, 2, T, ROPE], k_rot=[P, T, ROPE], k_turned=[P, T, ROPE],
               k_bias=[P, T],
               c_ss=[P, 4], c_root=[P, 4], c_rinv=[P, 4], rope_ss=[P, T],
               qk_ss=[P, T, 2 * HEADS], qk_root=[P, T, 2 * HEADS], qk_rinv=[P, T, 2 * HEADS])
        region(moe_g=[P, D], h=[P, T, D], logitsT=[E, S], rt=[P, 20, T, E], rc=[P, 8, T],
               slot_of=[P, T, 2 * E + 1], gate_of=[P, T, 2 * E + 1], most=[P, 2],
               pick=[P, T, P], put=[P, S], gslot=[P, 1],
               gT_hi=([P, KD, P], F32R), gT_lo=([P, KD, P], F32R), e_silu=[P, HALF], e_act=[P, HALF],
               eT_hi=([P, FE // P, P], F32R), eT_lo=([P, FE // P, P], F32R), y=[P, D])
        memory = dict(memT_hi=([P, KD, S], F32R), memT_lo=([P, KD, S], F32R), m_ss=[P, T], m_root=[P, T],
                      m_rinv=[P, T], mh_ss=[P, 2, T, MEM_HEADS], mh_root=[P, 2, T, MEM_HEADS],
                      mh_rinv=[P, 2, T, MEM_HEADS], mem_st=[P, 2, 4, 2])
        region(mem=[P, T, D])
        region(mkv=[P, T, 2 * MEM], **memory,
               z=[P, T, 3 * FOX + HALF], fqT=[P, FOX_HEADS // 2, S], fkT=[P, FOX_HEADS // 2, S],
               mixed=[P, S], cs=[P, 6, T, FOX_HEADS], cT=[FOX_HEADS, S],
               f_ss=[P, T, 2 * FOX_HEADS], f_root=[P, T, 2 * FOX_HEADS], f_rinv=[P, T, 2 * FOX_HEADS],
               fox_st=[P, 2, 4, 2], fox_tmp=[P, CHUNK], bands=[P, len(WINDOWS), T, S], w_pool=[P, len(WINDOWS), P])
        region(mkv_=[P, T, 2 * MEM], **{name + "_": spec for name, spec in memory.items()},
               mkT=[P, MEM_HEADS, S], mq=[P, T, MEM], mqT=[P, MEM_HEADS, S], mem_tmp=[P, 5 * HALF])

        def scratch(v, width):
            return (v[:, :width], v[:, width:3 * width].rearrange("p (b n) -> p b n", b=2),
                    v[:, 3 * width:5 * width].rearrange("p (b n) -> p b n", b=2))

        M["mla_s"], M["mla_p"], M["mla_pT"] = scratch(M["tmp"], 3 * P)
        M["fox_s"], M["fox_p"], M["fox_pT"] = scratch(M["fox_tmp"], 3 * P)
        M["mem_s"], M["mem_p"], M["mem_pT"] = scratch(M["mem_tmp"], 4 * P)

        bank = [ctx.enter_context(nc.psum_tensor(f"bank{i}", [P, HALF], F32)) for i in range(8)]
        block = ctx.enter_context(nc.Block())

        class Stream:
            def __init__(self, tag, chunks):
                self.chunks = chunks
                self.landed = [sem(f"{tag}_landed{i}") for i in range(RING)]
                self.high, self.low, self.used = sem(tag + "_high"), sem(tag + "_low"), sem(tag + "_used")

            def size(self, i):
                return self.chunks[i][2] * self.chunks[i][3] if i < len(self.chunks) else CHUNK

        W1, W2 = Stream("w1", first), Stream("w2", last)

        def load(i, e, stream, view, k, n):
            slot = i % RING
            if i >= RING:
                nc.sync.wait_ge(stream.low, i - RING + 1 + EXPERT_CHUNKS * e)
            nc.sync.dma_start(raw[:, slot, :k * n].rearrange("p (k n) -> p k n", k=k), view)\
                .then_inc(stream.landed[slot], 16)

        def split_high(i, e, stream):
            slot, n = i % RING, stream.size(i)
            nc.scalar.wait_ge(stream.landed[slot], 16 * (i // RING + 1) + 16 * (EXPERT_CHUNKS // RING) * e)
            if i >= RING:
                nc.scalar.wait_ge(stream.used, i - RING + 1 + EXPERT_CHUNKS * e)
            nc.scalar.activation(w_hi[:, slot, :n], raw[:, slot, :n], ACT.Copy).then_inc(stream.high, 1)

        def split_low(i, e, stream):
            slot, n = i % RING, stream.size(i)
            nc.vector.wait_ge(stream.high, i + 1 + EXPERT_CHUNKS * e)
            nc.vector.tensor_tensor(w_lo[:, slot, :n], raw[:, slot, :n], w_hi[:, slot, :n].bitcast(F32),
                                    ALU.subtract).then_inc(stream.low, 1)

        norm_parts = ["conv", "ffn1", "mla", "moe", "fox", "memkv", "mem", "ffn2"]
        per_norm, ffns = {p: 1 for p in norm_parts}, {"ffn1": 1, "ffn2": 1}
        heads = {"mla": HEADS, "fox": FOX_HEADS, "mem": MEM_HEADS}
        gives = {"xT_turned": (4, per_norm), "xT_high": (4, per_norm), "xT_low": (4, per_norm),
                 "squares": (T, per_norm), "root": (1, per_norm), "rinv": (1, per_norm),
                 "silu_done": (len(FF_GROUPS), ffns), "act_done": (len(FF_GROUPS), ffns),
                 "act_turned": (KF // 2, ffns), "act_high": (KF // 2, ffns), "act_low": (KF // 2, ffns),
                 "x_updated": (4, {p: 1 for p in PARTS}),
                 "left_half_summed": (1, {p: int(p != "moe") for p in PARTS})}
        gives |= {n: (1, heads) for n in ("scores_in_psum", "scores_ready", "exps_done", "probs_ready", "pT_turned", "pT",
                                          "values_in_psum", "value_high", "value_low")}

        def before(part, signal):
            times, by = gives[signal]
            names = list(by)
            return times * sum(by[n] for n in names[:names.index(part)])

        class Splitter:
            def __init__(self, split, stream, end):
                self.split, self.stream, self.end, self.done = split, stream, end, 0

            def ahead(self, i):
                while self.done < min(i + AHEAD + 1, self.end):
                    self.split(self.done, 0, self.stream)
                    self.done += 1

        ENDS1 = MOE0 + AHEAD if "moe" in parts else min(MOE0, start_of.get({"conv": "ffn1_up", "ffn1": "mla_down"}.get(parts[-1], ""), MOE0))
        ENDS2 = {"moe": 0, "fox": start_of["mem_q"], "mem": start_of["ffn2_up"]}.get(parts[-1], len(last))

        x_ready = {"conv": ("loaded_x", 16, 16)} | {
            p: ("x_updated", before(p, "x_updated") - 2, before(p, "x_updated")) for p in PARTS[1:]}
        GAIN_OF = {"conv": "norm_mix0", "ffn1": "norm_ffn0", "mla": "norm_mix1", "moe": "norm_ffn1", "fox": "g_mix_2",
                   "mem": "g_mem_q", "ffn2": "g_ffn_2"}

        def g(name, k=0):
            return gain[:, GAIN_AT[name] + k:GAIN_AT[name] + k + 1]

        def per_feature(c, n):
            return c.unsqueeze(len(c.shape)).broadcast_to(list(c.shape) + [n])

        @block.sync
        def _(sp):
            sp.dma_start(x[:, :, :], A["x"][0].rearrange("(t p) d -> p t d", p=P)).then_inc(sem("loaded_x"), 16)
            sp.dma_start(const[:, :], A["shape_const"]).then_inc(sem("loaded_const"), 16)
            for i, (_, view, k, n) in enumerate(first[:min(ENDS1, MOE0)]):
                load(i, 0, W1, view, k, n)
            if "moe" in parts:
                with sp.Fori(0, E) as e:
                    for c in range(EXPERT_CHUNKS):
                        load(MOE0 + c, e, W1, *expert_chunk(A, e, c))
                sp.wait_ge(sem("overflow_known"), 1)
                over = sp.value_load(overflow[0:1, 0:1], min_val=0, max_val=1)
                with sp.If(over > 0):
                    with sp.Fori(0, E) as e:
                        for c in range(EXPERT_CHUNKS):
                            load(MOE0 + E * EXPERT_CHUNKS + c, e, W1, *expert_chunk(A, e, c))
                for i, (_, view, k, n) in enumerate(last[:ENDS2]):
                    if i < RING:
                        last_one = MOE0 + E * EXPERT_CHUNKS - 1
                        last_one -= (last_one - i) % RING
                        sp.wait_ge(W1.low, last_one + 1 + over * (E * EXPERT_CHUNKS))
                    load(i, 0, W2, view, k, n)
            for half in range(2):
                sp.wait_ge(sem("x_updated"), before(parts[-1], "x_updated") + 2 * half + 2)
                cols = slice(half * HALF, (half + 1) * HALF)
                sp.dma_start(out[0, :, cols].rearrange("(t p) d -> p t d", p=P), x[:, :, cols])\
                    .then_inc(sem("stored"), 16)
            sp.wait_ge(sem("stored"), 32)

        @block.gpsimd
        def _(pool):
            def small(dst, src, name, scattered=False):
                pool.dma_start(dst, src, allow_slow_non_contiguous=scattered).then_inc(sem("loaded_" + name), 16)

            small(pos_i[:, :], A["positions"][0].rearrange("(t p) -> p t", p=P), "rope", True)
            small(rope_g[:, 0, :], A["mla_q_norm"][0:1, NOPE:].partition_broadcast(P), "rope")
            small(rope_g[:, 1, :], A["mla_k_norm"][0:1, NOPE:].partition_broadcast(P), "rope")
            small(router[:, :, :], A["moe_router"][0].rearrange("(k p) e -> p k e", p=P), "router")
            small(forget_w[:, :, :], A["w_in_2"][0][:, 3 * FOX + HALF:].rearrange("(k p) h -> p k h", p=P), "forget")
            small(forget_b[:, :], A["b_forget_2"][0:1, :].partition_broadcast(P), "forget")
            if "moe" in parts:
                pool.wait_ge(sem("x_updated"), before("mla", "x_updated") + 4)
                small(M["moe_g"][:, :], A["norm_ffn"][1:2, :].partition_broadcast(P), "moe_g")
            if "fox" in parts:
                pool.wait_ge(sem("x_updated"), before("moe", "x_updated") + 4)
                pool.wait_ge(W2.high, 2)
                small(M["mem"][:, :, :], A["mem_2"][0].rearrange("(t p) d -> p t d", p=P), "mem")
                pool.wait_ge(W2.high, 4)
                small(M["bands"][:, :, :, :].rearrange("p g t s -> p (g t s)"), A["shape_bands"], "pool")
                small(M["w_pool"][:, :, :], A["w_pool_2"][0].rearrange("g c d -> c g d"), "pool")

        @block.scalar
        def _(act):
            A_ = nc.scalar.activation
            at = GAIN_AT
            rows = M["gain_rows"]

            def load_rows(name, src, n):
                act.dma_start(rows[at[name]:at[name] + n, :], src).then_inc(sem("loaded_gains"), 16)

            def rows_of(v):
                return v.rearrange("(k p) -> k p", p=P)

            def load_pair(name, src):
                for half in (0, 1):
                    act.dma_start(rows[at[name]:at[name] + 1, half * FOX_DIM:(half + 1) * FOX_DIM],
                                  src).then_inc(sem("loaded_gains"), 16)

            load_rows("norm_mix0", rows_of(A["norm_mix"][0]), 8)
            load_rows("norm_ffn0", rows_of(A["norm_ffn"][0]), 8)
            load_rows("conv_w", A["conv_w"][0].rearrange("w (k p) -> (w k) p", p=P), 24)
            load_rows("norm_mix1", rows_of(A["norm_mix"][1]), 8)
            load_rows("norm_ffn1", rows_of(A["norm_ffn"][1]), 8)
            load_rows("q_a", rows_of(A["mla_q_a_norm"][0]), 3)
            load_rows("kv_a", rows_of(A["mla_kv_a_norm"][0]), 2)
            load_rows("q_nope", A["mla_q_norm"][0:1, :NOPE], 1)
            load_rows("k_nope", A["mla_k_norm"][0:1, :NOPE], 1)
            load_rows("g_mix_2", rows_of(A["g_mix_2"][0]), 8)
            load_pair("g_q_fox", A["g_q_fox_2"])
            load_pair("g_k_fox", A["g_k_fox_2"])
            load_rows("pool_scale", rows_of(A["pool_scale_2"][0]), 4)
            load_rows("g_mem_q", rows_of(A["g_mem_q_2"][0]), 8)
            load_rows("g_mem_kv", rows_of(A["g_mem_kv_2"][0]), 8)
            load_rows("g_q_mem", A["g_q_mem_2"], 1)
            load_rows("g_k_mem", A["g_k_mem_2"], 1)
            load_rows("g_ffn_2", rows_of(A["g_ffn_2"][0]), 8)

            w1, w2 = Splitter(split_high, W1, ENDS1), Splitter(split_high, W2, ENDS2)

            def used(w, i):
                w.ahead(i)
                act.wait_ge(w.stream.used, i + 1)

            def norm(p, src, ready, gname, hi, ss, rt, n=D):
                for b in range(4):
                    act.wait_ge(sem("xT_turned"), before(p, "xT_turned") + b + 1)
                    for j in range(2):
                        k = 2 * b + j
                        ins = A_(hi[:, k, :], bank[4 + b][:, j * S:(j + 1) * S], ACT.Copy, scale=g(gname, k))
                    ins.then_inc(sem("xT_high"), 1)
                act.wait_ge(sem(ready[0]), ready[2])
                mean_square(p, src, ss, rt)

            def mean_square(p, src, ss, rt):
                for t in range(T):
                    ins = A_(junk[:, t, :], src[:, t, :], ACT.Square, accum_out=ss[:, t:t + 1])
                    ins.then_inc(sem("squares"), 1)
                act.wait_ge(sem("squares"), before(p, "squares") + T)
                A_(rt[:, :], ss[:, :], ACT.Sqrt, bias=eps[:, :], scale=1.0 / D).then_inc(sem("root"), 1)

            def ffn(p, w):
                first_chunk, hi = start_of[p + "_up"], M[p + "_hi"]
                norm(p, x, x_ready[p], GAIN_OF[p], xT_hi, sumsq, root)
                act.wait_ge(sem("rinv"), before(p, "rinv") + 1)
                turned = 0

                def act_high(group):
                    nonlocal turned
                    for j in range(FF_GROUPS[group][1] // S):
                        act.wait_ge(sem("act_turned"), before(p, "act_turned") + turned + 1)
                        b = 4 + 2 * (group % 2) + j
                        A_(hi[:, 2 * turned:2 * turned + 2, :].rearrange("p k s -> p (k s)"), bank[b][:, :],
                           ACT.Copy).then_inc(sem("act_high"), 1)
                        turned += 1

                i = first_chunk
                for group, (_, n) in enumerate(FF_GROUPS):
                    parts_of = KD // (CHUNK // n) if CHUNK // n < KD else 1
                    used(w, i + parts_of - 1)
                    i += 2 * parts_of
                    if group:
                        act.wait_ge(sem("act_done"), before(p, "act_done") + group)
                    for t in range(T):
                        ins = A_(M[p + "_silu"][:, t, :n], bank[t][:, :n], ACT.Silu, scale=rinv[:, t:t + 1])
                    ins.then_inc(sem("silu_done"), 1)
                    if group:
                        act_high(group - 1)
                w.ahead(i - 1)
                act_high(len(FF_GROUPS) - 1)
                w.ahead(start_of[p + "_down"] + KF // 2 - 1)

            def attention(p, n_heads, blocks, scale, turn, value_part, filler=None):
                st, s_, p_, pT = M[p + "_st"], M[p + "_s"], M[p + "_p"], M[p + "_pT"]
                width = blocks[-1][1]

                def exps(h):
                    act.wait_ge(sem("scores_ready"), before(p, "scores_ready") + h + 1)
                    if h >= 2:
                        act.wait_ge(sem("pT_turned"), before(p, "pT_turned") + h - 1)
                    for t, (a, b) in enumerate(blocks):
                        ins = A_(p_[:, h % 2, a:b], s_[:, a:b], ACT.Exp, bias=st[:, h % 2, 1, t:t + 1],
                                 scale=scale, accum_out=st[:, h % 2, 2, t:t + 1])
                    ins.then_inc(sem("exps_done"), 1)

                def copy_turned(h):
                    act.wait_ge(sem("pT_turned"), before(p, "pT_turned") + h + 1)
                    if h >= 2:
                        act.wait_ge(sem("values_in_psum"), before(p, "values_in_psum") + h - 1)
                    A_(pT[:, h % 2, :], bank[7][:, :width], ACT.Copy).then_inc(sem("pT"), 1)

                def value_high(h):
                    act.wait_ge(sem("values_in_psum"), before(p, "values_in_psum") + h + 1)
                    dst, src = value_part(h, xT_hi)
                    A_(dst, src, ACT.Copy).then_inc(sem("value_high"), 1)

                def filled(h):
                    if filler:
                        filler(h)

                for i in range(-2, n_heads + 1):
                    for stage, h in ((turn, i + 2), (copy_turned, i), (value_high, i - 1), (filled, i), (exps, i + 1)):
                        if 0 <= h < n_heads:
                            stage(h)

            act.wait_ge(sem("gains_turned"), 1)
            A_(gain[:, :], bank[0][:, :N_GAINS], ACT.Copy).then_inc(sem("gains_ready"), 1)
            act.wait_ge(sem("angles"), 1)
            act.wait_ge(sem("gains_ready"), 1)
            for j in range(2):
                A_(cos2[:, :, j, :], angle[:, 1, :, :], ACT.Sin)
            A_(sin[:, :, :], angle[:, 0, :, :], ACT.Sin).then_inc(sem("rope_tables"), 1)
            act.wait_ge(sem("rope_tables"), 1)
            A_(nsin[:, :, :], sin[:, :, :], ACT.Copy, scale=-1.0).then_inc(sem("rope_tables"), 1)

            w1.ahead(0)
            norm("conv", x, x_ready["conv"], GAIN_OF["conv"], xT_hi, sumsq, root)
            act.wait_ge(sem("rinv"), before("conv", "rinv") + 1)

            def conv_gate(q, buf, name):
                used(w1, 2 * q + 1)
                for t in range(T):
                    ins = A_(buf[:, t, :], bank[2 * (q % 2) + t][:, :], ACT.Copy, scale=rinv[:, t:t + 1])
                ins.then_inc(sem(name), 1)

            def conv_v_turned(half):
                for j in range(2):
                    act.wait_ge(sem("conv_v_turned"), 2 * half + j + 1)
                    k = 4 * half + 2 * j
                    A_(M["vT"][:, k:k + 2, 2:], bank[4 + j][:, :].rearrange("p (k s) -> p k s", k=2),
                       ACT.Copy).then_inc(sem("conv_vT"), 1)

            def conv_high(half):
                act.wait_ge(sem("conv_y_done"), 4 * half + 4)
                A_(M["yT_hi"][:, 4 * half:4 * half + 4, :], M["conv_y"][:, :, :], ACT.Copy)\
                    .then_inc(sem("conv_y_high"), 1)

            conv_gate(0, M["conv_c"], "conv_c_done")
            conv_gate(2, M["conv_b"], "conv_b_done")
            conv_v_turned(0)
            act.wait_ge(sem("conv_v_done"), 1)
            conv_gate(3, M["conv_c"], "conv_c_done")
            w1.ahead(9)
            conv_high(0)
            act.wait_ge(sem("conv_b_turned"), 2)
            conv_gate(5, M["conv_b"], "conv_b_done")
            conv_v_turned(1)
            conv_high(1)
            w1.ahead(start_of["conv_out"] + 3)

            if "ffn1" in parts:
                ffn("ffn1", w1)

            if "mla" in parts:
                dn, q, kv, tmp = M["dn"], M["q"], M["kv"], M["tmp"]
                norm("mla", x, x_ready["mla"], GAIN_OF["mla"], xT_hi, sumsq, root)
                act.wait_ge(sem("rinv"), before("mla", "rinv") + 1)
                i, n = start_of["mla_down"], DOWN_COLS // 2
                for j in range(2):
                    used(w1, i + 2 * j + 1)
                    for t in range(T):
                        ins = A_(dn[:, t, j * n:(j + 1) * n], bank[2 * j + t][:, :n], ACT.Copy,
                                 scale=rinv[:, t:t + 1])
                    ins.then_inc(sem("mla_dn"), 1)
                for b in range(3):
                    act.wait_ge(sem("mla_c_turned"), b + 1)
                    for k in range(2 * b, min(2 * b + 2, KQ + KKV)):
                        gk = g("q_a", k) if k < KQ else g("kv_a", k - KQ)
                        ins = A_(M["cT_hi"][:, k, :], bank[4 + b][:, (k % 2) * S:(k % 2 + 1) * S], ACT.Copy, scale=gk)
                    ins.then_inc(sem("mla_c_high"), 1)
                act.wait_ge(sem("mla_dn"), 2)
                for t in range(T):
                    for j, (a, b) in enumerate(((0, Q_RANK), (Q_RANK, Q_RANK + KV_RANK))):
                        ins = A_(junk[:, t, a:b], dn[:, t, a:b], ACT.Square, accum_out=M["c_ss"][:, 2 * j + t:2 * j + t + 1])
                    ins.then_inc(sem("mla_c_squares"), 1)
                act.wait_ge(sem("mla_c_squares"), T)
                A_(M["c_root"][:, 0:2], M["c_ss"][:, 0:2], ACT.Sqrt, bias=eps[:, :], scale=1.0 / Q_RANK)
                A_(M["c_root"][:, 2:4], M["c_ss"][:, 2:4], ACT.Sqrt, bias=eps[:, :], scale=1.0 / KV_RANK)\
                    .then_inc(sem("mla_c_root"), 1)
                for t in range(T):
                    ins = A_(junk[:, t, Q_RANK + KV_RANK:DOWN_COLS], dn[:, t, Q_RANK + KV_RANK:], ACT.Square,
                             accum_out=M["rope_ss"][:, t:t + 1])
                ins.then_inc(sem("mla_rope_squares"), 1)
                act.wait_ge(sem("mla_rope_squares"), 1)
                for pair in range(HEADS // 2):
                    w1.ahead(start_of["mla_ukv"] + pair // 2)
                    act.wait_ge(sem("mla_kv_done"), pair + 1)
                    for h in (2 * pair, 2 * pair + 1):
                        for t in range(T):
                            ins = A_(junk[:, t, h * NOPE:(h + 1) * NOPE], kv[:, t, h * 2 * P:h * 2 * P + NOPE],
                                     ACT.Square, accum_out=M["qk_ss"][:, t, HEADS + h:HEADS + h + 1])
                    ins.then_inc(sem("mla_k_squares"), 1)
                act.wait_ge(sem("mla_k_squares"), HEADS // 2)
                act.wait_ge(sem("mla_k_bias"), 1)
                for t in range(T):
                    ins = A_(M["qk_root"][:, t, HEADS:], M["qk_ss"][:, t, HEADS:], ACT.Sqrt, bias=M["k_bias"][:, t:t + 1],
                             scale=1.0 / QK)
                ins.then_inc(sem("mla_qk_root"), 1)
                w1.ahead(start_of["mla_uq"])
                in_junk = D // QK
                for pair in range(UQ_GROUPS):
                    act.wait_ge(W1.used, start_of["mla_uq"] + pair + 1)
                    for t in range(T):
                        ins = A_(q[:, t, pair * 2 * QK:(pair + 1) * 2 * QK], bank[2 * (pair % 2) + t][:, :2 * QK], ACT.Copy,
                                 scale=M["c_rinv"][:, t:t + 1])
                    ins.then_inc(sem("mla_q_done"), 1)
                    act.wait_ge(sem("mla_q_done"), pair + 1)
                    for h in (2 * pair, 2 * pair + 1):
                        for t in range(T):
                            at_ = HALF + ((h - in_junk) * T + t) * QK
                            dst = junk[:, t, h * QK:(h + 1) * QK] if h < in_junk else tmp[:, at_:at_ + QK]
                            ins = A_(dst, q[:, t, h * QK:(h + 1) * QK], ACT.Square,
                                     accum_out=M["qk_ss"][:, t, h:h + 1])
                    ins.then_inc(sem("mla_q_squares"), 1)
                act.wait_ge(sem("mla_q_squares"), UQ_GROUPS)
                A_(M["qk_root"][:, :, :HEADS], M["qk_ss"][:, :, :HEADS], ACT.Sqrt, bias=eps[:, :], scale=1.0 / QK)\
                    .then_inc(sem("mla_qk_root"), 1)

                def turn(h):
                    act.wait_ge(sem("mla_nope_turned"), h + 1)
                    if h >= 2:
                        act.wait_ge(sem("scores_in_psum"), before("mla", "scores_in_psum") + h - 1)
                    A_(M["qkT"][:, h % 2, :S], bank[4][:, :S], ACT.Copy, scale=g("q_nope"))
                    A_(M["qkT"][:, h % 2, S:], bank[4][:, S:], ACT.Copy, scale=g("k_nope")).then_inc(sem("mla_qkT"), 1)

                def split_out(h):
                    w1.ahead(start_of["mla_o"] + h // 2 - AHEAD)

                attention("mla", HEADS, [(0, P), (P, 3 * P)], QK ** -0.5, turn,
                          lambda h, o: (o[:, h, :], bank[h % 2][:, :S]), split_out)
                w1.ahead(start_of["mla_o"] + 3)

            if "moe" in parts:
                h_, rt, rc = M["h"], M["rt"], M["rc"]
                act.wait_ge(sem("loaded_router"), 16)
                A_(router_hi[:, :, :], router[:, :, :], ACT.Copy).then_inc(sem("router_high"), 1)
                norm("moe", x, x_ready["moe"], GAIN_OF["moe"], xT_hi, sumsq, root)
                act.wait_ge(sem("moe_logits_ready"), 1)
                for t in range(T):
                    ins = A_(rt[:, 1, t, :], rt[:, 0, t, :], ACT.Exp, bias=rc[:, 0, t:t + 1],
                             accum_out=rc[:, 1, t:t + 1])
                ins.then_inc(sem("moe_exp"), 1)

                def job_high(job, e, dst):
                    act.wait_ge(sem("moe_job"), PROLOGUE_JOBS + job + 1 + JOBS * e)
                    A_(dst, bank[6 + job % 2][:, :], ACT.Copy).then_inc(sem("moe_job_high"), 1)

                def gather_high(job, e, half):
                    job_high(job, e, M["gT_hi"][:, 4 * half:4 * half + 4, :].rearrange("p k s -> p (k s)"))

                def turn_high(job, e, group):
                    job_high(job, e, M["eT_hi"][:, 4 * group:4 * group + 4, :].rearrange("p k s -> p (k s)"))

                def silu(e, group):
                    act.wait_ge(W1.used, MOE0 + 4 * group + 2 + EXPERT_CHUNKS * e)
                    act.wait_ge(sem("moe_act_done"), 1 + group + EG * e)
                    A_(M["e_silu"][:, :], bank[2 * (group % 2)][:, :], ACT.Silu).then_inc(sem("moe_silu_done"), 1)

                def expert(e, more):
                    for c in range(EXPERT_CHUNKS):
                        if c + AHEAD < EXPERT_CHUNKS or more:
                            split_high(MOE0 + c + AHEAD, e, W1)
                        if c in (1, 5, 9, 13):
                            silu(e, c // 4)
                        if c in (5, 9, 13):
                            turn_high(JOB_TURN[c // 4 - 1], e, c // 4 - 1)
                        if c == 15:
                            gather_high(8, e, 0)
                            gather_high(9, e, 1)
                        if c == 16:
                            turn_high(11, e, 3)
                    act.wait_ge(W1.used, MOE0 + EXPERT_CHUNKS + EXPERT_CHUNKS * e)
                    for half in range(2):
                        ins = A_(M["y"][:, half * HALF:(half + 1) * HALF], bank[4 + half][:, :], ACT.Copy)
                    ins.then_inc(sem("moe_y"), 1)

                A_(M["y"][:, :], const[:, :D], ACT.Copy, scale=0.0).then_inc(sem("moe_y"), 1)
                gather_high(-4, 0, 0)
                gather_high(-3, 0, 1)
                with act.Fori(0, E - 1) as e:
                    expert(e, True)
                expert(E - 1, False)
                act.wait_ge(sem("overflow_known"), 1)
                over = act.value_load(overflow[0:1, 0:1], min_val=0, max_val=1)
                with act.If(over > 0):
                    for c in range(AHEAD):
                        split_high(MOE0 + c, E, W1)
                    with act.Fori(E, 2 * E - 1) as e:
                        expert(e, True)
                    expert(2 * E - 1, False)

            if "fox" in parts:
                act.wait_ge(W1.used, MOE0 + E * EXPERT_CHUNKS + over * (E * EXPERT_CHUNKS))
                w2.ahead(0)

                z, cs = M["z"], M["cs"]
                norm("fox", x, x_ready["fox"], GAIN_OF["fox"], xT_hi, sumsq, root)
                act.wait_ge(sem("loaded_forget"), 32)
                A_(forget_hi[:, :, :], forget_w[:, :, :], ACT.Copy).then_inc(sem("forget_high"), 1)
                act.wait_ge(sem("rinv"), before("fox", "rinv") + 1)
                for j in range(2):
                    used(w2, 2 * j + 1)
                    for t in range(T):
                        ins = A_(z[:, t, j * HALF:(j + 1) * HALF], bank[2 * j + t][:, :], ACT.Copy,
                                 scale=rinv[:, t:t + 1])
                    ins.then_inc(sem("fox_qk_done"), 1)
                    if j == 0:
                        norm("memkv", M["mem"], ("loaded_mem", 16, 16), "g_mem_kv", M["memT_hi"], M["m_ss"], M["m_root"])
                act.wait_ge(sem("fox_qk_done"), 2)
                for t in range(T):
                    A_(M["fox_tmp"][:, t * 2 * FOX:(t + 1) * 2 * FOX], z[:, t, :2 * FOX], ACT.Square)\
                        .then_inc(sem("fox_head_squares"), 1)
                act.wait_ge(sem("fox_sums"), T)
                A_(M["f_root"][:, :, :], M["f_ss"][:, :, :], ACT.Sqrt, bias=eps[:, :], scale=1.0 / FOX_DIM)\
                    .then_inc(sem("fox_qk_root"), 1)
                act.wait_ge(sem("forget_abs"), 1)
                A_(cs[:, 2, :, :], cs[:, 1, :, :], ACT.Exp).then_inc(sem("forget_exp"), 1)
                act.wait_ge(sem("forget_exp"), 1)
                A_(cs[:, 3, :, :], cs[:, 2, :, :], ACT.Ln, bias=ones[:, 0:1]).then_inc(sem("forget_ln"), 1)
                w2.ahead(start_of["mem_kv"] - 3)
                for k in range(FOX_HEADS // 2):
                    act.wait_ge(sem("fox_pair_turned"), k + 1)
                    A_(M["fqT"][:, k, :], bank[4 + k % 2][:, :S], ACT.Copy, scale=g("g_q_fox"))
                    A_(M["fkT"][:, k, :], bank[4 + k % 2][:, S:], ACT.Copy, scale=g("g_k_fox"))\
                        .then_inc(sem("fox_qkT"), 1)
                w2.ahead(start_of["mem_kv"] - 1)

                def fox_value(h, o):
                    rows_ = slice(FOX_DIM * (h % 2), FOX_DIM * (h % 2 + 1))
                    return o[rows_, h // 2, :], bank[h // 2 % 2][rows_, :S]

                def beside(h):
                    if 1 <= h <= len(WINDOWS):
                        act.wait_ge(sem("pool_mapped"), h)
                        A_(xT_hi[:, KD // 2 + h - 1, :], bank[5][:, :S], ACT.Copy, scale=g("pool_scale", h - 1))\
                            .then_inc(sem("pool_high"), 1)
                    if h < len(WINDOWS):
                        act.wait_ge(sem("pool_mixed"), h + 1)
                        if h:
                            act.wait_ge(sem("pool_mapped"), h)
                        A_(M["mixed"][:, :], bank[4][:, :S], ACT.Copy).then_inc(sem("pool_mixed_copied"), 1)
                    if h in SPLIT_BESIDE:
                        w2.ahead(start_of["mem_kv"] + SPLIT_BESIDE.index(h))
                    if h == 5:
                        act.wait_ge(W2.used, start_of["mem_kv"] + 2)
                        for t in range(T):
                            ins = A_(M["mkv"][:, t, :MEM], bank[2 + t][:, :], ACT.Copy, scale=M["m_rinv"][:, t:t + 1])
                        ins.then_inc(sem("mem_k_done"), 1)

                attention("fox", FOX_HEADS, [(0, P), (P, 3 * P)], FOX_DIM ** -0.5, lambda h: None, fox_value, beside)
                w2.ahead(start_of["fox_out"])

                def memory_squares(j, src):
                    A_(M["mem_tmp"][:, :T * MEM].rearrange("p (t n) -> p t n", t=T), src, ACT.Square)\
                        .then_inc(sem("mem_head_squares"), 1)
                    act.wait_ge(sem("mem_sums"), j + 1)
                    A_(M["mh_root"][:, j, :, :], M["mh_ss"][:, j, :, :], ACT.Sqrt, bias=eps[:, :], scale=1.0 / MEM_DIM)\
                        .then_inc(sem("mem_qk_root"), 1)

                def turned_pairs(dst, gname, signal, name):
                    for k in range(MEM_HEADS // 2):
                        act.wait_ge(sem(signal), k + 1)
                        A_(dst[:, 2 * k:2 * k + 2, :], bank[4 + k][:, :].rearrange("p (h s) -> p h s", h=2), ACT.Copy,
                           scale=g(gname)).then_inc(sem(name), 1)

                act.wait_ge(sem("mem_k_done"), 1)
                act.wait_ge(sem("value_low"), before("fox", "value_low") + FOX_HEADS)
                memory_squares(0, M["mkv"][:, :, :MEM])
                w2.ahead(start_of["fox_out"] + 1)
                turned_pairs(M["mkT"], "g_k_mem", "mem_keys_turned", "mem_kT")
                w2.ahead(start_of["fox_out"] + 3)

            if "mem" in parts:
                mq = M["mq"]
                norm("mem", x, x_ready["mem"], GAIN_OF["mem"], xT_hi, sumsq, root)
                act.wait_ge(sem("rinv"), before("mem", "rinv") + 1)
                used(w2, start_of["mem_q"] + 1)
                for t in range(T):
                    ins = A_(mq[:, t, :], bank[t][:, :], ACT.Copy, scale=rinv[:, t:t + 1])
                ins.then_inc(sem("mem_q_done"), 1)
                turned_pairs(M["mqT"], "g_q_mem", "mem_queries_turned", "mem_qT")
                act.wait_ge(sem("mem_q_done"), 1)
                memory_squares(1, mq[:, :, :])
                attention("mem", MEM_HEADS, [(0, S), (S, 2 * S)], MEM_DIM ** -0.5, lambda h: None,
                          lambda h, o: (o[:, h, :], bank[h % 2][:, :S]))
                w2.ahead(start_of["mem_out"] + 1)

            if "ffn2" in parts:
                ffn("ffn2", w2)

        @block.vector
        def _(dve):
            V = nc.vector
            links = 0

            def link(ins):
                nonlocal links
                links += 1
                ins.then_inc(sem("vector_chain"), 1)
                dve.wait_ge(sem("vector_chain"), links)

            w1, w2 = Splitter(split_low, W1, ENDS1), Splitter(split_low, W2, ENDS2)

            def used(w, i):
                w.ahead(i)
                dve.wait_ge(w.stream.used, i + 1)

            def norm_low(p, gname, lo, hi):
                for b in range(4):
                    dve.wait_ge(sem("xT_high"), before(p, "xT_high") + b + 1)
                    for j in range(2):
                        k = 2 * b + j
                        ins = V.scalar_tensor_tensor(lo[:, k, :], bank[4 + b][:, j * S:(j + 1) * S], g(gname, k),
                                                     hi[:, k, :].bitcast(F32), ALU.mult, ALU.subtract)
                    ins.then_inc(sem("xT_low"), 1)

            def inverse(of, name, n, out_, in_):
                dve.wait_ge(sem(of), n)
                V.reciprocal(out_, in_).then_inc(sem(name), 1)
                dve.wait_ge(sem(name), n)

            def norm(p):
                norm_low(p, GAIN_OF[p], xT_lo, xT_hi)
                inverse("root", "rinv", before(p, "rinv") + 1, rinv[:, :], root[:, :])

            def residual(p, w, last_chunk):
                w.ahead(last_chunk)
                for half in range(2):
                    if half == 0:
                        dve.wait_ge(sem("left_half_summed"), before(p, "left_half_summed") + 1)
                    else:
                        dve.wait_ge(w.stream.used, last_chunk + 1)
                    for t in range(T):
                        xs = x[:, t, half * HALF:(half + 1) * HALF]
                        V.tensor_tensor(xs, xs, bank[2 * t + half][:, :], ALU.add).then_inc(sem("x_updated"), 1)
                dve.wait_ge(sem("x_updated"), before(p, "x_updated") + 4)

            def ffn(p, w):
                act_, lo, hi = M[p + "_act"], M[p + "_lo"], M[p + "_hi"]
                norm(p)
                turned = 0

                def act_low(group):
                    nonlocal turned
                    for j in range(FF_GROUPS[group][1] // S):
                        dve.wait_ge(sem("act_high"), before(p, "act_high") + turned + 1)
                        b = 4 + 2 * (group % 2) + j
                        pair = slice(2 * turned, 2 * turned + 2)
                        V.tensor_tensor(lo[:, pair, :].rearrange("p k s -> p (k s)"), bank[b][:, :],
                                        hi[:, pair, :].bitcast(F32).rearrange("p k s -> p (k s)"),
                                        ALU.subtract).then_inc(sem("act_low"), 1)
                        turned += 1

                i = start_of[p + "_up"]
                for group, (_, n) in enumerate(FF_GROUPS):
                    parts_of = KD // (CHUNK // n) if CHUNK // n < KD else 1
                    i += 2 * parts_of
                    if group:
                        w.ahead(i - parts_of - 1)
                        act_low(group - 1)
                    used(w, i - 1)
                    dve.wait_ge(sem("silu_done"), before(p, "silu_done") + group + 1)
                    for t in range(T):
                        ins = V.scalar_tensor_tensor(act_[:, t, :n], bank[2 + t][:, :n], rinv[:, t:t + 1],
                                                     M[p + "_silu"][:, t, :n], ALU.mult, ALU.mult)
                    ins.then_inc(sem("act_done"), 1)
                w.ahead(i - 1)
                act_low(len(FF_GROUPS) - 1)
                residual(p, w, start_of[p + "_down"] + KF // 2 - 1)

            def attention(p, n_heads, blocks, scale, turn, add_bias, value_part, filler=None):
                st, s_, p_ = M[p + "_st"], M[p + "_s"], M[p + "_p"]

                def scores(h):
                    dve.wait_ge(sem("scores_in_psum"), before(p, "scores_in_psum") + h + 1)
                    if h:
                        dve.wait_ge(sem("exps_done"), before(p, "exps_done") + h)
                    add_bias(h, s_)
                    for t, (a, b) in enumerate(blocks):
                        ins = V.tensor_reduce(st[:, h % 2, 0, t:t + 1], s_[:, a:b], AX.X, ALU.max)
                    link(ins)
                    V.tensor_scalar(st[:, h % 2, 1, :], st[:, h % 2, 0, :], -scale, None, ALU.mult)\
                        .then_inc(sem("scores_ready"), 1)

                def probabilities(h):
                    dve.wait_ge(sem("exps_done"), before(p, "exps_done") + h + 1)
                    link(V.reciprocal(st[:, h % 2, 3, :], st[:, h % 2, 2, :]))
                    for t, (a, b) in enumerate(blocks):
                        ins = V.tensor_scalar(p_[:, h % 2, a:b], p_[:, h % 2, a:b], st[:, h % 2, 3, t:t + 1], None,
                                              ALU.mult)
                    ins.then_inc(sem("probs_ready"), 1)

                def value_low(h):
                    dve.wait_ge(sem("value_high"), before(p, "value_high") + h + 1)
                    lo_, src = value_part(h, xT_lo)
                    hi_, _ = value_part(h, xT_hi)
                    V.tensor_tensor(lo_, src, hi_.bitcast(F32), ALU.subtract).then_inc(sem("value_low"), 1)

                def filled(h):
                    if filler:
                        filler(h)

                for i in range(-2, n_heads + 1):
                    for stage, h in ((probabilities, i), (turn, i + 2), (scores, i + 1), (value_low, i - 1),
                                     (filled, i)):
                        if 0 <= h < n_heads:
                            stage(h)

            V.memset(eps[:, :], EPS).then_inc(sem("zeroed"), 1)
            V.memset(M["vT"][:, :, 0:2], 0.0).then_inc(sem("zeroed"), 1)
            dve.wait_ge(sem("zeroed"), 2)
            dve.wait_ge(sem("loaded_rope"), 48)
            dve.wait_ge(sem("loaded_const"), 16)
            link(V.tensor_copy(pos_f[:, :], pos_i[:, :]))
            freq = const[:, C_FREQ:C_FREQ + ROPE // 2]
            for t in range(T):
                ins = V.tensor_scalar(angle[:, 0, t, :], freq, pos_f[:, t:t + 1], None, ALU.mult)
            link(ins)
            a0, a1 = angle[:, 0, :, :], angle[:, 1, :, :]
            link(V.tensor_scalar(turns[:, :, :], a0, float(1 / (2 * np.pi)), 1.5 * 2.0 ** 23, ALU.mult, ALU.add))
            link(V.tensor_scalar(turns[:, :, :], turns[:, :, :], 1.5 * 2.0 ** 23, None, ALU.subtract))
            two_pi = 2 * np.pi
            c1 = 6.28125
            c2 = float(np.round((two_pi - c1) * 2.0 ** 20) / 2.0 ** 20)
            c3 = float(two_pi - c1 - c2)
            for c in (c1, c2, c3):
                link(V.scalar_tensor_tensor(a0, turns[:, :, :], -c, a0, ALU.mult, ALU.add))
            link(V.tensor_scalar(a1, a0, float(np.pi / 2), None, ALU.add))
            link(V.tensor_scalar(turns[:, :, :], a1, float(np.pi), -two_pi, ALU.is_gt, ALU.mult))
            link(V.tensor_tensor(a1, a1, turns[:, :, :], ALU.add))
            V.tensor_scalar(angle[:, :, :, :], angle[:, :, :, :], 3.1415925, -3.1415925, ALU.min, ALU.max)\
                .then_inc(sem("angles"), 1)

            dve.wait_ge(sem("gains_ready"), 1)
            w1.ahead(0)
            norm("conv")

            def conv_v(half):
                used(w1, 6 * half + 3)
                dve.wait_ge(sem("conv_c_done"), half + 1)
                if half:
                    dve.wait_ge(sem("conv_v_turned"), 2)
                for t in range(T):
                    ins = V.scalar_tensor_tensor(M["conv_v"][:, t, :], bank[2 * ((3 * half + 1) % 2) + t][:, :],
                                                 rinv[:, t:t + 1], M["conv_c"][:, t, :], ALU.mult, ALU.mult)
                ins.then_inc(sem("conv_v_done"), 1)

            def conv_taps(half):
                if half:
                    dve.wait_ge(sem("conv_y_high"), 1)
                for k in range(4 * half, 4 * half + 4):
                    j = k // 2 % 2
                    dve.wait_ge(sem("conv_vT"), 2 * half + j + 1)
                    vT, t1 = M["vT"], M["conv_t"][:, :]
                    link(V.tensor_scalar(t1, vT[:, k, 0:S], g("conv_w", k), None, ALU.mult))
                    for tap in (1, 2):
                        link(V.scalar_tensor_tensor(t1, vT[:, k, tap:tap + S], g("conv_w", KD * tap + k), t1,
                                                    ALU.mult, ALU.add))
                    dve.wait_ge(sem("conv_b_turned"), 2 * half + j + 1)
                    V.tensor_tensor(M["conv_y"][:, k % 4, :], t1, bank[6 + j][:, (k % 2) * S:(k % 2 + 1) * S],
                                    ALU.mult).then_inc(sem("conv_y_done"), 1)
                    dve.wait_ge(sem("conv_y_done"), k + 1)
                dve.wait_ge(sem("conv_y_high"), half + 1)
                part = slice(4 * half, 4 * half + 4)
                V.tensor_tensor(M["yT_lo"][:, part, :], M["conv_y"][:, :, :], M["yT_hi"][:, part, :].bitcast(F32),
                                ALU.subtract).then_inc(sem("conv_y_low"), 1)

            conv_v(0)
            w1.ahead(8)
            conv_taps(0)
            conv_v(1)
            w1.ahead(11)
            conv_taps(1)
            residual("conv", w1, start_of["conv_out"] + 3)

            if "ffn1" in parts:
                ffn("ffn1", w1)

            if "mla" in parts:
                dn, q, kv, tmp, rp = M["dn"], M["q"], M["kv"], M["tmp"], M["rope"]
                norm("mla")
                w1.ahead(start_of["mla_down"] + 3)
                n2, cosT, sinT = ROPE // 2, M["rope_cos"], M["rope_sin"]
                dve.wait_ge(sem("rope_tables"), 2)
                for j in range(2):
                    for t in range(T):
                        V.tensor_tensor(cosT[:, j, t, :], cos2[:, t, :, :].rearrange("p a b -> p (a b)"),
                                        rope_g[:, j, :], ALU.mult)
                        V.tensor_tensor(sinT[:, j, t, :n2], nsin[:, t, :], rope_g[:, j, n2:], ALU.mult)
                        ins = V.tensor_tensor(sinT[:, j, t, n2:], sin[:, t, :], rope_g[:, j, :n2], ALU.mult)
                link(ins)
                for b in range(3):
                    dve.wait_ge(sem("mla_c_high"), b + 1)
                    for k in range(2 * b, min(2 * b + 2, KQ + KKV)):
                        gk = g("q_a", k) if k < KQ else g("kv_a", k - KQ)
                        ins = V.scalar_tensor_tensor(M["cT_lo"][:, k, :], bank[4 + b][:, (k % 2) * S:(k % 2 + 1) * S],
                                                     gk, M["cT_hi"][:, k, :].bitcast(F32), ALU.mult, ALU.subtract)
                    ins.then_inc(sem("mla_c_low"), 1)
                inverse("mla_c_root", "mla_c_rinv", 1, M["c_rinv"][:, :], M["c_root"][:, :])
                dve.wait_ge(sem("mla_dn"), 2)
                dn_rope = dn[:, :, Q_RANK + KV_RANK:]
                kr, kt = M["k_rot"], M["k_turned"]
                V.tensor_tensor(kr[:, :, :], dn_rope, cosT[:, 1, :, :], ALU.mult)
                V.tensor_tensor(kt[:, :, :n2], dn_rope[:, :, n2:], sinT[:, 1, :, :n2], ALU.mult)
                link(V.tensor_tensor(kt[:, :, n2:], dn_rope[:, :, :n2], sinT[:, 1, :, n2:], ALU.mult))
                V.tensor_tensor(kr[:, :, :], kr[:, :, :], kt[:, :, :], ALU.add)
                dve.wait_ge(sem("mla_rope_squares"), 1)
                V.tensor_scalar(M["k_bias"][:, :], M["rope_ss"][:, :], 1.0 / QK, EPS, ALU.mult, ALU.add)\
                    .then_inc(sem("mla_k_bias"), 1)
                for c in range(2):
                    for s in range(2):
                        if s == 0:
                            w1.ahead(start_of["mla_ukv"] + c)
                            dve.wait_ge(sem("mla_kv_first"), c + 1)
                        else:
                            used(w1, start_of["mla_ukv"] + c)
                        for t in range(T):
                            ins = V.tensor_scalar(kv[:, t, c * D + s * HALF:c * D + (s + 1) * HALF],
                                                  bank[2 * s + t][:, :], M["c_rinv"][:, 2 + t:3 + t], None, ALU.mult)
                        ins.then_inc(sem("mla_kv_done"), 1)
                w1.ahead(start_of["mla_uq"])

                def rotate_queries(pair):
                    dve.wait_ge(sem("mla_q_done"), pair + 1)
                    heads_ = slice(2 * pair, 2 * pair + 2)
                    turned_ = tmp[:, pair % 2 * S:(pair % 2 + 1) * S].rearrange("p (t h d) -> p t h d", t=T, h=2)
                    for t in range(T):
                        qr = q[:, t, :].rearrange("p (h d) -> p h d", h=HEADS)[:, heads_, NOPE:]

                        def over_heads(v):
                            return v.unsqueeze(1).broadcast_to([P, 2, v.shape[-1]])
                        V.tensor_tensor(turned_[:, t, :, :n2], qr[:, :, n2:], over_heads(sinT[:, 0, t, :n2]), ALU.mult)
                        V.tensor_tensor(turned_[:, t, :, n2:], qr[:, :, :n2], over_heads(sinT[:, 0, t, n2:]), ALU.mult)
                        ins = V.tensor_tensor(rp[:, t, heads_, :], qr, over_heads(cosT[:, 0, t, :]), ALU.mult)
                    link(ins)
                    return V.tensor_tensor(rp[:, :, heads_, :], rp[:, :, heads_, :], turned_, ALU.add)

                def scale_keys(t):
                    rk = M["qk_rinv"][:, t, HEADS:]
                    kh = kv[:, t, :].rearrange("p (h d) -> p h d", h=HEADS)
                    V.tensor_tensor(kh[:, :, :NOPE], kh[:, :, :NOPE], per_feature(rk, NOPE), ALU.mult)
                    V.tensor_tensor(rp[:, t, HEADS:, :], kr[:, t, :].unsqueeze(1).broadcast_to([P, HEADS, ROPE]),
                                    per_feature(rk, ROPE), ALU.mult)

                inverse("mla_qk_root", "mla_qk_rinv", 1, M["qk_rinv"][:, :, HEADS:], M["qk_root"][:, :, HEADS:])
                for t in range(T):
                    rotate_queries(t)
                    scale_keys(t)
                rotate_queries(2)
                rotate_queries(3)
                V.memset(M["mla_st"][:, :, :, :], 0.0).then_inc(sem("mla_heads_ready"), 1)
                inverse("mla_qk_root", "mla_qk_rinv", 2, M["qk_rinv"][:, :, :HEADS], M["qk_root"][:, :, :HEADS])

                def turn(h):
                    dve.wait_ge(sem("mla_rope_turned"), h + 1)
                    if h >= 2:
                        dve.wait_ge(sem("scores_in_psum"), before("mla", "scores_in_psum") + h - 1)
                    V.tensor_copy(M["ropeT"][:, h % 2, :], bank[5][:ROPE, :]).then_inc(sem("mla_ropeT"), 1)

                def add_mask(h, s_):
                    for t, (a, b) in enumerate(((0, P), (P, 3 * P))):
                        ins = V.scalar_tensor_tensor(s_[:, a:b], bank[6][:, a:b], M["qk_rinv"][:, t, h:h + 1],
                                                     mask[:, a:b], ALU.mult, ALU.add)
                    link(ins)

                def split_out(h):
                    w1.ahead(start_of["mla_o"] + h // 2 - AHEAD)

                attention("mla", HEADS, [(0, P), (P, 3 * P)], QK ** -0.5, turn, add_mask,
                          lambda h, o: (o[:, h, :], bank[h % 2][:, :S]), split_out)
                residual("mla", w1, start_of["mla_o"] + 3)

            if "moe" in parts:
                rt, rc, slot_of, gate_of = M["rt"], M["rc"], M["slot_of"], M["gate_of"]
                dve.wait_ge(sem("router_high"), 1)
                V.tensor_tensor(router_lo[:, :, :], router[:, :, :], router_hi[:, :, :].bitcast(F32), ALU.subtract)\
                    .then_inc(sem("router_low"), 1)
                norm("moe")
                dve.wait_ge(sem("moe_product"), 1)
                V.tensor_copy(M["logitsT"][:, :], bank[0][:E, :S]).then_inc(sem("moe_product_copied"), 1)

                def normed(t):
                    V.scalar_tensor_tensor(M["h"][:, t, :], x[:, t, :], rinv[:, t:t + 1], M["moe_g"][:, :],
                                           ALU.mult, ALU.mult).then_inc(sem("moe_h"), 1)

                w1.ahead(MOE0 - 1)
                dve.wait_ge(sem("moe_logits"), 1)
                L = [rt[:, j, :, :] for j in range(20)]
                R = [rc[:, j, :] for j in range(8)]

                def wide_(c):
                    return per_feature(c, E)

                for t in range(T):
                    ins = V.tensor_scalar(L[0][:, t, :], bank[0][:, S + t * E:S + (t + 1) * E], rinv[:, t:t + 1], None,
                                          ALU.mult)
                link(ins)
                link(V.tensor_reduce(R[2], L[0], AX.X, ALU.max))
                V.tensor_scalar(R[0], R[2], -1.0, None, ALU.mult).then_inc(sem("moe_logits_ready"), 1)
                dve.wait_ge(sem("loaded_moe_g"), 16)
                normed(0)
                dve.wait_ge(sem("moe_exp"), 1)
                link(V.reciprocal(R[3], R[1]))
                link(V.tensor_tensor(L[2], L[1], wide_(R[3]), ALU.mult))
                ties = const[:, C_TIE:C_TIE + E].unsqueeze(1).broadcast_to([P, T, E])
                p_at = L[2]
                for n, (best, hot) in enumerate(((R[4], L[5]), (R[5], L[9]))):
                    link(V.tensor_reduce(best, p_at, AX.X, ALU.max))
                    link(V.tensor_tensor(L[3], p_at, wide_(best), ALU.is_equal))
                    link(V.tensor_tensor(L[4], L[3], ties, ALU.mult))
                    link(V.tensor_reduce(R[6], L[4], AX.X, ALU.max))
                    link(V.tensor_tensor(hot, L[4], wide_(R[6]), ALU.is_equal))
                    if n == 0:
                        link(V.scalar_tensor_tensor(L[6], L[5], -2.0, L[2], ALU.mult, ALU.add))
                        p_at = L[6]
                link(V.tensor_tensor(L[7], L[5], L[9], ALU.add))
                V.tensor_copy(L[8], L[7]).then_inc(sem("moe_chosen"), 1)
                link(V.tensor_tensor(R[7], R[4], R[5], ALU.add))
                link(V.reciprocal(R[6], R[7]))
                link(V.tensor_tensor(L[10], L[7], L[2], ALU.mult))
                V.memset(gate_of[:, :, 2 * E:], 0.0).then_inc(sem("moe_act_done"), 1)
                for n in range(2):
                    link(V.tensor_tensor(gate_of[:, :, n * E:(n + 1) * E], L[10], wide_(R[6]), ALU.mult))
                normed(1)
                dve.wait_ge(sem("moe_placed"), 1)
                place = bank[1][:, :3 * E]
                link(V.tensor_scalar(L[11], place[:, :T * E].rearrange("p (t e) -> p t e", t=T), 1.0, None, ALU.add))
                link(V.tensor_tensor(L[12], L[11], L[7], ALU.mult))
                V.memset(slot_of[:, :, 2 * E:], -1.0)
                V.tensor_scalar(slot_of[:, :, :E], L[12], -1.0, None, ALU.add)
                link(V.tensor_scalar(slot_of[:, :, E:2 * E], L[12], -1.0 - P, None, ALU.add))
                link(V.tensor_reduce(M["most"][:, 0:1], place[:, T * E:], AX.X, ALU.max))
                V.tensor_scalar(overflow[:, :], M["most"][0:1, 0:1], float(P) + 0.5, None, ALU.is_gt)\
                    .then_inc(sem("overflow_known"), 1)

                def pick(e):
                    for t in range(T):
                        ins = V.tensor_scalar(M["pick"][:, t, :], iota, slot_of[:, t, bass.ds(e, 1)], None,
                                              ALU.is_equal)
                    ins.then_inc(sem("moe_pick"), 1)

                def job_left(job, e):
                    dve.wait_ge(sem("moe_job"), PROLOGUE_JOBS + job + 1 + JOBS * e)
                    return bank[6 + job % 2]

                def job_low(job, n_high, e, lo, hi):
                    src = bank[6 + job % 2]
                    dve.wait_ge(sem("moe_job_high"), 2 + n_high + 1 + 6 * e)
                    V.tensor_tensor(lo.rearrange("p k s -> p (k s)"), src[:, :],
                                    hi.bitcast(F32).rearrange("p k s -> p (k s)"), ALU.subtract)\
                        .then_inc(sem("moe_drained"), 1)

                def gather_low(job, n_high, e, half):
                    part = slice(4 * half, 4 * half + 4)
                    job_low(job, n_high, e, M["gT_lo"][:, part, :], M["gT_hi"][:, part, :])

                def turn_low(group, n_high, e):
                    part = slice(4 * group, 4 * group + 4)
                    job_low(JOB_TURN[group], n_high, e, M["eT_lo"][:, part, :], M["eT_hi"][:, part, :])

                def scatter_add(job, e, t, half, done):
                    xs = x[:, t, half * HALF:(half + 1) * HALF]
                    V.tensor_tensor(xs, xs, job_left(job, e)[:, :], ALU.add).then_inc(sem(done), 1)

                def gate_copy(job, e):
                    V.tensor_copy(M["gslot"][:, :], job_left(job, e)[:, 0:1]).then_inc(sem("moe_drained"), 1)

                def put_copy(job, e):
                    V.tensor_copy(M["put"][:, :], job_left(job, e)[:, :S]).then_inc(sem("moe_drained"), 1)

                def expert_act(e, group):
                    dve.wait_ge(W1.used, MOE0 + 4 * group + 4 + EXPERT_CHUNKS * e)
                    dve.wait_ge(sem("moe_silu_done"), 1 + group + EG * e)
                    if group:
                        dve.wait_ge(sem("moe_job"), PROLOGUE_JOBS + JOB_TURN[group - 1] + 1 + JOBS * e)
                    else:
                        dve.wait_ge(sem("moe_job"), PROLOGUE_JOBS + JOBS * e)
                    V.scalar_tensor_tensor(M["e_act"][:, :], bank[2 * (group % 2) + 1][:, :], M["gslot"][:, :],
                                           M["e_silu"][:, :], ALU.mult, ALU.mult).then_inc(sem("moe_act_done"), 1)

                def expert(e, more):
                    for c in range(EXPERT_CHUNKS):
                        if c + AHEAD < EXPERT_CHUNKS or more:
                            split_low(MOE0 + c + AHEAD, e, W1)
                        if c == 3:
                            expert_act(e, 0)
                            scatter_add(0, e, 0, 0, "moe_drained")
                            scatter_add(1, e, 0, 1, "moe_drained")
                        if c == 5:
                            turn_low(0, 0, e)
                        if c == 7:
                            expert_act(e, 1)
                            scatter_add(3, e, 1, 0, "moe_drained")
                            scatter_add(4, e, 1, 1, "moe_drained")
                        if c == 9:
                            turn_low(1, 1, e)
                        if c == 11:
                            expert_act(e, 2)
                            put_copy(JOB_PUT, e)
                            pick(e + 1)
                        if c == 13:
                            turn_low(2, 2, e)
                        if c == 15:
                            expert_act(e, 3)
                            gather_low(8, 3, e, 0)
                            gather_low(9, 4, e, 1)
                            gate_copy(JOB_GATE, e)
                        if c == 16:
                            turn_low(3, 5, e)

                w1.ahead(MOE0)
                pick(0)
                gather_low(-4, -2, 0, 0)
                gather_low(-3, -1, 0, 1)
                gate_copy(-2, 0)
                put_copy(-1, 0)
                with dve.Fori(0, E - 1) as e:
                    expert(e, True)
                expert(E - 1, False)
                dve.wait_ge(sem("overflow_known"), 1)
                over = dve.value_load(overflow[0:1, 0:1], min_val=0, max_val=1)
                with dve.If(over > 0):
                    for c in range(AHEAD):
                        split_low(MOE0 + c, E, W1)
                    with dve.Fori(E, 2 * E - 1) as e:
                        expert(e, True)
                    expert(2 * E - 1, False)
                for n, (t, half) in enumerate(((0, 0), (1, 0), (0, 1), (1, 1))):
                    dve.wait_ge(sem("moe_last_scatter"), n + 1)
                    xs = x[:, t, half * HALF:(half + 1) * HALF]
                    V.tensor_tensor(xs, xs, bank[4 + n][:, :], ALU.add).then_inc(sem("x_updated"), 1)
                dve.wait_ge(sem("x_updated"), before("moe", "x_updated") + 4)

            if "fox" in parts:
                z, cs = M["z"], M["cs"]
                w2.ahead(0)
                norm("fox")
                dve.wait_ge(sem("forget_high"), 1)
                V.tensor_tensor(forget_lo[:, :, :], forget_w[:, :, :], forget_hi[:, :, :].bitcast(F32), ALU.subtract)\
                    .then_inc(sem("forget_low"), 1)
                w2.ahead(1)
                norm_low("memkv", "g_mem_kv", M["memT_lo"], M["memT_hi"])
                inverse("root", "rinv", before("memkv", "rinv") + 1, M["m_rinv"][:, :], M["m_root"][:, :])
                dve.wait_ge(sem("forget_product"), 1)
                V.tensor_copy(M["cT"][:, :], bank[7][:FOX_HEADS, :S]).then_inc(sem("forget_cT"), 1)
                w2.ahead(3)
                for t in range(T):
                    dve.wait_ge(sem("fox_head_squares"), t + 1)
                    V.tensor_reduce(M["f_ss"][:, t, :],
                                    M["fox_tmp"][:, t * 2 * FOX:(t + 1) * 2 * FOX].rearrange("p (h d) -> p h d", h=2 * FOX_HEADS),
                                    AX.X, ALU.add).then_inc(sem("fox_sums"), 1)
                dve.wait_ge(sem("forget_logits"), 1)
                for t in range(T):
                    ins = V.scalar_tensor_tensor(cs[:, 0, t, :], bank[7][:, S + t * FOX_HEADS:S + (t + 1) * FOX_HEADS],
                                                 rinv[:, t:t + 1], forget_b[:, :], ALU.mult, ALU.add)
                link(ins)
                link(V.tensor_scalar(cs[:, 4, :, :], cs[:, 0, :, :], -1.0, None, ALU.mult))
                V.tensor_tensor(cs[:, 1, :, :], cs[:, 0, :, :], cs[:, 4, :, :], ALU.min).then_inc(sem("forget_abs"), 1)
                inverse("fox_qk_root", "fox_qk_rinv", 1, M["f_rinv"][:, :, :], M["f_root"][:, :, :])
                for t in range(T):
                    zh = z[:, t, :2 * FOX].rearrange("p (h d) -> p h d", h=2 * FOX_HEADS)
                    ins = V.tensor_tensor(zh, zh, per_feature(M["f_rinv"][:, t, :], FOX_DIM), ALU.mult)
                    ins.then_inc(sem("fox_heads_ready"), 1)
                dve.wait_ge(sem("forget_ln"), 1)
                V.scalar_tensor_tensor(cs[:, 5, :, :], cs[:, 0, :, :], 0.0, cs[:, 3, :, :], ALU.min, ALU.subtract)\
                    .then_inc(sem("forget_log"), 1)
                def fox_group(j):
                    used(w2, 2 * j + 1)
                    for t in range(T):
                        ins = V.tensor_scalar(z[:, t, j * HALF:(j + 1) * HALF], bank[2 * (j % 2) + t][:, :],
                                              rinv[:, t:t + 1], None, ALU.mult)
                    ins.then_inc(sem("fox_vp_done"), 1)

                fox_group(2)
                dve.wait_ge(sem("forget_sum"), 1)
                summed = bank[7][:, :T * FOX_HEADS].rearrange("p (t h) -> p t h", t=T)
                V.tensor_copy(cs[:, 0, :, :], summed)
                V.tensor_scalar(cs[:, 4, :, :], summed, FOX_DIM ** 0.5, None, ALU.mult).then_inc(sem("forget_sum_copied"), 1)
                dve.wait_ge(sem("forget_sum_turned"), 1)
                V.tensor_copy(M["cT"][:, :], bank[7][:FOX_HEADS, :S]).then_inc(sem("forget_cT"), 1)
                fox_group(3)

                def beside(h):
                    if 1 <= h <= len(WINDOWS):
                        dve.wait_ge(sem("pool_high"), h)
                        V.scalar_tensor_tensor(xT_lo[:, KD // 2 + h - 1, :], bank[5][:, :S], g("pool_scale", h - 1),
                                               xT_hi[:, KD // 2 + h - 1, :].bitcast(F32), ALU.mult, ALU.subtract)\
                            .then_inc(sem("pool_low"), 1)
                    if h in SPLIT_BESIDE:
                        w2.ahead(start_of["mem_kv"] + SPLIT_BESIDE.index(h))

                def add_forget(h, s_):
                    for t, (a, b) in enumerate(((0, P), (P, 3 * P))):
                        ins = V.scalar_tensor_tensor(s_[:, a:b], bank[6][:, a:b], cs[:, 4, t, h:h + 1], mask[:, a:b],
                                                     ALU.add, ALU.add)
                    link(ins)

                def fox_value(h, o):
                    rows_ = slice(FOX_DIM * (h % 2), FOX_DIM * (h % 2 + 1))
                    return o[rows_, h // 2, :], bank[h // 2 % 2][rows_, :S]

                attention("fox", FOX_HEADS, [(0, P), (P, 3 * P)], FOX_DIM ** -0.5, lambda h: None, add_forget,
                          fox_value, beside)
                w2.ahead(start_of["fox_out"])
                mkv = M["mkv"]
                dve.wait_ge(W2.used, start_of["mem_kv"] + 4)
                for t in range(T):
                    ins = V.tensor_scalar(mkv[:, t, MEM:], bank[4 + t][:, :], M["m_rinv"][:, t:t + 1], None, ALU.mult)
                ins.then_inc(sem("mem_v_done"), 1)

                def memory_sums(j):
                    dve.wait_ge(sem("mem_head_squares"), j + 1)
                    V.tensor_reduce(M["mh_ss"][:, j, :, :].rearrange("p t h -> p (t h)"),
                                    M["mem_tmp"][:, :T * MEM].rearrange("p (h d) -> p h d", d=MEM_DIM),
                                    AX.X, ALU.add).then_inc(sem("mem_sums"), 1)
                    inverse("mem_qk_root", "mem_qk_rinv", j + 1, M["mh_rinv"][:, j, :, :], M["mh_root"][:, j, :, :])

                memory_sums(0)
                for t in range(T):
                    v = mkv[:, t, :MEM].rearrange("p (h d) -> p h d", h=MEM_HEADS)
                    ins = V.tensor_tensor(v, v, per_feature(M["mh_rinv"][:, 0, t, :], MEM_DIM), ALU.mult)
                ins.then_inc(sem("mem_keys_ready"), 1)
                residual("fox", w2, start_of["fox_out"] + 3)

            if "mem" in parts:
                norm("mem")
                w2.ahead(start_of["mem_q"] + 1)
                memory_sums(1)

                def scale_scores(h, s_):
                    for t in range(T):
                        ins = V.tensor_scalar(s_[:, t * S:(t + 1) * S], bank[6][:, t * S:(t + 1) * S],
                                              M["mh_rinv"][:, 1, t, h:h + 1], None, ALU.mult)
                    link(ins)

                attention("mem", MEM_HEADS, [(0, S), (S, 2 * S)], MEM_DIM ** -0.5, lambda h: None, scale_scores,
                          lambda h, o: (o[:, h, :], bank[h % 2][:, :S]))
                residual("mem", w2, start_of["mem_out"] + 1)

            if "ffn2" in parts:
                ffn("ffn2", w2)

        @block.tensor
        def _(pe):
            mm, turn_ = nc.tensor.matmul, nc.tensor.transpose

            def weights(w, i, e, hold=False):
                pe.wait_ge(w.low, i + 1 + EXPERT_CHUNKS * e)
                slot = i % RING
                return w_hi[:, slot, :], w_lo[:, slot, :]

            def three(dst, a_hi, a_lo, b_hi, b_lo, start, stop):
                mm(dst, a_hi, b_hi, start=start, stop=False)
                mm(dst, a_hi, b_lo, start=False, stop=False)
                return mm(dst, a_lo, b_hi, start=False, stop=stop)

            def tall(w, i, e, xh, xl, k0, kn, n, banks, start, stop, tokens=T, turned_for=None):
                wh, wl = weights(w, i, e)
                for k in range(kn):
                    if turned_for and k % 2 == 0:
                        pe.wait_ge(sem("xT_low"), before(turned_for, "xT_low") + (k0 + k) // 2 + 1)
                    for t in range(tokens):
                        tok = slice(t * P, (t + 1) * P)
                        ins = three(bank[banks[t]][:, :n], xh[:, k0 + k, tok], xl[:, k0 + k, tok],
                                    wh[:, k * n:(k + 1) * n], wl[:, k * n:(k + 1) * n],
                                    start and k == 0, stop and k == kn - 1)
                ins.then_inc(w.used, 1)

            def wide(w, i, e, xh, xl, k0, banks, start, stop, tokens=T, halves_signal=None):
                wh, wl = weights(w, i, e)
                for half in range(2):
                    for k in range(2):
                        for t in range(tokens):
                            tok = slice(t * P, (t + 1) * P)
                            cols = slice(k * D + half * HALF, k * D + (half + 1) * HALF)
                            ins = three(bank[banks[2 * t + half]][:, :], xh[:, k0 + k, tok], xl[:, k0 + k, tok],
                                        wh[:, cols], wl[:, cols], start and k == 0, stop and k == 1)
                    if halves_signal and half == 0:
                        ins.then_inc(sem(halves_signal), 1)
                ins.then_inc(w.used, 1)

            def group(w, i, xh, xl, n, banks, turned_for=None, between=None):
                step = CHUNK // n if CHUNK // n < KD else KD
                for j in range(KD // step):
                    tall(w, i + j, 0, xh, xl, j * step, step, n, banks, j == 0, (j + 1) * step == KD,
                         turned_for=turned_for)
                    if between and j == 0:
                        between()

            def wide_all(w, name, xh, xl, kn, ready):
                for c in range(kn // 2):
                    ready(c)
                    last_one = c == kn // 2 - 1
                    wide(w, start_of[name] + c, 0, xh, xl, 2 * c, (0, 1, 2, 3), c == 0, last_one,
                         halves_signal="left_half_summed" if last_one else None)

            def norm(p, src, ready):
                for b in range(4):
                    if b in (0, 2):
                        pe.wait_ge(sem(ready[0]), ready[1 + b // 2])
                    for k in (2 * b, 2 * b + 1):
                        for t in range(T):
                            at_ = ((k % 2) * T + t) * P
                            ins = turn_(bank[4 + b][:, at_:at_ + P], src[:, t, k * P:(k + 1) * P], ident)
                    ins.then_inc(sem("xT_turned"), 1)

            def ffn(p, w):
                norm(p, x, x_ready[p])
                i, turned = start_of[p + "_up"], 0

                def turn_group(gr):
                    nonlocal turned
                    pe.wait_ge(sem("act_done"), before(p, "act_done") + gr + 1)
                    n = FF_GROUPS[gr][1]
                    for j in range(n // S):
                        if gr >= 2:
                            pe.wait_ge(sem("act_low"), before(p, "act_low") + 2 * (gr - 2) + j + 1)
                        for k in range(2):
                            for t in range(T):
                                c0 = (2 * j + k) * P
                                ins = turn_(bank[4 + 2 * (gr % 2) + j][:, (k * T + t) * P:(k * T + t + 1) * P],
                                            M[p + "_act"][:, t, c0:c0 + P], ident)
                        ins.then_inc(sem("act_turned"), 1)
                        turned += 1

                for gr, (_, n) in enumerate(FF_GROUPS):
                    parts_of = KD // (CHUNK // n) if CHUNK // n < KD else 1
                    if gr:
                        pe.wait_ge(sem("silu_done"), before(p, "silu_done") + gr)
                    group(w, i, xT_hi, xT_lo, n, (0, 1), p)
                    if gr:
                        turn_group(gr - 1)
                        pe.wait_ge(sem("act_done"), before(p, "act_done") + gr)
                    group(w, i + parts_of, xT_hi, xT_lo, n, (2, 3))
                    i += 2 * parts_of
                turn_group(len(FF_GROUPS) - 1)
                wide_all(w, p + "_down", M[p + "_hi"], M[p + "_lo"], KF,
                         lambda c: pe.wait_ge(sem("act_low"), before(p, "act_low") + c + 1))

            def attention(p, n_heads, blocks, turn, score, value, filler=None):
                def probabilities(h):
                    pe.wait_ge(sem("probs_ready"), before(p, "probs_ready") + h + 1)
                    if h:
                        pe.wait_ge(sem("pT"), before(p, "pT") + h)
                    for at_, (a, b) in enumerate(blocks):
                        ins = turn_(bank[7][:, at_ * P:(at_ + 1) * P], M[p + "_p"][:, h % 2, a:b], ident)
                    ins.then_inc(sem("pT_turned"), 1)

                def scores(h):
                    if h:
                        pe.wait_ge(sem("scores_ready"), before(p, "scores_ready") + h)
                    score(h)

                def values(h):
                    pe.wait_ge(sem("pT"), before(p, "pT") + h + 1)
                    value(h)

                def filled(h):
                    if filler:
                        filler(h)

                for i in range(-2, n_heads + 1):
                    for stage, h in ((turn, i + 2), (scores, i + 1), (filled, i), (values, i - 1), (probabilities, i)):
                        if 0 <= h < n_heads:
                            stage(h)

            pe.wait_ge(sem("loaded_const"), 16)
            pe.wait_ge(sem("loaded_gains"), 16 * N_GAIN_LOADS)
            turn_(bank[0][:, :N_GAINS], M["gain_rows"][:N_GAINS, :], ident[:N_GAINS, :N_GAINS])\
                .then_inc(sem("gains_turned"), 1)

            def turn_half(buf, first_bank, name):
                for j in range(2):
                    for k in range(2):
                        for t in range(T):
                            c0 = (2 * j + k) * P
                            ins = turn_(bank[first_bank + j][:, (k * T + t) * P:(k * T + t + 1) * P],
                                        buf[:, t, c0:c0 + P], ident)
                    ins.then_inc(sem(name), 1)

            norm("conv", x, x_ready["conv"])
            pe.wait_ge(sem("gains_ready"), 1)
            bank_free = [None, None, ("conv_c_done", 1), ("conv_v_done", 1), ("conv_b_done", 1), ("conv_c_done", 2)]
            for q_ in range(6):
                if bank_free[q_]:
                    pe.wait_ge(sem(bank_free[q_][0]), bank_free[q_][1])
                pair = (2 * (q_ % 2), 2 * (q_ % 2) + 1)
                group(W1, 2 * q_, xT_hi, xT_lo, HALF, pair, "conv" if q_ == 0 else None)
                if q_ == 2:
                    pe.wait_ge(sem("conv_v_done"), 1)
                    turn_half(M["conv_v"], 4, "conv_v_turned")
                if q_ == 3:
                    pe.wait_ge(sem("conv_b_done"), 1)
                    turn_half(M["conv_b"], 6, "conv_b_turned")
            pe.wait_ge(sem("conv_v_done"), 2)
            pe.wait_ge(sem("conv_vT"), 2)
            turn_half(M["conv_v"], 4, "conv_v_turned")
            pe.wait_ge(sem("conv_b_done"), 2)
            pe.wait_ge(sem("conv_y_done"), 4)
            turn_half(M["conv_b"], 6, "conv_b_turned")
            wide_all(W1, "conv_out", M["yT_hi"], M["yT_lo"], KD,
                     lambda c: pe.wait_ge(sem("conv_y_low"), c // 2 + 1))

            if "ffn1" in parts:
                ffn("ffn1", W1)

            if "mla" in parts:
                dn, q, kv = M["dn"], M["q"], M["kv"]
                norm("mla", x, x_ready["mla"])
                n = DOWN_COLS // 2
                for j in range(2):
                    for c in range(2):
                        tall(W1, start_of["mla_down"] + 2 * j + c, 0, xT_hi, xT_lo, 4 * c, 4, n, (2 * j, 2 * j + 1),
                             c == 0, c == 1, turned_for="mla")
                pe.wait_ge(sem("mla_dn"), 2)
                for b in range(3):
                    for k in range(2 * b, min(2 * b + 2, KQ + KKV)):
                        for t in range(T):
                            ins = turn_(bank[4 + b][:, ((k % 2) * T + t) * P:((k % 2) * T + t + 1) * P],
                                        dn[:, t, k * P:(k + 1) * P], ident)
                    ins.then_inc(sem("mla_c_turned"), 1)
                cth, ctl = M["cT_hi"], M["cT_lo"]
                pe.wait_ge(sem("mla_c_low"), 3)
                for c in range(2):
                    wh, wl = weights(W1, start_of["mla_ukv"] + c, 0)
                    for s in range(2):
                        if c:
                            pe.wait_ge(sem("mla_kv_done"), s + 1)
                        for k in range(KKV):
                            cols = slice(k * D + s * HALF, k * D + (s + 1) * HALF)
                            for t in range(T):
                                tok = slice(t * P, (t + 1) * P)
                                ins = three(bank[2 * s + t][:, :], cth[:, KQ + k, tok], ctl[:, KQ + k, tok],
                                            wh[:, cols], wl[:, cols], k == 0, k == KKV - 1)
                        ins.then_inc(W1.used if s else sem("mla_kv_first"), 1)
                free = [("mla_kv_done", 3), ("mla_kv_done", 4), ("mla_q_done", 1), ("mla_q_done", 2)]
                for j in range(UQ_GROUPS):
                    pe.wait_ge(sem(free[j][0]), free[j][1])
                    tall(W1, start_of["mla_uq"] + j, 0, cth, ctl, 0, KQ, 2 * QK, (2 * (j % 2), 2 * (j % 2) + 1), True, True)
                pe.wait_ge(sem("mla_heads_ready"), 1)

                def turn(h):
                    if h:
                        pe.wait_ge(sem("mla_qkT"), h)
                    for j, (src, c0) in enumerate(((q, h * QK), (kv, h * 2 * P))):
                        for t in range(T):
                            ins = turn_(bank[4][:, (j * T + t) * P:(j * T + t + 1) * P], src[:, t, c0:c0 + P], ident)
                    ins.then_inc(sem("mla_nope_turned"), 1)
                    if h:
                        pe.wait_ge(sem("mla_ropeT"), h)
                    for j in range(2):
                        for t in range(T):
                            ins = turn_(bank[5][:ROPE, (j * T + t) * P:(j * T + t + 1) * P],
                                        M["rope"][:, t, j * HEADS + h, :], ident)
                    ins.then_inc(sem("mla_rope_turned"), 1)

                def score(h):
                    pe.wait_ge(sem("mla_qkT"), h + 1)
                    pe.wait_ge(sem("mla_ropeT"), h + 1)
                    qk, ro = M["qkT"][:, h % 2, :], M["ropeT"][:, h % 2, :]
                    for t, (a, keys) in enumerate(((0, P), (P, S))):
                        tok = slice(t * P, (t + 1) * P)
                        mm(bank[6][:, a:a + keys], qk[:, tok], qk[:, S:S + keys], start=True, stop=False)
                        ins = mm(bank[6][:, a:a + keys], ro[:, tok], ro[:, S:S + keys], start=False, stop=True)
                    ins.then_inc(sem("scores_in_psum"), 1)

                def value(h):
                    if h >= 2:
                        pe.wait_ge(sem("value_low"), before("mla", "value_low") + h - 1)
                    v = kv[:, :, h * 2 * P + P:(h + 1) * 2 * P]
                    pT = M["mla_pT"][:, h % 2, :]
                    mm(bank[h % 2][:, :S], v[:, 0, :], pT[:, :S], start=True, stop=False)
                    mm(bank[h % 2][:, P:S], v[:, 1, :], pT[:, S:], start=False, stop=True).then_inc(sem("values_in_psum"), 1)

                CAUSAL = [(0, P), (P, 2 * P), (2 * P, 3 * P)]
                attention("mla", HEADS, CAUSAL, turn, score, value)
                wide_all(W1, "mla_o", xT_hi, xT_lo, KD, lambda c: pe.wait_ge(sem("value_low"), before("mla", "value_low") + HEADS))

            if "moe" in parts:
                norm("moe", x, x_ready["moe"])
                pe.wait_ge(sem("router_low"), 1)
                for k in range(KD):
                    pe.wait_ge(sem("xT_low"), before("moe", "xT_low") + k // 2 + 1)
                    ins = three(bank[0][:E, :S], router_hi[:, k, :], router_lo[:, k, :], xT_hi[:, k, :], xT_lo[:, k, :],
                                k == 0, k == KD - 1)
                ins.then_inc(sem("moe_product"), 1)
                pe.wait_ge(sem("moe_product_copied"), 1)
                for t in range(T):
                    ins = turn_(bank[0][:, S + t * E:S + (t + 1) * E], M["logitsT"][:, t * P:(t + 1) * P], ident[:E, :E])
                ins.then_inc(sem("moe_logits"), 1)
                pe.wait_ge(sem("moe_chosen"), 1)
                chosen = M["rt"][:, 8, :, :]
                mm(bank[1][:, 0:E], earlier, chosen[:, 0, :], start=True, stop=True)
                mm(bank[1][:, E:2 * E], ones, chosen[:, 0, :], start=True, stop=False)
                mm(bank[1][:, E:2 * E], earlier, chosen[:, 1, :], start=False, stop=True)
                mm(bank[1][:, 2 * E:3 * E], ones, chosen[:, 0, :], start=True, stop=False)
                mm(bank[1][:, 2 * E:3 * E], ones, chosen[:, 1, :], start=False, stop=True).then_inc(sem("moe_placed"), 1)
                pick_, put = M["pick"], M["put"]

                def job_bank(job, e):
                    if job >= 0:
                        pe.wait_ge(sem("moe_drained"), PROLOGUE_JOBS + job - 1 + JOBS * e)
                    elif job >= -2:
                        pe.wait_ge(sem("moe_drained"), PROLOGUE_JOBS + job - 1)
                    return bank[6 + job % 2]

                def gather(job, e, half):
                    b = job_bank(job, e)
                    for k in range(4):
                        feat = slice((4 * half + k) * P, (4 * half + k + 1) * P)
                        for t in range(T):
                            ins = mm(b[:, k * P:(k + 1) * P], M["h"][:, t, feat], pick_[:, t, :],
                                     start=(t == 0), stop=(t == T - 1))
                    ins.then_inc(sem("moe_job"), 1)

                def gates(job, e, e_next):
                    b = job_bank(job, e)
                    for t in range(T):
                        ins = mm(b[:, 0:1], pick_[:, t, :], M["gate_of"][:, t, bass.ds(e_next, 1)],
                                 start=(t == 0), stop=(t == T - 1))
                    ins.then_inc(sem("moe_job"), 1)

                def turn_pick(job, e):
                    b = job_bank(job, e)
                    for t in range(T):
                        ins = turn_(b[:, t * P:(t + 1) * P], pick_[:, t, :], ident)
                    ins.then_inc(sem("moe_job"), 1)

                def turn_act(job, e, gr):
                    pe.wait_ge(sem("moe_act_done"), gr + 2 + EG * e)
                    b = job_bank(job, e)
                    for k in range(4):
                        ins = turn_(b[:, k * P:(k + 1) * P], M["e_act"][:, k * P:(k + 1) * P], ident)
                    ins.then_inc(sem("moe_job"), 1)

                def scatter_into(b, t, half):
                    return mm(b[:, :], put[:, t * P:(t + 1) * P], M["y"][:, half * HALF:(half + 1) * HALF],
                              start=True, stop=True)

                def scatter(job, e, t, half):
                    scatter_into(job_bank(job, e), t, half).then_inc(sem("moe_job"), 1)

                gth, gtl, eth, etl = M["gT_hi"], M["gT_lo"], M["eT_hi"], M["eT_lo"]

                def expert(e):
                    for c in range(4 * EG):
                        gr, up, half = c // 4, c // 2 % 2, c % 2
                        if c == 0:
                            pe.wait_ge(sem("moe_drained"), PROLOGUE_JOBS - 2 + JOBS * e)
                        if half == 0:
                            pe.wait_ge(sem("moe_act_done"), max(gr, 1) + EG * e)
                        tall(W1, MOE0 + c, e, gth, gtl, 4 * half, 4, HALF, (2 * (gr % 2) + up,), half == 0, half == 1,
                             tokens=1)
                        if c == 3:
                            pe.wait_ge(sem("moe_y"), 1 + e)
                            scatter(0, e, 0, 0)
                            scatter(1, e, 0, 1)
                        if c == 5:
                            turn_act(2, e, 0)
                        if c == 7:
                            scatter(3, e, 1, 0)
                            scatter(4, e, 1, 1)
                        if c == 9:
                            turn_act(5, e, 1)
                        if c == 11:
                            turn_pick(JOB_PUT, e)
                        if c == 13:
                            turn_act(7, e, 2)
                    pe.wait_ge(sem("moe_pick"), 2 + e)
                    gather(8, e, 0)
                    gather(9, e, 1)
                    gates(JOB_GATE, e, e + 1)
                    for c in range(FE // 256):
                        if c == 1:
                            turn_act(11, e, 3)
                        if c == 0:
                            pe.wait_ge(sem("moe_drained"), PROLOGUE_JOBS + 8 + JOBS * e)
                        if c == 6:
                            pe.wait_ge(sem("moe_drained"), PROLOGUE_JOBS + 12 + JOBS * e)
                        wide(W1, MOE0 + 4 * EG + c, e, eth, etl, 2 * c, (4, 5), c == 0, c == FE // 256 - 1, tokens=1)

                pe.wait_ge(sem("moe_h"), T)
                pe.wait_ge(sem("moe_pick"), 1)
                gather(-4, 0, 0)
                gather(-3, 0, 1)
                gates(-2, 0, 0)
                turn_pick(-1, 0)
                with pe.Fori(0, E) as e:
                    expert(e)
                pe.wait_ge(sem("overflow_known"), 1)
                over = pe.value_load(overflow[0:1, 0:1], min_val=0, max_val=1)
                with pe.If(over > 0):
                    with pe.Fori(E, 2 * E) as e:
                        expert(e)
                pe.wait_ge(sem("moe_y"), 1 + E + over * E)
                pe.wait_ge(sem("moe_drained"), PROLOGUE_JOBS + E * JOBS + over * (E * JOBS))
                for n_, (t, half) in enumerate(((0, 0), (1, 0), (0, 1), (1, 1))):
                    scatter_into(bank[4 + n_], t, half).then_inc(sem("moe_last_scatter"), 1)

            if "fox" in parts:
                z, cs = M["z"], M["cs"]
                norm("fox", x, x_ready["fox"])
                free = [None, None, ("fox_qk_done", 1), ("fox_qk_done", 2)]
                def fox_group(j, between=None):
                    if free[j]:
                        pe.wait_ge(sem(free[j][0]), free[j][1])
                    group(W2, 2 * j, xT_hi, xT_lo, HALF, (2 * (j % 2), 2 * (j % 2) + 1), "fox" if j == 0 else None,
                          between)

                fox_group(0)
                norm("memkv", M["mem"], ("loaded_mem", 16, 16))
                def forget_product():
                    pe.wait_ge(sem("xT_low"), before("memkv", "xT_low") + 4)
                    pe.wait_ge(sem("forget_low"), 1)
                    for k in range(KD):
                        ins = three(bank[7][:FOX_HEADS, :S], forget_hi[:, k, :], forget_lo[:, k, :], xT_hi[:, k, :],
                                    xT_lo[:, k, :], k == 0, k == KD - 1)
                    ins.then_inc(sem("forget_product"), 1)

                fox_group(1, forget_product)
                pe.wait_ge(sem("forget_cT"), 1)
                for t in range(T):
                    ins = turn_(bank[7][:, S + t * FOX_HEADS:S + (t + 1) * FOX_HEADS], M["cT"][:, t * P:(t + 1) * P],
                                ident[:FOX_HEADS, :FOX_HEADS])
                ins.then_inc(sem("forget_logits"), 1)
                fox_group(2)
                pe.wait_ge(sem("fox_heads_ready"), 2)
                for k in range(FOX_HEADS // 2):
                    if k >= 2:
                        pe.wait_ge(sem("fox_qkT"), k - 1)
                    for j in range(2):
                        for t in range(T):
                            c0 = j * FOX + k * P
                            ins = turn_(bank[4 + k % 2][:, (j * T + t) * P:(j * T + t + 1) * P], z[:, t, c0:c0 + P], ident)
                    ins.then_inc(sem("fox_pair_turned"), 1)
                pe.wait_ge(sem("forget_log"), 1)
                b = bank[7]
                ls = cs[:, 5, :, :]
                mm(b[:, 0:FOX_HEADS], upto_now, ls[:, 0, :], start=True, stop=True)
                mm(b[:, FOX_HEADS:2 * FOX_HEADS], ones, ls[:, 0, :], start=True, stop=False)
                mm(b[:, FOX_HEADS:2 * FOX_HEADS], upto_now, ls[:, 1, :], start=False, stop=True)\
                    .then_inc(sem("forget_sum"), 1)
                pe.wait_ge(sem("forget_sum_copied"), 1)
                for t in range(T):
                    ins = turn_(b[:FOX_HEADS, t * P:(t + 1) * P], cs[:, 0, t, :], ident)
                ins.then_inc(sem("forget_sum_turned"), 1)
                fox_group(3)
                pe.wait_ge(sem("forget_cT"), 2)

                def memory_product(quarter):
                    c, half, for_v = quarter // 2, quarter % 2, quarter // 4
                    wh, wl = weights(W2, start_of["mem_kv"] + c, 0)
                    if quarter == 4:
                        pe.wait_ge(sem("pool_low"), len(WINDOWS))
                    for k in (2 * half, 2 * half + 1):
                        row = 4 * (c % 2) + k
                        for t in range(T):
                            tok = slice(t * P, (t + 1) * P)
                            ins = three(bank[2 + 2 * for_v + t][:, :], M["memT_hi"][:, row, tok], M["memT_lo"][:, row, tok],
                                        wh[:, k * HALF:(k + 1) * HALF], wl[:, k * HALF:(k + 1) * HALF],
                                        row == 0, row == KD - 1)
                    if half:
                        ins.then_inc(W2.used, 1)

                def beside(h):
                    if h == 0:
                        pe.wait_ge(sem("fox_vp_done"), 2)
                        pe.wait_ge(sem("loaded_pool"), 32)
                        pe.wait_ge(sem("fox_qkT"), FOX_HEADS // 2)
                    if h < len(WINDOWS):
                        if h:
                            pe.wait_ge(sem("pool_mixed_copied"), h)
                        zp = z[:, :, 3 * FOX + h * P:3 * FOX + (h + 1) * P]
                        mm(bank[4][:, :S], zp[:, 0, :], M["bands"][:, h, 0, :], start=True, stop=False)
                        mm(bank[4][:, P:S], zp[:, 1, :], M["bands"][:, h, 1, P:], start=False, stop=True)\
                            .then_inc(sem("pool_mixed"), 1)
                    if 1 <= h <= len(WINDOWS):
                        pe.wait_ge(sem("pool_mixed_copied"), h)
                        if h > 1:
                            pe.wait_ge(sem("pool_low"), h - 1)
                        mm(bank[5][:, :S], M["w_pool"][:, h - 1, :], M["mixed"][:, :], start=True, stop=True)\
                            .then_inc(sem("pool_mapped"), 1)
                    if h != 4:
                        memory_product(h if h < 4 else h - 1)

                def score(h):
                    pe.wait_ge(sem("fox_qkT"), h // 2 + 1)
                    rows_ = slice(FOX_DIM * (h % 2), FOX_DIM * (h % 2 + 1))
                    qT, kT = M["fqT"][rows_, h // 2, :], M["fkT"][rows_, h // 2, :]
                    sel = const[:FOX_HEADS, C_SEL + h * P:C_SEL + (h + 1) * P]
                    for t, (a, keys) in enumerate(((0, P), (P, S))):
                        mm(bank[6][:, a:a + keys], qT[:, t * P:(t + 1) * P], kT[:, :keys], start=True, stop=False)
                        ins = mm(bank[6][:, a:a + keys], sel, M["cT"][:, :keys], start=False, stop=True)
                    ins.then_inc(sem("scores_in_psum"), 1)

                def value(h):
                    if h >= 4:
                        pe.wait_ge(sem("value_low"), before("fox", "value_low") + h - 3)
                    v = z[:, :, 2 * FOX + h * FOX_DIM:2 * FOX + (h + 1) * FOX_DIM]
                    o = bank[h // 2 % 2][FOX_DIM * (h % 2):FOX_DIM * (h % 2 + 1), :]
                    pT = M["fox_pT"][:, h % 2, :]
                    mm(o[:, :S], v[:, 0, :], pT[:, :S], start=True, stop=False)
                    mm(o[:, P:S], v[:, 1, :], pT[:, S:], start=False, stop=True).then_inc(sem("values_in_psum"), 1)

                attention("fox", FOX_HEADS, CAUSAL, lambda h: None, score, value, beside)
                memory_product(7)

                def turn_memory(src, name):
                    for k in range(MEM_HEADS // 2):
                        for h in range(2):
                            for t in range(T):
                                ins = turn_(bank[4 + k][:, (h * T + t) * P:(h * T + t + 1) * P],
                                            src[:, t, (2 * k + h) * P:(2 * k + h + 1) * P], ident)
                        ins.then_inc(sem(name), 1)

                def before_out(c):
                    pe.wait_ge(sem("value_low"), before("fox", "value_low") + FOX_HEADS)
                    if c == 2:
                        pe.wait_ge(sem("mem_v_done"), 1)
                        pe.wait_ge(sem("mem_keys_ready"), 1)
                        turn_memory(M["mkv"], "mem_keys_turned")

                wide_all(W2, "fox_out", xT_hi, xT_lo, KD, before_out)

            if "mem" in parts:
                mkv, mq = M["mkv"], M["mq"]
                pe.wait_ge(sem("mem_kT"), MEM_HEADS // 2)
                norm("mem", x, x_ready["mem"])
                group(W2, start_of["mem_q"], xT_hi, xT_lo, HALF, (0, 1), "mem")
                pe.wait_ge(sem("mem_q_done"), 1)
                turn_memory(mq, "mem_queries_turned")

                def score_m(h):
                    pe.wait_ge(sem("mem_qT"), h // 2 + 1)
                    for t in range(T):
                        ins = mm(bank[6][:, t * S:(t + 1) * S], M["mqT"][:, h, t * P:(t + 1) * P], M["mkT"][:, h, :],
                                 start=True, stop=True)
                    ins.then_inc(sem("scores_in_psum"), 1)

                def value_m(h):
                    if h >= 2:
                        pe.wait_ge(sem("value_low"), before("mem", "value_low") + h - 1)
                    pT = M["mem_pT"][:, h % 2, :]
                    for m in range(T):
                        ins = mm(bank[h % 2][:, :S], mkv[:, m, MEM + h * P:MEM + (h + 1) * P], pT[:, m * S:(m + 1) * S],
                                 start=(m == 0), stop=(m == T - 1))
                    ins.then_inc(sem("values_in_psum"), 1)

                attention("mem", MEM_HEADS, [(0, P), (S, S + P), (P, S), (S + P, 2 * S)], lambda h: None, score_m, value_m)
                wide_all(W2, "mem_out", xT_hi, xT_lo, MEM // P, lambda c: pe.wait_ge(sem("value_low"), before("mem", "value_low") + MEM_HEADS))

            if "ffn2" in parts:
                ffn("ffn2", W2)


N_GAIN_LOADS = len(GAINS) + 2


def layout(inputs):
    const, bands = shape_constants()
    arrays = {n: np.ascontiguousarray(a) for n, a in inputs.items()}
    return arrays | {"shape_const": const, "shape_bands": bands}


def kernel(**inputs):
    import concourse.bacc as bacc
    from concourse.bass_utils import run_bass_kernel_spmd

    nc = bacc.Bacc("TRN2", target_bir_lowering=False, num_devices=1)
    arrays = {f"in_{n}": a for n, a in layout(inputs).items()}
    A = {n[3:]: nc.dram_tensor(n, a.shape, mybir.dt.from_np(a.dtype), kind="ExternalInput").ap()
         for n, a in arrays.items()}
    out = nc.dram_tensor("out_0", (1, S, D), F32, kind="ExternalOutput").ap()
    build(nc, A, out)
    return run_bass_kernel_spmd(nc, [arrays], core_ids=[0]).results[0]["out_0"]
```
